# Optimizing a Trainium2 kernel written in Bass

```python
import math
import jax, jax.numpy as jnp
from jax import lax
import numpy as np

D_MODEL = 2048
BATCH = 1
SEQ = 256
DEPTH = 1
DEC_BATCH = 8
DEC_SEQ = 1
PAST_LEN = 256
PAGE_SIZE = 128

D_MIX = D_MODEL
D_ATTN = D_MIX // 2
D_SSM = D_MIX - D_ATTN
N_HEADS = 16
HEAD_DIM = D_ATTN // N_HEADS
N_KV = 4
GQ = N_HEADS // N_KV
D_KV = N_KV * HEAD_DIM
CMP_BLOCK = 32
CMP_STRIDE = 16
SEL_BLOCK = 64
N_SEL = 8
WINDOW = 512
Q_BLOCK = 128
FORCE = 1e4
SSM_GROUP = 16
N_SSM_GROUPS = D_SSM // SSM_GROUP
SSM_STATE = 64
MEM_LEN = 256
X_HEADS = 4
X_HEAD_DIM = D_MODEL // X_HEADS
PEER_KEYS = 128
N_EXPERTS = PEER_KEYS * PEER_KEYS
PEER_HEADS = 8
PEER_QDIM = 256
PEER_TOPK = 16
PEER_BLOCK = 128
D_IN = D_ATTN + 6 * D_KV + 3 * N_HEADS + D_SSM
EPS = 1e-6
NEG = -1e30
TINY = 1e-30

kernel_name = "hybrid_nsa_s5_peer_step"

F32 = jnp.float32

def rms_norm(x, g):
    x32 = x.astype(F32)
    y = x32 * lax.rsqrt(jnp.mean(x32 * x32, axis=-1, keepdims=True) + EPS) * g.astype(F32)
    return y.astype(x.dtype)

def masked_softmax(s, mask):
    s = jnp.where(mask, s, NEG)
    p = jnp.where(mask, jnp.exp(s - jnp.max(s, axis=-1, keepdims=True)), 0.0)
    return p / jnp.maximum(jnp.sum(p, axis=-1, keepdims=True), TINY)

def alibi_slopes():
    h = np.arange(1, N_HEADS + 1, dtype=np.float32)
    return jnp.asarray(2.0 ** (-8.0 * h / N_HEADS), dtype=F32).reshape(N_KV, GQ)

def sel_overlap(n_cmp, n_sel):
    i = np.arange(n_cmp)[:, None]
    j = np.arange(n_sel)[None, :]
    lo = np.maximum(i * CMP_STRIDE, j * SEL_BLOCK)
    hi = np.minimum(i * CMP_STRIDE + CMP_BLOCK, (j + 1) * SEL_BLOCK)
    return jnp.asarray(np.maximum(hi - lo, 0).astype(np.float32) / CMP_BLOCK)

def compress(k, w):
    bsz, L = k.shape[:2]
    lp = -(-L // CMP_STRIDE) * CMP_STRIDE
    k = jnp.pad(k, ((0, 0), (0, lp - L), (0, 0), (0, 0)))
    ch = k.reshape(bsz, lp // CMP_STRIDE, CMP_STRIDE, N_KV, HEAD_DIM)
    blocks = jnp.concatenate([ch[:, :-1], ch[:, 1:]], axis=2)
    return jnp.einsum('bnjhd,hj->bnhd', blocks, w)

def sel_blocks(k, n_sel):
    bsz, L = k.shape[:2]
    k = jnp.pad(k, ((0, 0), (0, n_sel * SEL_BLOCK - L), (0, 0), (0, 0)))
    return k.reshape(bsz, n_sel, SEL_BLOCK, N_KV, HEAD_DIM).transpose(0, 3, 1, 2, 4)

def nsa_attend(q, qpos, gates, ck, cv, kb, vb, kw, vw, kwpos):
    bsz, T = q.shape[:2]
    qg = q.reshape(bsz, T, N_KV, GQ, HEAD_DIM)
    scale = HEAD_DIM ** -0.5
    slope = alibi_slopes()
    nc = ck.shape[1]
    cend = jnp.arange(nc, dtype=jnp.int32) * CMP_STRIDE + (CMP_BLOCK - 1)
    dist_c = qpos[:, None] - cend[None, :]
    s_c = jnp.einsum('bthgd,bnhd->bhgtn', qg, ck).astype(F32) * scale \
        - slope[:, :, None, None] * dist_c.astype(F32)
    p_c = masked_softmax(s_c, dist_c >= 0)
    o_c = jnp.einsum('bhgtn,bnhd->bthgd', p_c.astype(cv.dtype), cv)
    n_sel = kb.shape[2]
    imp = jnp.einsum('bhgtn,nj->bhtj', p_c, sel_overlap(nc, n_sel))
    blk = jnp.arange(n_sel, dtype=jnp.int32)
    valid_blk = blk[None, :] * SEL_BLOCK <= qpos[:, None]
    forced = (blk[None, :] == (qpos // SEL_BLOCK)[:, None]) | (blk[None, :] == 0)
    imp = jnp.where(valid_blk, imp + jnp.where(forced, FORCE, 0.0), NEG)
    top_s, idx = lax.top_k(imp, N_SEL)
    ok = top_s > 0.5 * NEG
    bi = jnp.arange(bsz)[:, None, None, None]
    hi = jnp.arange(N_KV)[None, :, None, None]
    ks = kb[bi, hi, idx]
    vs = vb[bi, hi, idx]
    kpos = idx[..., None] * SEL_BLOCK + jnp.arange(SEL_BLOCK, dtype=jnp.int32)
    dist_s = qpos[None, None, :, None, None] - kpos
    mask_s = ok[..., None] & (dist_s >= 0)
    s_s = jnp.einsum('bthgd,bhtnkd->bhgtnk', qg, ks).astype(F32) * scale \
        - slope[None, :, :, None, None, None] * dist_s[:, :, None].astype(F32)
    flat = s_s.shape[:4] + (N_SEL * SEL_BLOCK,)
    p_s = masked_softmax(s_s.reshape(flat), jnp.broadcast_to(mask_s[:, :, None], s_s.shape).reshape(flat)).reshape(s_s.shape)
    o_s = jnp.einsum('bhgtnk,bhtnkd->bthgd', p_s.astype(vs.dtype), vs)
    dist_w = qpos[:, None] - kwpos[None, :]
    mask_w = (dist_w >= 0) & (dist_w < WINDOW) & (kwpos[None, :] >= 0)
    s_w = jnp.einsum('bthgd,bnhd->bhgtn', qg, kw).astype(F32) * scale \
        - slope[:, :, None, None] * dist_w.astype(F32)
    p_w = masked_softmax(s_w, mask_w)
    o_w = jnp.einsum('bhgtn,bnhd->bthgd', p_w.astype(vw.dtype), vw)
    shp = (bsz, T, N_HEADS, HEAD_DIM)
    o = gates[:, :, 0, :, None] * o_c.reshape(shp) + gates[:, :, 1, :, None] * o_s.reshape(shp) \
        + gates[:, :, 2, :, None] * o_w.reshape(shp)
    return o.astype(q.dtype).reshape(bsz, T, D_ATTN)

def nsa_prompt(q, gates, kc, vc, ks, vs, kw, vw, w_ck, w_cv):
    bsz, S = q.shape[:2]
    ck = compress(kc, w_ck)
    cv = compress(vc, w_cv)
    n_sel = max(-(-S // SEL_BLOCK), N_SEL)
    kb = sel_blocks(ks, n_sel)
    vb = sel_blocks(vs, n_sel)
    pad = ((0, 0), (WINDOW, 0), (0, 0), (0, 0))
    kw_pad = jnp.pad(kw, pad)
    vw_pad = jnp.pad(vw, pad)
    nb = S // Q_BLOCK
    qb = q.reshape(bsz, nb, Q_BLOCK, N_HEADS, HEAD_DIM).swapaxes(0, 1)
    gb = gates.reshape(bsz, nb, Q_BLOCK, 3, N_HEADS).swapaxes(0, 1)
    q0s = jnp.arange(nb, dtype=jnp.int32) * Q_BLOCK

    def one_block(args):
        qx, gx, q0 = args
        qpos = q0 + jnp.arange(Q_BLOCK, dtype=jnp.int32)
        kwin = lax.dynamic_slice_in_dim(kw_pad, q0, WINDOW + Q_BLOCK, axis=1)
        vwin = lax.dynamic_slice_in_dim(vw_pad, q0, WINDOW + Q_BLOCK, axis=1)
        kwpos = q0 - WINDOW + jnp.arange(WINDOW + Q_BLOCK, dtype=jnp.int32)
        return nsa_attend(qx, qpos, gx, ck, cv, kb, vb, kwin, vwin, kwpos)

    out = lax.map(one_block, (qb, gb, q0s))
    return out.swapaxes(0, 1).reshape(bsz, S, D_ATTN)

def _ssm_combine(e1, e2):
    a1r, a1i, b1r, b1i = e1
    a2r, a2i, b2r, b2i = e2
    return (a2r * a1r - a2i * a1i, a2r * a1i + a2i * a1r,
            a2r * b1r - a2i * b1i + b2r, a2r * b1i + a2i * b1r + b2i)

def s5_mixer(u, lp, h0_re, h0_im):
    bsz, T = u.shape[:2]
    lr = lp['lam_re'].astype(F32)
    li = lp['lam_im'].astype(F32)
    dt = jnp.exp(lp['log_dt'].astype(F32))[:, None]
    mag = jnp.exp(lr * dt)
    ar = mag * jnp.cos(li * dt)
    ai = mag * jnp.sin(li * dt)
    den = lr * lr + li * li
    fr = ((ar - 1.0) * lr + ai * li) / den
    fi = (ai * lr - (ar - 1.0) * li) / den
    br = lp['b_re'].astype(F32)
    bim = lp['b_im'].astype(F32)
    bbr = fr[..., None] * br - fi[..., None] * bim
    bbi = fr[..., None] * bim + fi[..., None] * br
    ug = u.astype(F32).reshape(bsz, T, N_SSM_GROUPS, SSM_GROUP)
    bur = jnp.einsum('btgp,gnp->btgn', ug, bbr)
    bui = jnp.einsum('btgp,gnp->btgn', ug, bbi)
    a_r = jnp.broadcast_to(ar, bur.shape)
    a_i = jnp.broadcast_to(ai, bur.shape)
    _, _, hr, hi = lax.associative_scan(_ssm_combine, (a_r, a_i, bur, bui), axis=1)
    if h0_re is not None:
        k = jnp.arange(1, T + 1, dtype=F32)[:, None, None]
        pm = jnp.exp(lr * dt * k)
        pr = pm * jnp.cos(li * dt * k)
        pi = pm * jnp.sin(li * dt * k)
        h0r = h0_re.astype(F32)[:, None]
        h0i = h0_im.astype(F32)[:, None]
        hr = hr + pr * h0r - pi * h0i
        hi = hi + pr * h0i + pi * h0r
    y = jnp.einsum('btgn,gpn->btgp', hr, lp['c_re'].astype(F32)) \
        - jnp.einsum('btgn,gpn->btgp', hi, lp['c_im'].astype(F32)) \
        + lp['d_skip'].astype(F32).reshape(N_SSM_GROUPS, SSM_GROUP) * ug
    y = jax.nn.gelu(y.reshape(bsz, T, D_SSM))
    y = y * jax.nn.sigmoid(y @ lp['w_glu'].astype(F32))
    return y.astype(u.dtype), hr[:, -1], hi[:, -1]

def split_in(z):
    bsz, T = z.shape[:2]
    q = z[..., :D_ATTN].reshape(bsz, T, N_HEADS, HEAD_DIM)
    o = D_ATTN
    kv = z[..., o:o + 6 * D_KV].reshape(bsz, T, 6, N_KV, HEAD_DIM)
    o += 6 * D_KV
    gates = jax.nn.sigmoid(z[..., o:o + 3 * N_HEADS].astype(F32)).reshape(bsz, T, 3, N_HEADS)
    o += 3 * N_HEADS
    u = z[..., o:]
    return (q, kv[:, :, 0], kv[:, :, 1], kv[:, :, 2], kv[:, :, 3], kv[:, :, 4], kv[:, :, 5], gates, u)

def merge_heads(o_a, o_s, lp):
    o = jnp.concatenate([rms_norm(o_a, lp['g_attn_out']), rms_norm(o_s, lp['g_ssm_out'])], axis=-1)
    return o @ lp['w_out']

def mem_kv(mem, lp):
    bsz, m = mem.shape[:2]
    mn = rms_norm(mem, lp['g_mem'])
    mk = (mn @ lp['w_xk']).reshape(bsz, m, X_HEADS, X_HEAD_DIM)
    mv = (mn @ lp['w_xv']).reshape(bsz, m, X_HEADS, X_HEAD_DIM)
    return mk, mv

def cross_attn(hn, mk, mv, lp):
    bsz, T = hn.shape[:2]
    q = (hn @ lp['w_xq']).reshape(bsz, T, X_HEADS, X_HEAD_DIM)
    s = jnp.einsum('bthd,bmhd->bhtm', q, mk).astype(F32) * (X_HEAD_DIM ** -0.5)
    p = jax.nn.softmax(s, axis=-1)
    o = jnp.einsum('bhtm,bmhd->bthd', p.astype(mv.dtype), mv).reshape(bsz, T, D_MODEL)
    return o @ lp['w_xo']

def peer_ffn(xn, lp):
    shp = xn.shape
    xf = xn.reshape(-1, D_MODEL)
    n = xf.shape[0]
    nb = -(-n // PEER_BLOCK)
    xf = jnp.pad(xf, ((0, nb * PEER_BLOCK - n), (0, 0))).reshape(nb, PEER_BLOCK, D_MODEL)
    half = PEER_QDIM // 2
    w_pq, k1, k2, u_tab, v_tab = lp['w_pq'], lp['peer_k1'], lp['peer_k2'], lp['peer_u'], lp['peer_v']

    def one(xb):
        q = (xb @ w_pq).reshape(PEER_BLOCK, PEER_HEADS, 2, half)
        s1 = jnp.einsum('thd,kd->thk', q[:, :, 0], k1).astype(F32)
        s2 = jnp.einsum('thd,kd->thk', q[:, :, 1], k2).astype(F32)
        t1, i1 = lax.top_k(s1, PEER_TOPK)
        t2, i2 = lax.top_k(s2, PEER_TOPK)
        cand = (t1[..., :, None] + t2[..., None, :]).reshape(PEER_BLOCK, PEER_HEADS, PEER_TOPK * PEER_TOPK)
        cidx = (i1[..., :, None] * PEER_KEYS + i2[..., None, :]).reshape(PEER_BLOCK, PEER_HEADS, PEER_TOPK * PEER_TOPK)
        top, pos = lax.top_k(cand, PEER_TOPK)
        eidx = jnp.take_along_axis(cidx, pos, axis=-1)
        g = jax.nn.softmax(top, axis=-1)
        u = u_tab[eidx]
        v = v_tab[eidx]
        a = jax.nn.gelu(jnp.einsum('thkd,td->thk', u, xb).astype(F32))
        return jnp.einsum('thk,thkd->td', (g * a).astype(v.dtype), v)

    out = lax.map(one, xf).reshape(nb * PEER_BLOCK, D_MODEL)[:n]
    return out.reshape(shp)

def gather_pages(pool, page_table):
    g = pool[page_table]
    return g.reshape(g.shape[0], g.shape[1] * g.shape[2], N_KV, HEAD_DIM)

def layer_prompt(h, mem, lp):
    q, kc, vc, ks, vs, kw, vw, gates, u = split_in(rms_norm(h, lp['g_mix']) @ lp['w_in'])
    o_a = nsa_prompt(q, gates, kc, vc, ks, vs, kw, vw, lp['w_cmp_k'], lp['w_cmp_v'])
    o_s, sr, si = s5_mixer(u, lp, None, None)
    h = h + merge_heads(o_a, o_s, lp)
    mk, mv = mem_kv(mem, lp)
    h = h + cross_attn(rms_norm(h, lp['g_x']), mk, mv, lp)
    h = h + peer_ffn(rms_norm(h, lp['g_ffn']), lp)
    wl = min(WINDOW, h.shape[1])
    return h, (kc, vc, ks, vs, kw[:, -wl:], vw[:, -wl:], sr, si, mk, mv)

def layer_sample(h, lp, pool_kc, pool_vc, pool_ks, pool_vs, buf_kw, buf_vw, s_re, s_im, mk, mv, page_table):
    T = h.shape[1]
    past = page_table.shape[1] * PAGE_SIZE
    q, kc, vc, ks, vs, kw, vw, gates, u = split_in(rms_norm(h, lp['g_mix']) @ lp['w_in'])
    kc_all = jnp.concatenate([gather_pages(pool_kc, page_table), kc], axis=1)
    vc_all = jnp.concatenate([gather_pages(pool_vc, page_table), vc], axis=1)
    ks_all = jnp.concatenate([gather_pages(pool_ks, page_table), ks], axis=1)
    vs_all = jnp.concatenate([gather_pages(pool_vs, page_table), vs], axis=1)
    ck = compress(kc_all, lp['w_cmp_k'])
    cv = compress(vc_all, lp['w_cmp_v'])
    n_sel = max(-(-(past + T) // SEL_BLOCK), N_SEL)
    kb = sel_blocks(ks_all, n_sel)
    vb = sel_blocks(vs_all, n_sel)
    wbuf = buf_kw.shape[1]
    kw_all = jnp.concatenate([buf_kw, kw], axis=1)
    vw_all = jnp.concatenate([buf_vw, vw], axis=1)
    kwpos = past - wbuf + jnp.arange(wbuf + T, dtype=jnp.int32)
    qpos = past + jnp.arange(T, dtype=jnp.int32)
    o_a = nsa_attend(q, qpos, gates, ck, cv, kb, vb, kw_all, vw_all, kwpos)
    o_s, sr, si = s5_mixer(u, lp, s_re, s_im)
    h = h + merge_heads(o_a, o_s, lp)
    h = h + cross_attn(rms_norm(h, lp['g_x']), mk, mv, lp)
    h = h + peer_ffn(rms_norm(h, lp['g_ffn']), lp)
    wl = min(WINDOW, past + T)
    return h, (kc, vc, ks, vs, kw_all[:, -wl:], vw_all[:, -wl:], sr, si)

def setup_inputs(seed: int = 0) -> dict:
    key = jax.random.key(seed)
    keys = iter(jax.random.split(key, 64))

    def nrm(shape, scale):
        return jax.random.normal(next(keys), shape, F32) * scale

    def gain(shape):
        return 1.0 + nrm(shape, 0.01)

    n_pages = PAST_LEN // PAGE_SIZE
    n_used = DEC_BATCH * n_pages
    n_phys = n_used + -(-n_used // 4)
    wbuf = min(WINDOW, PAST_LEN)
    L = DEPTH
    G, N, P = N_SSM_GROUPS, SSM_STATE, SSM_GROUP
    inp = {}
    inp['x_prompt'] = nrm((BATCH, SEQ, D_MODEL), 1.0)
    inp['x_sample'] = nrm((DEC_BATCH, DEC_SEQ, D_MODEL), 1.0)
    inp['mem_prompt'] = nrm((BATCH, MEM_LEN, D_MODEL), 1.0)
    inp['cache_k_cmp'] = nrm((L, n_phys, PAGE_SIZE, N_KV, HEAD_DIM), 1.0)
    inp['cache_v_cmp'] = nrm((L, n_phys, PAGE_SIZE, N_KV, HEAD_DIM), 1.0)
    inp['cache_k_sel'] = nrm((L, n_phys, PAGE_SIZE, N_KV, HEAD_DIM), 1.0)
    inp['cache_v_sel'] = nrm((L, n_phys, PAGE_SIZE, N_KV, HEAD_DIM), 1.0)
    inp['cache_k_win'] = nrm((L, DEC_BATCH, wbuf, N_KV, HEAD_DIM), 1.0)
    inp['cache_v_win'] = nrm((L, DEC_BATCH, wbuf, N_KV, HEAD_DIM), 1.0)
    inp['state_s5_re'] = nrm((L, DEC_BATCH, G, N), 1.0)
    inp['state_s5_im'] = nrm((L, DEC_BATCH, G, N), 1.0)
    inp['cache_mem_k'] = nrm((L, DEC_BATCH, MEM_LEN, X_HEADS, X_HEAD_DIM), 1.0)
    inp['cache_mem_v'] = nrm((L, DEC_BATCH, MEM_LEN, X_HEADS, X_HEAD_DIM), 1.0)
    inp['page_table'] = jax.random.permutation(next(keys), n_phys)[:n_used].reshape(DEC_BATCH, n_pages).astype(jnp.int32)
    inp['g_mix'] = gain((L, D_MODEL))
    inp['w_in'] = nrm((L, D_MODEL, D_IN), D_MODEL ** -0.5)
    inp['w_cmp_k'] = (1.0 + nrm((L, N_KV, CMP_BLOCK), 0.1)) * CMP_BLOCK ** -0.5
    inp['w_cmp_v'] = (1.0 + nrm((L, N_KV, CMP_BLOCK), 0.1)) * CMP_BLOCK ** -0.5
    inp['lam_re'] = -0.5 + nrm((L, G, N), 0.01)
    inp['lam_im'] = math.pi * jnp.arange(N, dtype=F32) + nrm((L, G, N), 0.01)
    inp['log_dt'] = jax.random.uniform(next(keys), (L, G), F32, math.log(1e-3), math.log(1e-1))
    inp['b_re'] = nrm((L, G, N, P), (2 * P) ** -0.5)
    inp['b_im'] = nrm((L, G, N, P), (2 * P) ** -0.5)
    inp['c_re'] = nrm((L, G, P, N), N ** -0.5)
    inp['c_im'] = nrm((L, G, P, N), N ** -0.5)
    inp['d_skip'] = nrm((L, D_SSM), 1.0)
    inp['w_glu'] = nrm((L, D_SSM, D_SSM), D_SSM ** -0.5)
    inp['g_attn_out'] = gain((L, D_ATTN))
    inp['g_ssm_out'] = gain((L, D_SSM))
    inp['w_out'] = nrm((L, D_MIX, D_MODEL), D_MIX ** -0.5)
    inp['g_x'] = gain((L, D_MODEL))
    inp['g_mem'] = gain((L, D_MODEL))
    inp['w_xq'] = nrm((L, D_MODEL, D_MODEL), D_MODEL ** -0.5)
    inp['w_xk'] = nrm((L, D_MODEL, D_MODEL), D_MODEL ** -0.5)
    inp['w_xv'] = nrm((L, D_MODEL, D_MODEL), D_MODEL ** -0.5)
    inp['w_xo'] = nrm((L, D_MODEL, D_MODEL), D_MODEL ** -0.5)
    inp['g_ffn'] = gain((L, D_MODEL))
    inp['w_pq'] = nrm((L, D_MODEL, PEER_HEADS * PEER_QDIM), D_MODEL ** -0.5)
    inp['peer_k1'] = nrm((L, PEER_KEYS, PEER_QDIM // 2), (PEER_QDIM // 2) ** -0.5)
    inp['peer_k2'] = nrm((L, PEER_KEYS, PEER_QDIM // 2), (PEER_QDIM // 2) ** -0.5)
    inp['peer_u'] = nrm((L, N_EXPERTS, D_MODEL), D_MODEL ** -0.5)
    inp['peer_v'] = nrm((L, N_EXPERTS, D_MODEL), PEER_HEADS ** -0.5)
    inp['g_final'] = gain((D_MODEL,))
    return inp

def reference(x_prompt, x_sample, mem_prompt, cache_k_cmp, cache_v_cmp, cache_k_sel, cache_v_sel,
              cache_k_win, cache_v_win, state_s5_re, state_s5_im, cache_mem_k, cache_mem_v, page_table,
              g_mix, w_in, w_cmp_k, w_cmp_v, lam_re, lam_im, log_dt, b_re, b_im, c_re, c_im, d_skip, w_glu,
              g_attn_out, g_ssm_out, w_out, g_x, g_mem, w_xq, w_xk, w_xv, w_xo, g_ffn, w_pq,
              peer_k1, peer_k2, peer_u, peer_v, g_final):
    h_p = x_prompt
    h_s = x_sample
    p_list = []
    s_list = []
    for l in range(DEPTH):
        lp = dict(g_mix=g_mix[l], w_in=w_in[l], w_cmp_k=w_cmp_k[l], w_cmp_v=w_cmp_v[l],
                  lam_re=lam_re[l], lam_im=lam_im[l], log_dt=log_dt[l], b_re=b_re[l], b_im=b_im[l],
                  c_re=c_re[l], c_im=c_im[l], d_skip=d_skip[l], w_glu=w_glu[l],
                  g_attn_out=g_attn_out[l], g_ssm_out=g_ssm_out[l], w_out=w_out[l],
                  g_x=g_x[l], g_mem=g_mem[l], w_xq=w_xq[l], w_xk=w_xk[l], w_xv=w_xv[l], w_xo=w_xo[l],
                  g_ffn=g_ffn[l], w_pq=w_pq[l], peer_k1=peer_k1[l], peer_k2=peer_k2[l],
                  peer_u=peer_u[l], peer_v=peer_v[l])
        h_p, st_p = layer_prompt(h_p, mem_prompt, lp)
        h_s, st_s = layer_sample(h_s, lp, cache_k_cmp[l], cache_v_cmp[l], cache_k_sel[l], cache_v_sel[l],
                                 cache_k_win[l], cache_v_win[l], state_s5_re[l], state_s5_im[l],
                                 cache_mem_k[l], cache_mem_v[l], page_table)
        p_list.append(st_p)
        s_list.append(st_s)
    y_prompt = rms_norm(h_p, g_final)
    y_sample = rms_norm(h_s, g_final)
    (p_k_cmp, p_v_cmp, p_k_sel, p_v_sel, p_k_win, p_v_win, p_s5_re, p_s5_im, p_mem_k, p_mem_v) = \
        [jnp.stack(s) for s in zip(*p_list)]
    (s_k_cmp, s_v_cmp, s_k_sel, s_v_sel, s_k_win, s_v_win, s_s5_re, s_s5_im) = \
        [jnp.stack(s) for s in zip(*s_list)]
    return (y_prompt, y_sample,
            p_k_cmp, p_v_cmp, p_k_sel, p_v_sel, p_k_win, p_v_win, p_s5_re, p_s5_im, p_mem_k, p_mem_v,
            s_k_cmp, s_v_cmp, s_k_sel, s_v_sel, s_k_win, s_v_win, s_s5_re, s_s5_im)


_drawn_inputs = setup_inputs


def setup_inputs(seed=0):
    import zlib

    import numpy as np

    out = dict(_drawn_inputs(seed))
    spreads = {}
    factors = {'g_mix': 3.777,
     'lam_re': 16.727,
     'g_attn_out': 5.44,
     'g_ssm_out': 4.862,
     'g_x': 8.0,
     'g_mem': 5.776,
     'g_ffn': 29.266,
     'g_final': 32.656}
    for name, (base, spread) in spreads.items():
        noise = np.random.default_rng([zlib.crc32(name.encode()), seed]).standard_normal(out[name].shape)
        drawn = base * np.exp(spread * noise) if base else spread * noise
        out[name] = __import__('jax').numpy.asarray(drawn.astype(out[name].dtype))
    for name, factor in factors.items():
        out[name] = (out[name] * factor).astype(out[name].dtype)
    return out
```

```python
from contextlib import ExitStack

import numpy as np
import concourse.bass as bass
from concourse import mybir

ALU = mybir.AluOpType
ACT = mybir.ActivationFunctionType
AXX = mybir.AxisListType.X
F32 = mybir.dt.float32
I32 = mybir.dt.int32
U32 = mybir.dt.uint32

P = 128
D = 2048
KT = D // P
TP, TS = 256, 8
NT = TP + TS
QB = TP // P
HEADS, KV, GQ, HD = 16, 4, 4, 64
CMP, STRIDE = 32, 16
NC = TP // STRIDE - 1
PAST = 256
SCALE = HD ** -0.5
NEG, TINY, EPS = -1e30, 1e-30, 1e-6
XH, XD, MEM = 4, 512, 256
XSCALE = XD ** -0.5
GROUPS, SG, SN = 64, 16, 64
ST = GROUPS * SN // P
PH, PK, TOPK = 8, 128, 16
SLOTS = PH * TOPK
SLOPE = [2.0 ** (-8.0 * (h + 1) / HEADS) for h in range(HEADS)]
MAGIC = 12582912.0
TWO_PI = 6.2831850

Q0, K_CMP, V_CMP, K_SEL, V_SEL, K_WIN, V_WIN, U0, NZ = 0, 8, 10, 12, 14, 16, 18, 20, 28

C = {}
for _name, _n in (("ident", P), ("ones", P), ("d0", P), ("d1", TP), ("dc", QB * NC), ("mc", QB * NC), ("ds", PAST + 1),
                  ("dcs", NC), ("t", TP), ("sel", P), ("selT", TS), ("kmask", 16), ("iota", 16), ("pidx", 1),
                  ("half_pi", 1), ("eps", 1)):
    C[_name] = (sum(n for _, n in C.values()), _n)
NCONST = sum(n for _, n in C.values())
G_MIX, G_X, G_MEM, G_FFN, G_ATT, G_SSM, D_SKIP, NGAIN = 0, 16, 32, 48, 64, 72, 80, 88


def constants():
    c = np.zeros((P, NCONST), np.float32)

    def put(name, value):
        a, n = C[name]
        c[: value.shape[0], a:a + n] = value

    p = np.arange(P)
    put("ident", np.eye(P))
    put("ones", np.ones((P, P)))
    for b, name in enumerate(("d0", "d1")):
        n = C[name][1]
        dist = (b * P + p)[:, None] - np.arange(n)[None]
        put(name, np.where(dist >= 0, -dist, NEG))
    dist = np.stack([(b * P + p)[:, None] - (np.arange(NC) * STRIDE + CMP - 1)[None] for b in range(QB)], 1)
    put("dc", np.where(dist >= 0, -dist, NEG).reshape(P, -1))
    put("mc", (dist >= 0).reshape(P, -1))
    slope = np.array([SLOPE[i % HEADS] for i in range(P)])[:, None] / SCALE
    put("ds", -slope * (PAST - np.arange(PAST + 1))[None])
    put("dcs", -slope * (PAST - np.arange(NC) * STRIDE - CMP + 1)[None])
    put("t", np.tile(np.arange(TP), (P, 1)))
    put("sel", (p[None] // 16 == np.arange(TS)[:, None]))
    put("selT", (p[:, None] // 16 == np.arange(TS)[None]))
    put("kmask", (p[:, None] % 16 == np.arange(16)[None]))
    put("iota", np.tile(np.arange(16), (P, 1)))
    put("pidx", p[:, None])
    put("half_pi", np.full((P, 1), np.pi / 2))
    put("eps", np.full((P, 1), EPS))
    return c


INS = {
    "consts": (P, NCONST), "gains": (P, NGAIN), "x_t": (P, KT, NT), "mem_t": (P, KT, TP),
    "w_z": (NZ, P, KT * P), "w_gate": (P, KT * 48), "w_xk": (KT, P, D), "w_xv": (KT, P, D), "w_glu": (8, P, 8 * P),
    "w_out": (KT, P, D), "w_xq": (KT, P, D), "w_xo": (KT, P, D), "w_pq": (KT, P, D),
    "s5_par": (P, 3, ST), "s5_b": (P, 2, ST * 32), "s5_c": (P, 2, ST * 32), "s5_h0": (P, 2, ST * TS),
    "w_cmp": (P, 2, 2, CMP), "page": (16,),
    "pool_kc": (2560, 256), "pool_vc": (2560, 256), "pool_ks": (2560, 256), "pool_vs": (2560, 256),
    "win_k": (TS, P, 512), "win_v": (TS, P, 512), "mem_k": (TS, 2, P, D), "mem_v": (TS, 2, P, D),
    "keys": (P, 2, PK), "peer_u": (16384, D), "peer_v": (16384, D), "g_ffn": (D,), "g_final": (D,),
    "buf_k": (TS, 256 * 256), "buf_v": (TS, 256 * 256),
}
OUTS = {
    "y_p": (TP, D), "y_s": (TS, D), "z_kv": (12, P, NT), "s5_p": (P, 2 * ST), "s5_s": (P, 2 * ST * TS),
    "m_k": (KT, P, TP), "m_v": (QB, P, D), "new_k": (TS, 257 * 256), "new_v": (TS, 257 * 256),
}


class Counted:

    def __init__(self, eng, sem, loop=0):
        self.eng, self.sem, self.n, self.loop = eng, sem, 0, loop

    def __call__(self, ins):
        ins.then_inc(self.sem, 1)
        self.n += 1
        return self.n

    def wait(self, n=None):
        self.eng.wait_ge(self.sem, self.loop + (self.n if n is None else n))


def build(nc, A):
    with ExitStack() as ctx:
        def sb(name, n, dt=F32):
            return ctx.enter_context(nc.sbuf_tensor("sb_" + name, [P, n], dt))

        sems = {}

        def S(name):
            if name not in sems:
                sems[name] = ctx.enter_context(nc.semaphore("s_" + name))
            return sems[name]

        bank = [ctx.enter_context(nc.psum_tensor(f"bank{i}", [P, 512], F32)) for i in range(8)]

        con = sb("con", NCONST)
        gain = sb("gain", NGAIN)
        h_t = sb("h_t", KT * NT)
        x_t = sb("x_t", 19 * 256)
        m_t = sb("m_t", KT * TP)
        y_t = sb("y_t", KT * NT)
        z_t = sb("z_t", NZ * NT)
        gate = sb("gate", NT)
        ring = sb("ring", 4 * D)
        mk_t = sb("mk_t", KT * TP)
        mv_n = sb("mv_n", QB * D)
        b_st = sb("b_st", 2 * 8 * P)
        c_st = sb("c_st", 2 * ST * 32)
        par = sb("par", 3 * ST)
        prm = sb("prm", 26 * ST)
        s5s = sb("s5s", 8 * ST * TS)
        s5p = sb("s5p", 2 * ST)
        wcmp = sb("wcmp", 2 * 2 * CMP)
        rst = sb("rst", 2 * NT)
        gn = sb("gn", 208)
        small = sb("small", 96)
        idx_i = sb("idx_i", 16, I32)

        def cc(name, lo=0, n=None, rows=P):
            a, w = C[name]
            return con[0:rows, a + lo:a + lo + (w - lo if n is None else n)]

        ident = cc("ident")
        H = h_t[:, :].rearrange("p (t n) -> p t n", n=NT)
        X = x_t[:, 0:KT * NT].rearrange("p (t n) -> p t n", n=NT)
        M = m_t[:, :].rearrange("p (t n) -> p t n", n=TP)
        Y = y_t[:, :].rearrange("p (t n) -> p t n", n=NT)
        Z = z_t[:, :].rearrange("p (t n) -> p t n", n=NT)
        R = ring[:, :].rearrange("p (s t n) -> p s t n", s=4, n=P)
        MK = mk_t[:, :].rearrange("p (t n) -> p t n", n=TP)
        MV = mv_n[:, :].rearrange("p (b n) -> p b n", b=QB)

        segs = [("z", NZ), ("gate", 1), ("xk", 16), ("xv", 16), ("glu", 8), ("dk", 8), ("dv", 8), ("out", 16),
                ("xq", 16), ("mk", 16), ("mv", 16), ("xo", 16), ("pq", 16)]
        nd = {"dk": 7, "dv": 3}
        full, start, at, fill = {}, {}, 0, {}
        users = []
        tiles_before, tiles = {}, 0
        for seg, n in segs:
            start[seg] = at
            gemm = seg not in ("dk", "dv", "mk", "mv")
            tiles_before[seg] = tiles
            for j in range(n):
                s = at % 4
                by = ("cache" if seg in nd else "full") + str(s)
                fill[by] = fill.get(by, 0) + 16 * nd.get(seg, 1)
                full[seg, j] = (s, by, fill[by])
                last = j | 1 if seg == "xv" else j
                users.append(("tile", tiles + last + 1) if gemm else (seg + "_used", j + 1))
                at += 1
            tiles += n if gemm else 0
            if seg == "gate":
                at += 3
                users += [None] * 3

        def arrived(eng, seg, j):
            s, by, v = full[seg, j]
            eng.wait_ge(S(by), v)
            return s

        def free(eng, g):
            while g >= 4:
                g -= 4
                if users[g] is not None:
                    eng.wait_ge(S(users[g][0]), users[g][1])
                    return

        block = ctx.enter_context(nc.Block())

        def sp_stream(sp):
            sp.dma_start(h_t[:, :], A["x_t"].rearrange("p t n -> p (t n)")).then_inc(S("ld_x"), 16)
            sp.dma_start(con[:, :], A["consts"]).then_inc(S("ld_c"), 16)
            sp.dma_start(gain[:, :], A["gains"]).then_inc(S("ld_g"), 16)

            def stream(seg, src, cols=D):
                n = dict(segs)[seg]
                s0 = start[seg]

                def load(j, k):
                    sp.dma_start(ring[:, k * D:k * D + cols], src(j)).then_inc(S(f"full{k}"), 16)

                for j in range(min(4, n)):
                    free(sp, s0 + j)
                    load(j, (s0 + j) % 4)
                if n > 4:
                    with sp.Fori(1, n // 4) as i:
                        for k in range(4):
                            last = k | 1 if seg == "xv" else k
                            if seg in ("mk", "mv"):
                                sp.wait_ge(S(seg + "_used"), i * 4 + (k - 3))
                            else:
                                sp.wait_ge(S("tile"), i * 4 + (tiles_before[seg] + last - 3))
                            load(i * 4 + k, k)

            def tiles_of(w):
                return lambda j: w[bass.ds(j, 1)].rearrange("a p n -> (a p) n")

            stream("z", tiles_of(A["w_z"]))
            stream("gate", lambda j: A["w_gate"], KT * 48)
            stream("xk", tiles_of(A["w_xk"]))
            stream("xv", tiles_of(A["w_xv"]))
            stream("glu", tiles_of(A["w_glu"]), 8 * P)
            stream("out", tiles_of(A["w_out"]))
            stream("xq", tiles_of(A["w_xq"]))
            stream("mk", lambda j: A["mem_k"].rearrange("b c p n -> (b c) p n")[bass.ds(j, 1)].rearrange("a p n -> (a p) n"))
            stream("mv", lambda j: A["mem_v"].rearrange("b c p n -> (b c) p n")[bass.ds(j, 1)].rearrange("a p n -> (a p) n"))
            stream("xo", tiles_of(A["w_xo"]))
            stream("pq", tiles_of(A["w_pq"]))

        def act_norm(act, tag, src, sq, t, width, bk=7):
            for k in range(4):
                a, b = k * t // 4, (k + 1) * t // 4
                act.activation(sq[:, a:b, :], src[:, a:b, :], ACT.Square).then_inc(S(tag + "_sq"), 1)
            act.wait_ge(S(tag + "_sum"), 1)
            act.activation(rst[:, 0:src.shape[2]], bank[bk][:, 0:src.shape[2]], ACT.Sqrt, bias=cc("eps"),
                           scale=1.0 / width).then_inc(S(tag + "_rms"), 1)

        def pe_norm(pe, tag, sq, t, bk=7):
            n = sq.shape[2]
            for k in range(t):
                if k % (t // 4) == 0:
                    pe.wait_ge(S(tag + "_sq"), k // (t // 4) + 1)
                last = pe.matmul(bank[bk][:, 0:n], lhsT=cc("ones"), rhs=sq[:, k, :], start=(k == 0), stop=(k == t - 1))
            last.then_inc(S(tag + "_sum"), 1)

        def dve_norm(dve, tag, dst, src, t, g0):
            n = src.shape[2]
            dve.wait_ge(S(tag + "_rms"), 1)
            dve.reciprocal(rst[:, NT:NT + n], rst[:, 0:n]).then_inc(S(tag + "_x"), 1)
            dve.wait_ge(S(tag + "_x"), 1)
            for k in range(t):
                dve.scalar_tensor_tensor(out=dst[:, k, :], in0=src[:, k, :], scalar=gain[:, g0 + k:g0 + k + 1],
                                         in1=rst[:, NT:NT + n], op0=ALU.mult, op1=ALU.mult).then_inc(S(tag + "_x"), 1)

        SQ = Y
        SQM = y_t[:, 0:KT * TP].rearrange("p (t n) -> p t n", n=TP)

        def pe_gemm(pe, seg, src, kts, first=False):
            n, base = dict(segs)[seg], tiles_before[seg]

            def four(i, waits):
                for k in range(4):
                    s, by, v = full[seg, k]
                    pe.wait_ge(S(by), i * 16 + v)
                    if waits:
                        pe.wait_ge(S("evac"), i * 4 + (base + k - 3))
                    for t in range(kts):
                        mm = pe.matmul(bank[k][:, 0:src.shape[2]], lhsT=R[:, s, t, :], rhs=src[:, t, :],
                                       start=(t == 0), stop=(t == kts - 1))
                    mm.then_inc(S("tile"), 1)

            if first:
                four(0, False)
            else:
                pe.wait_ge(S("evac"), base)
            with pe.Fori(1 if first else 0, n // 4) as i:
                four(i, True)

        def copy_gemm(act, seg, dst, func=ACT.Copy):
            n, base = dict(segs)[seg], tiles_before[seg]
            with act.Fori(0, n // 4) as i:
                for k in range(4):
                    act.wait_ge(S("tile"), i * 4 + (base + k + 1))
                    act.activation(dst[:, bass.ds(i * 4 + k, 1), :].rearrange("p a n -> p (a n)"),
                                   bank[k][:, 0:dst.shape[2]], func).then_inc(S("evac"), 1)

        def add_gemm(dve, seg, dst):
            n, base = dict(segs)[seg], tiles_before[seg]
            with dve.Fori(0, n // 4) as i:
                for k in range(4):
                    at_ = dst[:, bass.ds(i * 4 + k, 1), :].rearrange("p a n -> p (a n)")
                    dve.wait_ge(S("tile"), i * 4 + (base + k + 1))
                    dve.tensor_tensor(at_, bank[k][:, 0:NT], at_, ALU.add).then_inc(S("evac"), 1)

        def W(i):
            return x_t[:, i * 256:(i + 1) * 256]

        COS, SIN = (W(0), W(1)), (W(2), W(3))
        ROUND, PROD, FRAC, ABS = W(4), W(5), W(6), W(7)
        M1, M2, M3, M4, GR, GI, N1 = (W(8 + i) for i in range(7))
        HR, HI = (W(15), W(16)), (W(17), W(18))

        def pr(i):
            return prm[:, i * ST:(i + 1) * ST]

        BRAW = mk_t[:, 0:D].rearrange("p (c j n) -> p c j n", c=2, n=32)
        BBAR = mk_t[:, D:2 * D].rearrange("p (c j n) -> p c j n", c=2, n=32)
        BT = b_st[:, :].rearrange("p (c t n) -> p c t n", c=2, n=P)
        CT = c_st[:, :].rearrange("p (c j n) -> p c j n", c=2, n=32)
        H0 = s5s[:, 0:2 * ST * TS].rearrange("p (c j b) -> p c j b", c=2, b=TS)
        BU = s5s[:, 2 * ST * TS:4 * ST * TS].rearrange("p (c j b) -> p c j b", c=2, b=TS)
        HS = s5s[:, 4 * ST * TS:6 * ST * TS].rearrange("p (c j b) -> p c j b", c=2, b=TS)
        TMP = s5s[:, 6 * ST * TS:8 * ST * TS].rearrange("p (c j b) -> p c j b", c=2, b=TS)

        def dve_s5_parameters(dve):
            lr, li = par[:, 0:ST], par[:, ST:2 * ST]
            do = Counted(dve, S("par_dve"))
            dve.wait_ge(S("ld_s5"), 16 * 4)
            dve.wait_ge(S("par_act"), 1)
            do(dve.tensor_tensor(pr(1), lr, pr(0), ALU.mult))
            do(dve.tensor_tensor(pr(2), li, pr(0), ALU.mult))
            do.wait()
            do(dve.tensor_scalar(pr(4), pr(2), 1 / (2 * np.pi), MAGIC, ALU.mult, ALU.add))
            do.wait()
            do(dve.tensor_scalar(pr(4), pr(4), MAGIC, None, ALU.subtract))
            do.wait()
            do(dve.scalar_tensor_tensor(out=pr(5), in0=pr(2), scalar=1 / (2 * np.pi), in1=pr(4),
                                        op0=ALU.mult, op1=ALU.subtract))
            dve.wait_ge(S("par_act"), 5)
            do(dve.tensor_tensor(pr(9), pr(3), pr(8), ALU.mult))
            do(dve.tensor_tensor(pr(10), pr(3), pr(7), ALU.mult))
            do(dve.tensor_tensor(pr(14), lr, lr, ALU.mult))
            do(dve.tensor_tensor(pr(15), li, li, ALU.mult))
            do.wait()
            do(dve.tensor_scalar(pr(11), pr(9), 1.0, None, ALU.subtract))
            do(dve.tensor_tensor(pr(14), pr(14), pr(15), ALU.add))
            do.wait()
            do(dve.reciprocal(pr(15), pr(14)))
            do(dve.tensor_tensor(pr(12), pr(11), lr, ALU.mult))
            do(dve.tensor_tensor(pr(13), pr(10), li, ALU.mult))
            do(dve.tensor_tensor(pr(18), pr(10), lr, ALU.mult))
            do(dve.tensor_tensor(pr(19), pr(11), li, ALU.mult))
            do.wait()
            do(dve.tensor_tensor(pr(12), pr(12), pr(13), ALU.add))
            do(dve.tensor_tensor(pr(18), pr(18), pr(19), ALU.subtract))
            do.wait()
            do(dve.tensor_tensor(pr(16), pr(12), pr(15), ALU.mult))
            do(dve.tensor_tensor(pr(17), pr(18), pr(15), ALU.mult))
            do(dve.tensor_scalar(c_st[:, 1024:2048], c_st[:, 1024:2048], -1.0, None, ALU.mult))
            do.wait()
            fr = pr(16).unsqueeze(2).to_broadcast([P, ST, 32])
            fi = pr(17).unsqueeze(2).to_broadcast([P, ST, 32])
            t1 = y_t[:, 0:1024].rearrange("p (j n) -> p j n", n=32)
            t2 = y_t[:, 1024:2048].rearrange("p (j n) -> p j n", n=32)
            for part, (f1, f2, op) in enumerate(((fr, fi, ALU.subtract), (fi, fr, ALU.add))):
                if part:
                    do.wait()
                do(dve.tensor_tensor(t1, BRAW[:, 0], f1, ALU.mult))
                do(dve.tensor_tensor(t2, BRAW[:, 1], f2, ALU.mult))
                do.wait()
                do(dve.tensor_tensor(BBAR[:, part], t1, t2, op))
            return do.n

        def act_s5_parameters(act):
            act.wait_ge(S("ld_s5"), 16 * 4)
            act.activation(pr(0), par[:, 2 * ST:3 * ST], ACT.Exp).then_inc(S("par_act"), 1)
            act.wait_ge(S("par_dve"), 1)
            act.activation(pr(3), pr(1), ACT.Exp).then_inc(S("par_act"), 1)
            act.wait_ge(S("par_dve"), 5)
            act.activation(pr(6), pr(5), ACT.Abs).then_inc(S("par_act"), 1)
            act.activation(pr(7), pr(5), ACT.Sin, scale=TWO_PI).then_inc(S("par_act"), 1)
            act.wait_ge(S("par_act"), 3)
            act.activation(pr(8), pr(6), ACT.Sin, scale=-TWO_PI, bias=cc("half_pi")).then_inc(S("par_act"), 1)

        PAR_DONE = 27

        def pe_b_transposes(pe):
            pe.wait_ge(S("par_dve"), PAR_DONE)
            for n in range(16):
                b = bank[4 + n // 4]
                tr = pe.transpose(b[:, (n % 4) * P:(n % 4 + 1) * P],
                                  mk_t[:, D + n * P:D + (n + 1) * P], ident)
                if n % 4 == 3:
                    tr.then_inc(S("b_turned"), 1)

        def act_b_transposes(act):
            for n in range(4):
                act.wait_ge(S("b_turned"), n + 1)
                act.activation(b_st[:, n * 512:(n + 1) * 512], bank[4 + n][:, :], ACT.Copy).then_inc(S("b_kept"), 1)

        DV, PO, AC = 13, 9, 3
        BANKS_READ, WR, GR_AT, ROT, HR_AT = 6, 8, 10, 12, 13

        def pool_s5_table(pool, j):
            f = pr(5)[:, j:j + 1]
            base = j * PO
            if j >= 1:
                pool.wait_ge(S("s5_act"), AC * j)
                pool.wait_ge(S("s5_tab"), 4 * j)
            pool.tensor_scalar(ROUND, cc("t"), f, MAGIC, ALU.mult, ALU.add).then_inc(S("s5_tab"), 1)
            pool.tensor_scalar(PROD, cc("t"), f, None, ALU.mult).then_inc(S("s5_tab"), 1)
            pool.wait_ge(S("s5_tab"), 4 * j + 2)
            pool.tensor_scalar(ROUND, ROUND, MAGIC, None, ALU.subtract).then_inc(S("s5_tab"), 1)
            pool.wait_ge(S("s5_tab"), 4 * j + 3)
            pool.tensor_tensor(FRAC, PROD, ROUND, ALU.subtract).then_inc(S("s5_tab"), 1)

        def act_s5_table(act, j):
            act.wait_ge(S("s5_tab"), 4 * j + 4)
            if j >= 2:
                act.wait_ge(S("s5_dve"), DV * (j - 2) + ROT)
                act.wait_ge(S("s5_im"), 5 * (j - 2) + 2)
            if j >= 1:
                act.wait_ge(S("s5_act"), AC * j)
            act.activation(ABS, FRAC, ACT.Abs).then_inc(S("s5_act"), 1)
            act.activation(SIN[j % 2], FRAC, ACT.Sin, scale=TWO_PI).then_inc(S("s5_act"), 1)
            act.wait_ge(S("s5_act"), AC * j + 1)
            act.activation(COS[j % 2], ABS, ACT.Sin, scale=-TWO_PI, bias=cc("half_pi")).then_inc(S("s5_act"), 1)

        def pe_s5_input(pe, j):
            jj, q = j % 4, j // 4
            if j >= 1:
                pe.wait_ge(S("s5_dve"), DV * (j - 1) + BANKS_READ)
            for part in range(2):
                mm = pe.matmul(bank[4 + part][:, 0:NT], lhsT=BT[32 * jj:32 * jj + 32, part, q, :],
                               rhs=Z[32 * jj:32 * jj + 32, U0 + q, :], start=True, stop=True, tile_position=(32 * jj, 0))
            mm.then_inc(S("s5_bu"), 1)

        def dve_s5(dve, j):
            do = Counted(dve, S("s5_dve"), DV * j)
            c, s = COS[j % 2], SIN[j % 2]
            br, bi = bank[4][:, 0:TP], bank[5][:, 0:TP]
            dve.wait_ge(S("s5_bu"), j + 1)
            dve.wait_ge(S("s5_act"), AC * (j + 1))
            if j >= 1:
                do.wait(0)
            do(dve.tensor_tensor(M1, c, br, ALU.mult))
            do(dve.tensor_tensor(M2, s, bi, ALU.mult))
            do(dve.tensor_tensor(M3, c, bi, ALU.mult))
            do(dve.tensor_tensor(M4, s, br, ALU.mult))
            do(dve.tensor_copy(BU[:, 0, j, :], bank[4][:, TP:NT]))
            do(dve.tensor_copy(BU[:, 1, j, :], bank[5][:, TP:NT]))
            do.wait(4)
            do(dve.tensor_tensor(M1, M1, M2, ALU.add))
            do(dve.tensor_tensor(M3, M3, M4, ALU.subtract))
            if j >= 1:
                dve.wait_ge(S("s5_im"), 5 * (j - 1) + 2)
            do.wait(7)
            r = pr(3)[:, j:j + 1].to_broadcast([P, TP])
            do(dve.tensor_tensor_scan(GR, r, M1, 0.0, ALU.mult, ALU.add))
            do.wait(8)
            do(dve.tensor_tensor_scan(GI, r, M3, 0.0, ALU.mult, ALU.add))
            do.wait(9)
            do(dve.tensor_tensor(M2, c, GR, ALU.mult))
            do.wait(10)
            do(dve.tensor_tensor(M4, s, GI, ALU.mult))
            if j >= 2:
                dve.wait_ge(S("s5_c"), j - 1)
                dve.wait_ge(S("s5_im"), 5 * (j - 2) + 5)
            do.wait(12)
            do(dve.tensor_tensor(HR[j % 2], M2, M4, ALU.subtract))

        def pool_s5(pool, j):
            do = Counted(pool, S("s5_im"), 5 * j)
            c, s = COS[j % 2], SIN[j % 2]
            pool.wait_ge(S("s5_dve"), DV * j + GR_AT)
            if j >= 1:
                do.wait(0)
            if j >= 2:
                pool.wait_ge(S("s5_c"), j - 1)
            do(pool.tensor_tensor(N1, s, GR, ALU.mult))
            do(pool.tensor_tensor(HI[j % 2], c, GI, ALU.mult))
            do.wait()
            do(pool.tensor_tensor(HI[j % 2], N1, HI[j % 2], ALU.add))
            do.wait()
            do(pool.tensor_copy(s5p[:, ST + j:ST + j + 1], HI[j % 2][:, TP - 1:TP]))
            pool.wait_ge(S("s5_dve"), DV * j + HR_AT)
            do(pool.tensor_copy(s5p[:, j:j + 1], HR[j % 2][:, TP - 1:TP]))

        def pe_s5_output(pe, j):
            jj, q = j % 4, j // 4
            pe.wait_ge(S("s5_dve"), DV * j + HR_AT)
            pe.wait_ge(S("s5_im"), 5 * j + 3)
            if jj == 0 and q >= 1:
                pe.wait_ge(S("s5_y"), q)
            for part, h in enumerate((HR, HI)):
                mm = pe.matmul(bank[6][32 * jj:32 * jj + 32, 0:TP], lhsT=CT[:, part, j, :], rhs=h[j % 2],
                               start=(part == 0), stop=(part == 1), tile_position=(0, 32 * jj))
            mm.then_inc(S("s5_c"), 1)

        def dve_s5_skip(dve, q):
            dve.wait_ge(S("s5_c"), 4 * q + 4)
            dve.scalar_tensor_tensor(out=Y[:, 8 + q, 0:TP], in0=Z[:, U0 + q, 0:TP],
                                     scalar=gain[:, D_SKIP + q:D_SKIP + q + 1], in1=bank[6][:, 0:TP],
                                     op0=ALU.mult, op1=ALU.add).then_inc(S("s5_y"), 1)

        def dve_s5_samples(dve):
            do = Counted(dve, S("s5_smp"))
            ar = pr(9).unsqueeze(2).to_broadcast([P, ST, TS])
            ai = pr(10).unsqueeze(2).to_broadcast([P, ST, TS])
            dve.wait_ge(S("s5_dve"), DV * ST)
            for part, (x, y, op) in enumerate(((ar, ai, ALU.subtract), (ai, ar, ALU.add))):
                if part:
                    do.wait()
                do(dve.tensor_tensor(TMP[:, 0], H0[:, 0], x, ALU.mult))
                do(dve.tensor_tensor(TMP[:, 1], H0[:, 1], y, ALU.mult))
                do.wait()
                do(dve.tensor_tensor(HS[:, part], TMP[:, 0], TMP[:, 1], op))
                do.wait()
                do(dve.tensor_tensor(HS[:, part], HS[:, part], BU[:, part], ALU.add))
            ds = gain[:, D_SKIP:D_SKIP + 8].unsqueeze(2).to_broadcast([P, 8, TS])
            do(dve.tensor_tensor(Y[:, 8:16, TP:NT], Z[:, U0:NZ, TP:NT], ds, ALU.mult))
            do.wait()
            dve.wait_ge(S("s5_cs"), 1)
            do(dve.tensor_tensor(Y[:, 8:16, TP:NT], Y[:, 8:16, TP:NT],
                                 bank[6][:, 0:8 * TS].rearrange("p (q b) -> p q b", b=TS), ALU.add))

        def pe_s5_samples(pe):
            pe.wait_ge(S("s5_y"), 8)
            pe.wait_ge(S("s5_smp"), 8)
            for j in range(ST):
                jj, q = j % 4, j // 4
                for part in range(2):
                    mm = pe.matmul(bank[6][32 * jj:32 * jj + 32, q * TS:(q + 1) * TS], lhsT=CT[:, part, j, :],
                                   rhs=HS[:, part, j, :], start=(part == 0), stop=(part == 1),
                                   tile_position=(0, 32 * jj))
            mm.then_inc(S("s5_cs"), 1)

        def pe_mem_tile(pe, n):
            base = tiles_before["xk"]
            pe.wait_ge(S("evac"), base + n - 3)
            if n < 16:
                s = arrived(pe, "xk", n)
                for t in range(KT):
                    mm = pe.matmul(bank[n % 4][:, 0:TP], lhsT=R[:, s, t, :], rhs=M[:, t, :],
                                   start=(t == 0), stop=(t == KT - 1))
            else:
                pair, b = (n - 16) // 2, n % 2
                s = arrived(pe, "xv", 2 * pair)
                arrived(pe, "xv", 2 * pair + 1)
                for t in range(KT):
                    mm = pe.matmul(bank[n % 4][:, 0:TP], lhsT=M[:, t, b * P:(b + 1) * P], rhs=R[:, s:s + 2, t, :],
                                   start=(t == 0), stop=(t == KT - 1))
            mm.then_inc(S("tile"), 1)

        def act_mem_tile(act, n):
            act.wait_ge(S("tile"), tiles_before["xk"] + n + 1)
            dst = MK[:, n, :] if n < 16 else MV[:, n % 2, (n - 16) // 2 * TP:((n - 16) // 2 + 1) * TP]
            act.activation(dst, bank[n % 4][:, 0:TP], ACT.Copy).then_inc(S("evac"), 1)

        def pe_front(pe):
            pe.wait_ge(S("ld_c"), 16)
            pe_norm(pe, "mix", SQ, KT)
            pe.wait_ge(S("mix_x"), KT + 1)
            pe_gemm(pe, "z", X, KT, first=True)
            pe.wait_ge(S("evac"), NZ - 3)
            s = arrived(pe, "gate", 0)
            for t in range(KT):
                mm = pe.matmul(bank[0][0:48, 0:NT], lhsT=ring[:, s * D + t * 48:s * D + (t + 1) * 48], rhs=X[:, t, :],
                               start=(t == 0), stop=(t == KT - 1))
            mm.then_inc(S("tile"), 1)
            pe_b_transposes(pe)
            pe.wait_ge(S("b_kept"), 4)
            pe_norm(pe, "mem", SQM, KT)
            pe.wait_ge(S("mem_x"), KT + 1)
            for j in range(ST):
                pe_s5_input(pe, j)
                pe_mem_tile(pe, j)
                if j >= 1:
                    pe_s5_output(pe, j - 1)
            pe_s5_output(pe, ST - 1)
            pe_s5_samples(pe)
            pe.wait_ge(S("y_gelu"), 1)
            pe_gemm(pe, "glu", Y[:, 8:16, :], 8)

        def act_front(act):
            act.wait_ge(S("ld_x"), 16)
            act.wait_ge(S("ld_c"), 16)
            act_norm(act, "mix", H, SQ, KT, D)
            act_s5_parameters(act)
            copy_gemm(act, "z", Z)
            act.wait_ge(S("tile"), NZ + 1)
            act.activation(gate[0:48, :], bank[0][0:48, 0:NT], ACT.Sigmoid).then_inc(S("evac"), 1)
            act_b_transposes(act)
            act.wait_ge(S("par_dve"), PAR_DONE)
            act.wait_ge(S("ld_m"), 16)
            act_norm(act, "mem", M, SQM, KT, D)
            for j in range(ST):
                act_s5_table(act, j)
                if j >= 1:
                    act_mem_tile(act, j - 1)
            act_mem_tile(act, ST - 1)
            act.wait_ge(S("s5_y"), 8)
            act.wait_ge(S("s5_smp"), 10)
            act.activation(Y[:, 8:16, :], Y[:, 8:16, :], ACT.Gelu_apprx_tanh).then_inc(S("y_gelu"), 1)
            copy_gemm(act, "glu", X, ACT.Sigmoid)

        def dve_front(dve):
            dve.wait_ge(S("ld_g"), 16)
            dve_norm(dve, "mix", X, H, KT, G_MIX)
            assert dve_s5_parameters(dve) == PAR_DONE
            dve_norm(dve, "mem", M, M, KT, G_MEM)
            dve.wait_ge(S("tile"), NZ + 1)
            for j in range(ST):
                dve_s5(dve, j)
                if j >= 5 and j % 4 == 1:
                    dve_s5_skip(dve, j // 4 - 1)
            dve_s5_skip(dve, 7)
            dve_s5_samples(dve)
            dve.wait_ge(S("evac"), tiles_before["glu"] + 8)
            dve.tensor_tensor(Y[:, 8:16, :], Y[:, 8:16, :], X[:, 0:8, :], ALU.mult).then_inc(S("o_ssm"), 1)

        def pool_front(pool):
            pool.dma_start(par[:, :], A["s5_par"].rearrange("p c j -> p (c j)")).then_inc(S("ld_s5"), 16)
            pool.dma_start(mk_t[:, 0:D], A["s5_b"].rearrange("p c n -> p (c n)")).then_inc(S("ld_s5"), 16)
            pool.dma_start(c_st[:, :], A["s5_c"].rearrange("p c n -> p (c n)")).then_inc(S("ld_s5"), 16)
            pool.dma_start(s5s[:, 0:2 * ST * TS], A["s5_h0"].rearrange("p c n -> p (c n)")).then_inc(S("ld_s5"), 16)
            pool.dma_start(m_t[:, :], A["mem_t"].rearrange("p t n -> p (t n)")).then_inc(S("ld_m"), 16)
            pool.dma_start(wcmp[:, :], A["w_cmp"].rearrange("p a b c -> p (a b c)")).then_inc(S("ld_w"), 16)
            pool.dma_start(idx_i[:, :], A["page"].partition_broadcast(P)).then_inc(S("ld_w"), 16)
            for name, src in (("new_k", "buf_k"), ("new_v", "buf_v")):
                pool.dma_start(A[name][:, 0:256 * 256], A[src]).then_inc(S("stored"), 16)
            pool.wait_ge(S("par_dve"), 5)
            pool.wait_ge(S("ld_c"), 16)
            pool.wait_ge(S("tile"), NZ + 1)
            for n in range(ST + 1):
                if n < ST:
                    pool_s5_table(pool, n)
                if n == 1:
                    pool.dma_start(A["z_kv"].rearrange("t p n -> p t n"), Z[:, K_CMP:U0, :]).then_inc(S("z_stored"), 16)
                if n >= 1:
                    pool_s5(pool, n - 1)
            pool.wait_ge(S("s5_im"), 5 * ST)
            pool.dma_start(A["s5_p"], s5p[:, :]).then_inc(S("stored"), 16)
            pool.wait_ge(S("s5_smp"), 8)
            pool.dma_start(A["s5_s"], s5s[:, 4 * ST * TS:6 * ST * TS]).then_inc(S("stored"), 16)
            pool.wait_ge(S("evac"), tiles_before["glu"])
            pool.dma_start(A["m_k"].rearrange("t p n -> p t n"), MK).then_inc(S("m_stored"), 16)
            pool.dma_start(A["m_v"].rearrange("b p n -> p b n"), MV).then_inc(S("m_stored"), 16)

        VN = c_st[:, 0:1024].rearrange("p (b n) -> p b n", b=QB)
        CVN = c_st[0:NC, 1024:1280]
        CK = c_st[:, 1280:1280 + 4 * NC].rearrange("p (t n) -> p t n", n=NC)
        HALVES = c_st[:, 1344:1472]
        WC = wcmp[:, :].rearrange("p (a b j) -> p a b j", a=2, b=2)

        def dve_compress(do, src, dst):
            prod = m_t[:, 0:D].rearrange("p (t g c j) -> p t g c j", t=8, g=2, j=STRIDE)
            for t in range(4):
                for half in range(2):
                    w = WC[:, t // 2, t % 2, half * STRIDE:(half + 1) * STRIDE]
                    do(do.eng.tensor_tensor(prod[:, 2 * t + half], src(t // 2, t % 2),
                                            w.unsqueeze(1).unsqueeze(1).to_broadcast([P, 2, 8, STRIDE]), ALU.mult))
            do.wait()
            do(do.eng.tensor_reduce(HALVES, m_t[:, 0:D].rearrange("p (n j) -> p n j", j=STRIDE), AXX, ALU.add))
            do.wait()
            hv = HALVES.rearrange("p (t h c) -> p t h c", t=4, h=2)
            return do(do.eng.tensor_tensor(dst, hv[:, :, 0, 0:NC], hv[:, :, 1, 1:NC + 1], ALU.add))

        COMPRESSED = 10

        NEW = x_t[0:TS, 2832:3600]
        GATE_S = gn[:, 192:195]

        def pe_by_token(pe):
            for b in range(QB):
                for n, t in enumerate((V_SEL, V_SEL + 1, V_WIN, V_WIN + 1)):
                    tr = pe.transpose(bank[4 + b][:, n * P:(n + 1) * P], Z[:, t, b * P:(b + 1) * P], ident)
                tr.then_inc(S("bt_pe"), 1)
            for b in range(QB):
                pe.transpose(bank[6][:, b * 48:(b + 1) * 48], gate[0:48, b * P:(b + 1) * P], ident[0:48, 0:48])
            pe.transpose(bank[6][0:TS, 96:144], gate[0:48, TP:NT], ident[0:48, 0:48]).then_inc(S("bt_pe"), 1)
            pe.wait_ge(S("evac"), tiles_before["out"])
            for n, t in enumerate((K_WIN, K_WIN + 1, V_SEL, V_SEL + 1, V_WIN, V_WIN + 1)):
                tr = pe.transpose(bank[n // 4][0:TS, n % 4 * P:(n % 4 + 1) * P], Z[:, t, TP:NT], ident)
            tr.then_inc(S("bt_pe"), 1)
            pe_norm(pe, "ssm", X[:, 0:8, :], 8, bk=3)
            pe.wait_ge(S("cmp_p"), COMPRESSED)
            for hp in range(2):
                tr = pe.transpose(bank[7][0:NC, hp * P:(hp + 1) * P], CK[:, 2 + hp, :], ident)
            tr.then_inc(S("bt_pe"), 1)
            pe.wait_ge(S("bt_act"), 4)
            pe.matmul(bank[6][:, 144:192], lhsT=cc("sel", rows=TS), rhs=gn[0:TS, 96:144], start=True, stop=True)\
                .then_inc(S("bt_pe"), 1)
            pe.wait_ge(S("bt_act"), 7)
            pe.wait_ge(S("gate_s"), 1)

        def act_by_token(act):
            act.wait_ge(S("s5_cs"), 1)
            for b in range(QB):
                act.wait_ge(S("bt_pe"), b + 1)
                act.activation(VN[:, b, :], bank[4 + b][:, :], ACT.Copy).then_inc(S("bt_act"), 1)
            act.wait_ge(S("bt_pe"), 3)
            act.activation(gn[:, 0:96], bank[6][:, 0:96], ACT.Copy).then_inc(S("bt_act"), 1)
            act.activation(gn[0:TS, 96:144], bank[6][0:TS, 96:144], ACT.Copy).then_inc(S("bt_act"), 1)
            act.wait_ge(S("bt_pe"), 4)
            act.wait_ge(S("o_ssm"), 1)
            act.activation(NEW[:, 0:512], bank[0][0:TS, :], ACT.Copy).then_inc(S("bt_act"), 1)
            act.activation(NEW[:, 512:768], bank[1][0:TS, 0:256], ACT.Copy).then_inc(S("bt_act"), 1)
            act_norm(act, "ssm", Y[:, 8:16, :], X[:, 0:8, :], 8, 1024, bk=3)
            act.wait_ge(S("bt_pe"), 5)
            act.activation(CVN, bank[7][0:NC, 0:256], ACT.Copy).then_inc(S("bt_act"), 1)

        def dve_by_token(dve):
            dve.wait_ge(S("s5_cs"), 1)
            dve.wait_ge(S("ld_w"), 32)
            do = Counted(dve, S("cmp_p"))
            dve_compress(do, lambda kv, hp: Z[:, K_CMP + 2 * kv + hp, 0:TP].rearrange("p (g c j) -> p g c j", g=2, j=STRIDE), CK)
            dve_sample_queries(dve)
            dve.wait_ge(S("bt_pe"), 6)
            gs = gn[:, 144:192].rearrange("p (r k) -> p r k", k=16)
            dve.tensor_tensor(gs, bank[6][:, 144:192].rearrange("p (r k) -> p r k", k=16),
                              cc("kmask").unsqueeze(1).to_broadcast([P, 3, 16]), ALU.mult).then_inc(S("gate_s"), 1)
            dve.wait_ge(S("gate_s"), 1)
            dve.tensor_reduce(GATE_S, gs, AXX, ALU.add).then_inc(S("gate_s"), 1)
            dve_norm(dve, "ssm", Y[:, 8:16, :], Y[:, 8:16, :], 8, G_SSM)

        UNITS = QB * HEADS
        SC = [m_t[:, b * 1056:b * 1056 + 528] for b in range(2)]
        PR = [m_t[:, b * 1056 + 528:(b + 1) * 1056] for b in range(2)]
        PT = [m_t[:, 2112 + b * 640:2112 + (b + 1) * 640] for b in range(2)]

        def st(b, k, n=3):
            return small[:, b * 24 + 3 * k:b * 24 + 3 * k + n]

        def unit(u):
            qb, hp, g, hh = u // 16, u // 8 % 2, u // 2 % 4, u % 2
            return qb, hp, g, hh, P * (qb + 1), 4 * (2 * hp + hh) + g

        A1, A2 = 5, 6

        def pe_scores(pe, u):
            qb, hp, g, hh, nk, _ = unit(u)
            r = slice(64 * hh, 64 * hh + 64)
            if u >= 2:
                pe.wait_ge(S("att_d1"), A1 * (u - 2) + 2)
                pe.wait_ge(S("att_pt"), 2 * (u - 1))
            q = Z[r, 4 * hp + g, qb * P:(qb + 1) * P]
            pe.matmul(bank[u % 2][:, 0:nk], lhsT=q, rhs=Z[r, K_SEL + hp, 0:nk], start=True, stop=True)
            pe.matmul(bank[u % 2][:, 256:256 + nk], lhsT=q, rhs=Z[r, K_WIN + hp, 0:nk], start=True, stop=True)
            pe.matmul(bank[2 + u % 2][:, 0:NC], lhsT=q, rhs=CK[r, hp, :], start=True, stop=True).then_inc(S("att_s"), 1)

        def dve_max(dve, u):
            qb, hp, g, hh, nk, head = unit(u)
            b = u % 2
            do = Counted(dve, S("att_d1"), A1 * u)
            dve.wait_ge(S("att_s"), u + 1)
            if u >= 2:
                dve.wait_ge(S("att_e"), 3 * (u - 1))
            sc = SC[b][:, 0:2 * nk].rearrange("p (r n) -> p r n", r=2)
            do(dve.scalar_tensor_tensor(
                out=sc, in0=cc(f"d{qb}").unsqueeze(1).to_broadcast([P, 2, nk]), scalar=SLOPE[head] / SCALE,
                in1=bank[b][:, :].rearrange("p (r n) -> p r n", r=2)[:, :, 0:nk], op0=ALU.mult, op1=ALU.add))
            do(dve.scalar_tensor_tensor(out=SC[b][:, 512:512 + NC], in0=cc("dc", qb * NC, NC), scalar=SLOPE[head] / SCALE,
                                        in1=bank[2 + b][:, 0:NC], op0=ALU.mult, op1=ALU.add))
            do.wait()
            do(dve.tensor_reduce(st(b, 0, 2), sc, AXX, ALU.max))
            do(dve.tensor_reduce(st(b, 0)[:, 2:3], SC[b][:, 512:512 + NC], AXX, ALU.max))
            do.wait()
            do(dve.tensor_scalar(st(b, 1), st(b, 0), -SCALE, None, ALU.mult))

        def act_exp(act, u):
            nk, b = unit(u)[4], u % 2
            act.wait_ge(S("att_d1"), A1 * (u + 1))
            if u >= 2:
                act.wait_ge(S("att_t"), u - 1)
            for r in range(2):
                act.activation(PR[b][:, r * nk:(r + 1) * nk], SC[b][:, r * nk:(r + 1) * nk], ACT.Exp, scale=SCALE,
                               bias=st(b, 1)[:, r:r + 1], accum_out=st(b, 2)[:, r:r + 1]).then_inc(S("att_e"), 1)
            act.activation(PR[b][:, 512:512 + NC], SC[b][:, 512:512 + NC], ACT.Exp, scale=SCALE,
                           bias=st(b, 1)[:, 2:3]).then_inc(S("att_e"), 1)

        def dve_weights(dve, u):
            qb, hp, g, hh, nk, head = unit(u)
            b = u % 2
            do = Counted(dve, S("att_d2"), A2 * u)
            dve.wait_ge(S("att_e"), 3 * (u + 1))
            do(dve.scalar_tensor_tensor(out=PR[b][:, 512:512 + NC], in0=PR[b][:, 512:512 + NC], scalar=1.0,
                                        in1=cc("mc", qb * NC, NC), op0=ALU.mult, op1=ALU.mult,
                                        accum_out=st(b, 2)[:, 2:3]))
            do.wait()
            do(dve.tensor_scalar(st(b, 3), st(b, 2), TINY, None, ALU.max))
            do.wait()
            do(dve.reciprocal(st(b, 4), st(b, 3)))
            do.wait()
            gv = gn[:, qb * 48:(qb + 1) * 48].rearrange("p (r k) -> p r k", k=16)
            rc = st(b, 4)
            for k, (r, where) in enumerate(((1, slice(0, nk)), (2, slice(nk, 2 * nk)), (0, slice(512, 512 + NC)))):
                do(dve.tensor_scalar(PR[b][:, where], PR[b][:, where], rc[:, k:k + 1], gv[:, r, head:head + 1],
                                     ALU.mult, ALU.mult))

        def pe_turn(pe, u):
            nk, b = unit(u)[4], u % 2
            pe.wait_ge(S("att_d2"), A2 * (u + 1))
            if u >= 2:
                pe.wait_ge(S("att_pt"), 2 * (u - 1))
            for n in range(2 * nk // P):
                pe.transpose(bank[4 + b][:, n * P:(n + 1) * P], PR[b][:, n * P:(n + 1) * P], ident)
            pe.transpose(bank[2 + b][0:NC, 64:64 + P], PR[b][:, 512:512 + NC], ident).then_inc(S("att_t"), 1)

        def act_keep(act, u):
            nk, b = unit(u)[4], u % 2
            act.wait_ge(S("att_t"), u + 1)
            if u >= 2:
                act.wait_ge(S("att_pv"), u - 1)
            act.activation(PT[b][:, 0:2 * nk], bank[4 + b][:, 0:2 * nk], ACT.Copy).then_inc(S("att_pt"), 1)
            act.activation(PT[b][0:NC, 512:640], bank[2 + b][0:NC, 64:64 + P], ACT.Copy).then_inc(S("att_pt"), 1)

        def pe_values(pe, u):
            qb, hp, g, hh, nk, _ = unit(u)
            b, pair = u % 2, u // 2
            kv = slice((2 * hp + hh) * HD, (2 * hp + hh + 1) * HD)
            pe.wait_ge(S("att_pt"), 2 * (u + 1))
            if pair >= 2:
                pe.wait_ge(S("att_o"), pair - 1)
            out = bank[6 + pair % 2][64 * hh:64 * hh + 64, 0:P]
            n = nk // P
            for r in range(2):
                for k in range(n):
                    pe.matmul(out, lhsT=VN[:, k, r * 256 + kv.start:r * 256 + kv.stop],
                              rhs=PT[b][:, (r * n + k) * P:(r * n + k + 1) * P], start=(r == 0 and k == 0), stop=False,
                              tile_position=(0, 64 * hh))
            pe.matmul(out, lhsT=CVN[:, kv], rhs=PT[b][0:NC, 512:640], start=False, stop=True,
                      tile_position=(0, 64 * hh)).then_inc(S("att_pv"), 1)

        def act_attended(act, pair):
            qb, hp, g = unit(2 * pair)[:3]
            act.wait_ge(S("att_pv"), 2 * (pair + 1))
            act.activation(Y[:, 4 * hp + g, qb * P:(qb + 1) * P], bank[6 + pair % 2][:, 0:P], ACT.Copy)\
                .then_inc(S("att_o"), 1)

        ST_T, ST_C, ST_N = x_t[:, 0:512], x_t[0:NC, 1952:2080], x_t[0:1, 1696:1952]
        SS = x_t[:, 512:1041]
        PTS, PTC, PTN = x_t[:, 1056:1568], x_t[0:NC, 1568:1696], x_t[0:TS, 2096:2352]
        PN = x_t[:, 2080:2096]
        CKS = x_t[:, 2352:2832].rearrange("p (t b n) -> p t b n", t=4, b=TS)
        CVS = b_st[0:NC, :]
        NK = PAST + 1

        QZ = x_t[:, 3600:3728]

        def qs(hp, b):
            return QZ[:, b * 16 + hp * 8:b * 16 + hp * 8 + 8]

        def dve_sample_queries(dve):
            q = QZ.rearrange("p (b h e g) -> p b h e g", b=TS, h=2, e=2)
            dve.memset(QZ, 0.0).then_inc(S("qz"), 1)
            dve.wait_ge(S("qz"), 1)
            for hh in range(2):
                r = slice(64 * hh, 64 * hh + 64)
                dve.tensor_copy(q[r, :, :, hh, :], Z[r, 0:8, TP:NT].rearrange("p (h g) b -> p b h g", h=2)).then_inc(S("qz"), 1)

        def dve_index(dve):
            do = Counted(dve, S("idx"))
            dve.wait_ge(S("ld_w"), 32)
            dve.wait_ge(S("ld_c"), 16)
            do(dve.tensor_copy(small[:, 48:64], idx_i[:, :]))
            do.wait()
            do(dve.tensor_scalar(small[:, 64:80], small[:, 48:64], float(P), cc("pidx"), ALU.mult, ALU.add))
            do.wait()
            do(dve.tensor_copy(idx_i[:, :], small[:, 64:80]))

        def pool_caches(pool):
            pool.wait_ge(S("idx"), 3)
            for b in range(TS):
                free(pool, start["dk"] + b)
                s, by, _ = full["dk", b]
                at_ = lambda o, n=256: ring[:, s * D + o:s * D + o + n]
                for pg in range(2):
                    ix = bass.IndirectOffsetOnAxis(idx_i[:, 2 * b + pg:2 * b + pg + 1], 0)
                    for name, o in (("pool_ks", 0), ("pool_kc", 1024), ("pool_vc", 1536)):
                        pool.indirect_dma_start(at_(o + 256 * pg), None, A[name], ix).then_inc(S(by), 16)
                pool.dma_start(at_(512, 512), A["win_k"][b]).then_inc(S(by), 16)
            for b in range(TS):
                free(pool, start["dv"] + b)
                s, by, _ = full["dv", b]
                at_ = lambda o, n=256: ring[:, s * D + o:s * D + o + n]
                for pg in range(2):
                    ix = bass.IndirectOffsetOnAxis(idx_i[:, 2 * b + pg:2 * b + pg + 1], 0)
                    pool.indirect_dma_start(at_(256 * pg), None, A["pool_vs"], ix).then_inc(S(by), 16)
                pool.dma_start(at_(512, 512), A["win_v"][b]).then_inc(S(by), 16)

        def pool_new_rows(pool):
            pool.wait_ge(S("bt_act"), 6)
            for name, a in (("new_k", 0), ("new_v", 512)):
                pool.dma_start(A[name][:, 256 * 256:257 * 256], NEW[:, a:a + 256]).then_inc(S("new_stored"), 16)

        def dve_sample_compress(dve):
            dve.wait_ge(S("att_o"), UNITS // 2)
            dve.wait_ge(S("o_ssm"), 1)
            do = Counted(dve, S("cmp_s"))
            for b in range(TS):
                s = arrived(dve, "dk", b)
                if b:
                    do.wait()
                dve_compress(do, lambda kv, hp: ring[:, s * D + 1024 + 512 * kv:s * D + 1536 + 512 * kv].rearrange(
                    "p (g h c j) -> p g h c j", g=2, h=2, j=STRIDE)[:, :, hp], CKS[:, :, b, :])

        def pe_sample_scores(pe):
            pe.wait_ge(S("att_d1"), A1 * UNITS)
            pe.wait_ge(S("att_pt"), 2 * UNITS)
            pe.wait_ge(S("o_ssm"), 1)
            pe.wait_ge(S("qz"), 3)
            for b in range(TS):
                s = arrived(pe, "dk", b)
                for hp in range(2):
                    c = b * 16 + hp * 8
                    for m in range(4):
                        o = s * D + m * 256 + hp * P
                        pe.matmul(bank[0][:, m * P + c:m * P + c + 8], lhsT=ring[:, o:o + P], rhs=qs(hp, b),
                                  start=True, stop=True)
                    for n, t in enumerate((K_SEL, K_WIN)):
                        pe.matmul(bank[2][0:1, n * P + c:n * P + c + 8], lhsT=Z[:, t + hp, TP + b:TP + b + 1],
                                  rhs=qs(hp, b), start=True, stop=True)
                pe.wait_ge(S("cmp_s"), COMPRESSED * (b + 1))
                for hp in range(2):
                    c = b * 16 + hp * 8
                    mm = pe.matmul(bank[1][0:NC, c:c + 8], lhsT=CKS[:, hp, b, :], rhs=qs(hp, b), start=True, stop=True)
                mm.then_inc(S("dk_used"), 1)
            pe.wait_ge(S("dec_act"), 3)
            for r in range(2):
                for n in range(2):
                    pe.transpose(bank[3 + r][:, n * P:(n + 1) * P], ST_T[:, (2 * r + n) * P:(2 * r + n + 1) * P], ident)
                pe.transpose(bank[3 + r][:, PAST:NK], ST_N[:, r * P:(r + 1) * P], ident[0:1, 0:1])
            pe.transpose(bank[5][:, 0:NC], ST_C, ident[0:NC, 0:NC]).then_inc(S("dec_pe"), 1)
            for n in range(4):
                for k in range(4):
                    b, hp = (4 * n + k) // 2, k % 2
                    tr = pe.transpose(bank[(0, 1, 2, 6)[n]][0:NC, k * P:(k + 1) * P], CKS[:, 2 + hp, b, :], ident)
            tr.then_inc(S("dec_pe"), 1)
            pe.wait_ge(S("dec_dve"), 13)
            pe.wait_ge(S("dec_act"), 10)
            for n in range(4):
                r, k = n // 2, n % 2
                pe.transpose(bank[6][:, n * P:(n + 1) * P], SS[:, r * NK + k * P:r * NK + (k + 1) * P], ident)
            pe.transpose(bank[7][0:NC, 0:P], SS[:, 2 * NK:2 * NK + NC], ident)
            for r in range(2):
                tr = pe.transpose(bank[7][0:TS, P * (r + 1):P * (r + 2)], PN[:, r * TS:(r + 1) * TS], ident)
            tr.then_inc(S("dec_pe"), 1)

        def act_sample_scores(act):
            act.wait_ge(S("dk_used"), TS)
            act.activation(ST_T, bank[0][:, :], ACT.Copy).then_inc(S("dec_act"), 1)
            act.activation(ST_C, bank[1][0:NC, 0:P], ACT.Copy).then_inc(S("dec_act"), 1)
            act.activation(ST_N, bank[2][0:1, 0:256], ACT.Copy).then_inc(S("dec_act"), 1)
            act.wait_ge(S("dec_pe"), 2)
            for n in range(4):
                act.activation(CVS[:, n * 512:(n + 1) * 512], bank[(0, 1, 2, 6)[n]][0:NC, :], ACT.Copy).then_inc(S("dec_act"), 1)
            act.wait_ge(S("dec_dve"), 6)
            for r, (a, n) in enumerate(((0, NK), (NK, NK), (2 * NK, NC))):
                act.activation(SS[:, a:a + n], SS[:, a:a + n], ACT.Exp, scale=SCALE, bias=st(0, 1)[:, r:r + 1],
                               accum_out=st(0, 2)[:, r:r + 1]).then_inc(S("dec_act"), 1)
            act.wait_ge(S("dec_pe"), 3)
            act.activation(PTS, bank[6][:, :], ACT.Copy).then_inc(S("dec_act"), 1)
            act.activation(PTC, bank[7][0:NC, 0:P], ACT.Copy).then_inc(S("dec_act"), 1)
            act.activation(PTN, bank[7][0:TS, P:3 * P], ACT.Copy).then_inc(S("dec_act"), 1)
            act.wait_ge(S("dv_used"), TS)
            o = bank[5][:, 0:P].rearrange("p (h b e) -> p h e b", h=2, b=TS)
            for hh in range(2):
                r = slice(64 * hh, 64 * hh + 64)
                act.activation(Y[r, 0:8, TP:NT].rearrange("p (h g) b -> p h g b", h=2), o[r, :, 4 * hh:4 * hh + 4, :],
                               ACT.Copy).then_inc(S("dec_out"), 1)

        def dve_sample_weights(dve):
            do = Counted(dve, S("dec_dve"))
            dve.wait_ge(S("dec_pe"), 1)
            for r in range(2):
                do(dve.tensor_tensor(SS[:, r * NK:(r + 1) * NK], bank[3 + r][:, 0:NK], cc("ds"), ALU.add))
            do(dve.tensor_tensor(SS[:, 2 * NK:2 * NK + NC], bank[5][:, 0:NC], cc("dcs"), ALU.add))
            do.wait()
            do(dve.tensor_reduce(st(0, 0, 2), SS[:, 0:2 * NK].rearrange("p (r n) -> p r n", r=2), AXX, ALU.max))
            do(dve.tensor_reduce(st(0, 0)[:, 2:3], SS[:, 2 * NK:2 * NK + NC], AXX, ALU.max))
            do.wait()
            do(dve.tensor_scalar(st(0, 1), st(0, 0), -SCALE, None, ALU.mult))
            dve.wait_ge(S("dec_act"), 10)
            do(dve.tensor_scalar(st(0, 3), st(0, 2), TINY, None, ALU.max))
            do.wait()
            do(dve.reciprocal(st(0, 4), st(0, 3)))
            do.wait()
            rc = st(0, 4)
            for k, (r, a, n) in enumerate(((1, 0, NK), (2, NK, NK), (0, 2 * NK, NC))):
                do(dve.tensor_scalar(SS[:, a:a + n], SS[:, a:a + n], rc[:, k:k + 1], GATE_S[:, r:r + 1], ALU.mult, ALU.mult))
            do.wait()
            for r in range(2):
                a = r * NK + PAST
                do(dve.tensor_scalar(PN[:, r * TS:(r + 1) * TS], cc("selT"), SS[:, a:a + 1], None, ALU.mult))
            return do.n

        def pe_sample_values(pe):
            pe.wait_ge(S("dec_act"), 13)
            out = bank[5]
            for hp in range(2):
                for r in range(2):
                    pe.matmul(out[:, hp * 64:(hp + 1) * 64], lhsT=NEW[:, 256 * (r + 1) + hp * P:256 * (r + 1) + (hp + 1) * P],
                              rhs=PTN[:, r * P:(r + 1) * P].rearrange("k (b e) -> k b e", e=16)[:, :, hp * 8:hp * 8 + 8],
                              start=(hp == 0 and r == 0), stop=False, skip_group_check=True)
            for b in range(TS):
                s = arrived(pe, "dv", b)
                for hp in range(2):
                    o, c = out[:, hp * 64 + b * 8:hp * 64 + b * 8 + 8], b * 16 + hp * 8
                    for m in range(4):
                        a = s * D + m * 256 + hp * P
                        pe.matmul(o, lhsT=ring[:, a:a + P], rhs=PTS[:, m * P + c:m * P + c + 8], start=False, stop=False,
                                  skip_group_check=True)
                    mm = pe.matmul(o, lhsT=CVS[:, (2 * b + hp) * P:(2 * b + hp + 1) * P], rhs=PTC[:, c:c + 8],
                                   start=False, stop=True, skip_group_check=True)
                mm.then_inc(S("dv_used"), 1)

        XQ = z_t[:, 0:KT * NT].rearrange("p (t n) -> p t n", n=NT)
        XP = [m_t[:, b * 256:(b + 1) * 256] for b in range(2)]
        XT = [m_t[:, 512 + b * 512:512 + (b + 1) * 512].rearrange("p (m n) -> p m n", m=2) for b in range(2)]
        XST, XSP, XTS = m_t[:, 1536:1600], m_t[0:32, 1600:1856], m_t[:, 1856:1920]

        def pe_cross(pe):
            pe.wait_ge(S("evac"), tiles_before["xo"])

            def scores(u):
                h, qb = u // 2, u % 2
                if u >= 2:
                    pe.wait_ge(S("x_e"), u - 1)
                for d in range(4):
                    mm = pe.matmul(bank[u % 2][:, 0:MEM], lhsT=XQ[:, 4 * h + d, qb * P:(qb + 1) * P],
                                   rhs=MK[:, 4 * h + d, :], start=(d == 0), stop=(d == 3))
                mm.then_inc(S("x_s"), 1)

            def values(h):
                pe.wait_ge(S("x_pt"), 2 * h + 2)
                if h:
                    pe.wait_ge(S("x_o"), 4 * h)
                for d in range(4):
                    for m in range(2):
                        mm = pe.matmul(bank[4 + d][:, 0:TP], lhsT=MV[:, m, h * XD + d * P:h * XD + (d + 1) * P],
                                       rhs=XT[h % 2][:, m, :], start=(m == 0), stop=(m == 1))
                mm.then_inc(S("x_pv"), 1)

            scores(0)
            for u in range(8):
                if u < 7:
                    scores(u + 1)
                if u >= 3 and u % 2:
                    values(u // 2 - 1)
                pe.wait_ge(S("x_d"), 4 * (u + 1))
                if u >= 2:
                    pe.wait_ge(S("x_pt"), u - 1)
                for m in range(2):
                    tr = pe.transpose(bank[2 + u % 2][:, m * P:(m + 1) * P], XP[u % 2][:, m * P:(m + 1) * P], ident)
                tr.then_inc(S("x_t"), 1)
            values(3)
            for j in range(16):
                b, half = j // 2, j % 2
                s = arrived(pe, "mk", j)
                for h in range(2):
                    for m in range(2):
                        c = m * 32 + b * 4 + 2 * half + h
                        for d in range(4):
                            t = 4 * h + d
                            o = s * D + t * 256 + m * P
                            mm = pe.matmul(bank[0][:, c:c + 1], lhsT=ring[:, o:o + P],
                                           rhs=XQ[:, 8 * half + t, TP + b:TP + b + 1], start=(d == 0), stop=(d == 3))
                mm.then_inc(S("mk_used"), 1)
            pe.wait_ge(S("xs_act"), 1)
            for m in range(2):
                tr = pe.transpose(bank[1][0:32, m * P:(m + 1) * P], XST[:, m * 32:(m + 1) * 32], ident)
            tr.then_inc(S("xs_pe"), 1)
            pe.wait_ge(S("xs_dve"), 4)
            for m in range(2):
                tr = pe.transpose(bank[2][:, m * 32:(m + 1) * 32], XSP[:, m * P:(m + 1) * P], ident[0:32, 0:32])
            tr.then_inc(S("xs_pe"), 1)
            pe.wait_ge(S("xs_act"), 3)
            for j in range(16):
                b, m = j // 2, j % 2
                s = arrived(pe, "mv", j)
                for d in range(KT):
                    c = m * 32 + b * 4 + d // 4
                    mm = pe.matmul(bank[3][:, d * TS + b:d * TS + b + 1], lhsT=ring[:, s * D + d * P:s * D + (d + 1) * P],
                                   rhs=XTS[:, c:c + 1], start=(j == 0 and d == 0), stop=(j == 15 and d == KT - 1),
                                   skip_group_check=True)
                mm.then_inc(S("mv_used"), 1)

        def dve_cross(dve):
            do = Counted(dve, S("x_d"))

            def outputs(h):
                dve.wait_ge(S("x_pv"), h + 1)
                for d in range(4):
                    dve.tensor_copy(Y[:, 4 * h + d, 0:TP], bank[4 + d][:, 0:TP]).then_inc(S("x_o"), 1)

            for u in range(8):
                b = u % 2
                dve.wait_ge(S("x_s"), u + 1)
                do(dve.tensor_reduce(st(b, 0, 1), bank[b][:, 0:MEM], AXX, ALU.max))
                do.wait()
                do(dve.tensor_scalar(st(b, 1, 1), st(b, 0, 1), -XSCALE, None, ALU.mult))
                dve.wait_ge(S("x_e"), u + 1)
                do(dve.reciprocal(st(b, 3, 1), st(b, 2, 1)))
                do.wait()
                do(dve.tensor_scalar(XP[b], XP[b], st(b, 3, 1), None, ALU.mult))
                if u >= 4 and u % 2 == 0:
                    outputs(u // 2 - 2)
            outputs(2)
            outputs(3)
            do = Counted(dve, S("xs_dve"))
            dve.wait_ge(S("xs_pe"), 1)
            do(dve.tensor_reduce(small[0:32, 0:1], bank[1][0:32, 0:MEM], AXX, ALU.max))
            do.wait()
            do(dve.tensor_scalar(small[0:32, 3:4], small[0:32, 0:1], -XSCALE, None, ALU.mult))
            dve.wait_ge(S("xs_act"), 2)
            do(dve.reciprocal(small[0:32, 9:10], small[0:32, 6:7]))
            do.wait()
            do(dve.tensor_scalar(XSP, XSP, small[0:32, 9:10], None, ALU.mult))

        def act_cross(act):
            def keep(u):
                h, qb = u // 2, u % 2
                act.wait_ge(S("x_t"), u + 1)
                if h >= 2:
                    act.wait_ge(S("x_pv"), h - 1)
                act.activation(XT[h % 2][:, :, qb * P:(qb + 1) * P],
                               bank[2 + u % 2][:, 0:256].rearrange("p (m n) -> p m n", m=2), ACT.Copy).then_inc(S("x_pt"), 1)

            for u in range(8):
                b = u % 2
                act.wait_ge(S("x_d"), 4 * u + 2)
                if u >= 2:
                    act.wait_ge(S("x_t"), u - 1)
                act.activation(XP[b], bank[b][:, 0:MEM], ACT.Exp, scale=XSCALE, bias=st(b, 1, 1),
                               accum_out=st(b, 2, 1)).then_inc(S("x_e"), 1)
                if u:
                    keep(u - 1)
            keep(7)
            act.wait_ge(S("mk_used"), 16)
            act.activation(XST, bank[0][:, 0:64], ACT.Copy).then_inc(S("xs_act"), 1)
            act.wait_ge(S("xs_dve"), 2)
            act.activation(XSP, bank[1][0:32, 0:MEM], ACT.Exp, scale=XSCALE, bias=small[0:32, 3:4],
                           accum_out=small[0:32, 6:7]).then_inc(S("xs_act"), 1)
            act.wait_ge(S("xs_pe"), 2)
            act.activation(XTS, bank[2][:, 0:64], ACT.Copy).then_inc(S("xs_act"), 1)
            act.wait_ge(S("mv_used"), 16)
            act.activation(Y[:, 0:KT, TP:NT], bank[3][:, 0:KT * TS].rearrange("p (t b) -> p t b", b=TS), ACT.Copy)\
                .then_inc(S("xs_out"), 1)

        def pe_middle(pe):
            pe_by_token(pe)
            pe_scores(pe, 0)
            for u in range(UNITS):
                if u + 1 < UNITS:
                    pe_scores(pe, u + 1)
                if u >= 1:
                    pe_values(pe, u - 1)
                pe_turn(pe, u)
            pe_values(pe, UNITS - 1)
            pe_sample_scores(pe)
            pe_sample_values(pe)
            pe_norm(pe, "att", X[:, 0:8, :], 8)
            pe.wait_ge(S("att_x"), 9)
            pe.wait_ge(S("ssm_x"), 9)
            pe_gemm(pe, "out", Y, KT)
            pe_norm(pe, "x", SQ, KT)
            pe.wait_ge(S("x_x"), KT + 1)
            pe_gemm(pe, "xq", X, KT)
            pe_cross(pe)
            pe.wait_ge(S("x_o"), 16)
            pe.wait_ge(S("xs_out"), 1)
            pe_gemm(pe, "xo", Y, KT)
            pe_norm(pe, "ffn", SQ, KT)
            pe_by_rows(pe)
            pe.wait_ge(S("ffn_x"), KT + 1)
            pe_gemm(pe, "pq", X, KT)

        def act_middle(act):
            act_by_token(act)
            for u in range(UNITS):
                act_exp(act, u)
                if u >= 1:
                    act_keep(act, u - 1)
                if u >= 3 and u % 2:
                    act_attended(act, (u - 3) // 2)
            act_keep(act, UNITS - 1)
            act_attended(act, UNITS // 2 - 1)
            act_sample_scores(act)
            act.wait_ge(S("dec_out"), 2)
            act_norm(act, "att", Y[:, 0:8, :], X[:, 0:8, :], 8, 1024)
            act.wait_ge(S("evac"), tiles_before["xq"])
            act_norm(act, "x", H, SQ, KT, D)
            act.wait_ge(S("z_stored"), 16)
            copy_gemm(act, "xq", XQ)
            act_cross(act)
            act.wait_ge(S("evac"), tiles_before["pq"])
            act_norm(act, "ffn", H, SQ, KT, D)
            act_by_rows(act)
            copy_gemm(act, "pq", XQ)

        def dve_middle(dve):
            dve_by_token(dve)
            dve_max(dve, 0)
            for u in range(UNITS):
                if u + 1 < UNITS:
                    dve_max(dve, u + 1)
                dve_weights(dve, u)
            dve_sample_compress(dve)
            dve_sample_weights(dve)
            dve_norm(dve, "att", Y[:, 0:8, :], Y[:, 0:8, :], 8, G_ATT)
            add_gemm(dve, "out", H)
            dve.wait_ge(S("new_stored"), 32)
            dve_norm(dve, "x", X, H, KT, G_X)
            dve_cross(dve)
            add_gemm(dve, "xo", H)
            dve_norm(dve, "ffn", X, H, KT, G_FFN)
            dve_by_rows(dve)

        def pool_middle(pool):
            pool_new_rows(pool)
            pool_caches(pool)
            pool.wait_ge(S("evac"), tiles_before["xq"])
            pool.wait_ge(S("z_stored"), 16)
            pool.dma_start(KEYS, A["keys"]).then_inc(S("ld_keys"), 16)
            pool.dma_start(GB, A["g_ffn"].partition_broadcast(P)).then_inc(S("ld_gf"), 16)

        BLOCKS = (P, P, TS)
        HN = [mv_n[:, 0:D], mv_n[:, D:2 * D], b_st[:, :]]
        XN = [y_t[:, 0:D], y_t[:, D:2 * D], c_st[:, :]]
        ACC_S = y_t[:, 0:D]
        GB = z_t[:, KT * NT:KT * NT + D]
        SLOT = [ring[:, i * D:(i + 1) * D] for i in range(4)] + [m_t[:, 0:D], m_t[:, D:2 * D], mk_t[:, 0:D], mk_t[:, D:2 * D]]
        NSLOT = len(SLOT)
        SCO, CAND = x_t[:, 0:D], x_t[:, D:2 * D]
        HOT = h_t[:, 0:D]

        def hw(a, n=SLOTS):
            return h_t[:, D + a:D + a + n]

        VAL, VIX, VIF = hw(0, 256), hw(256, 256), hw(512, 256)
        TOP, PIX, PF, PA, IA, IB = (hw(768 + 128 * i) for i in range(6))
        WGT = [hw(1536 + 128 * i) for i in range(3)]
        ACTV = hw(1920)
        EIX = [z_t[:, 6272 + 128 * i:6272 + 128 * (i + 1)].bitcast(I32) for i in range(2)]
        EXF, EXS = z_t[:, 6528:6536], z_t[:, 6864:6872].bitcast(I32)
        WS, AS, RED, STAT = z_t[:, 6536:6544], z_t[:, 6544:6552], z_t[:, 6552:6568], z_t[:, 6568:6592]
        KEYS = z_t[:, 6592:6848].rearrange("p (c n) -> p c n", c=2)
        IXS = [z_t[:, 6848 + 8 * i:6856 + 8 * i].bitcast(I32) for i in range(2)]
        EXPW = z_t[:, 6880:7008]

        def pe_by_rows(pe):
            pe.wait_ge(S("ffn_rms"), 1)
            for blk, n in enumerate(BLOCKS):
                lo = blk * P
                for q in range(4):
                    k = 4 * blk + q
                    if k >= 4:
                        pe.wait_ge(S("hn_act"), k - 3)
                    for d in range(4):
                        tr = pe.transpose(bank[4 + q][0:n, d * P:(d + 1) * P], H[:, 4 * q + d, lo:lo + n], ident)
                    tr.then_inc(S("hn_pe"), 1)

        def act_row_root(act, blk, junk, tag, base):
            n, c = BLOCKS[blk], STAT[:, base + 3 * blk:base + 3 * blk + 3]
            act.activation(junk[0:n, :], HN[blk][0:n, :], ACT.Square, accum_out=c[0:n, 0:1]).then_inc(S(tag), 1)
            act.wait_ge(S(tag), 2 * blk + 1)
            act.activation(c[0:n, 1:2], c[0:n, 0:1], ACT.Sqrt, bias=cc("eps", rows=n), scale=1.0 / D).then_inc(S(tag), 1)

        def dve_row_scale(dve, blk, dst, tag, done, base):
            n, c = BLOCKS[blk], STAT[:, base + 3 * blk:base + 3 * blk + 3]
            dve.wait_ge(S(tag), 2 * blk + 2)
            dve.reciprocal(c[0:n, 2:3], c[0:n, 1:2]).then_inc(S(done), 1)
            dve.wait_ge(S(done), 2 * blk + 1)
            dve.scalar_tensor_tensor(out=dst[0:n, :], in0=HN[blk][0:n, :], scalar=c[0:n, 2:3], in1=GB[0:n, :],
                                     op0=ALU.mult, op1=ALU.mult).then_inc(S(done), 1)

        def act_by_rows(act):
            act.wait_ge(S("m_stored"), 32)
            for blk, n in enumerate(BLOCKS):
                for q in range(4):
                    act.wait_ge(S("hn_pe"), 4 * blk + q + 1)
                    act.activation(HN[blk][0:n, q * 512:(q + 1) * 512], bank[4 + q][0:n, :], ACT.Copy).then_inc(S("hn_act"), 1)
            act.wait_ge(S("hn_act"), 12)
            for blk in range(3):
                if blk:
                    act.wait_ge(S("row_rms"), 2 * blk)
                act_row_root(act, blk, m_t[:, 0:D], "row_rms", 0)

        def dve_by_rows(dve):
            dve.wait_ge(S("ld_gf"), 16)
            for blk in range(3):
                dve_row_scale(dve, blk, XN[blk], "row_rms", "xn", 0)

        def pe_keys(pe, blk):
            n, lo = BLOCKS[blk], blk * P
            pe.wait_ge(S("evac"), tiles_before["pq"] + 16)
            pe.wait_ge(S("ld_keys"), 16)
            if blk:
                pe.wait_ge(S("sco_act"), 4 * blk)
            for q in range(4):
                for k in range(4):
                    t = 4 * q + k
                    mm = pe.matmul(bank[q][0:n, k * PK:(k + 1) * PK], lhsT=XQ[:, t, lo:lo + n], rhs=KEYS[:, t % 2, :],
                                   start=True, stop=True)
                mm.then_inc(S("sco_pe"), 1)

        TK_KEYS, TK_CAND, TK_IX, TK = 80, 123, 136, 139

        def act_keys(act, blk):
            n = BLOCKS[blk]
            if blk:
                act.wait_ge(S("tk"), TK * (blk - 1) + TK_CAND)
            for q in range(4):
                act.wait_ge(S("sco_pe"), 4 * blk + q + 1)
                act.activation(SCO[0:n, q * 512:(q + 1) * 512], bank[q][0:n, :], ACT.Copy).then_inc(S("sco_act"), 1)
            act.wait_ge(S("tk"), TK * blk + TK_CAND)
            act.activation(WGT[blk][0:n, :], WGT[blk][0:n, :], ACT.Exp).then_inc(S("tk_exp"), 1)

        def dve_sixteen(do, n, src, work, groups, width, val, ix):
            r, eng = slice(0, n), do.eng

            def part(t, m, w=width):
                return t[r, m * w:(m + 1) * w]

            def eight(t, m, k):
                return t[r, m * 16 + 8 * k:m * 16 + 8 * k + 8]

            for m in range(groups):
                do(eng.max(eight(val, m, 0), part(src, m)))
            do.wait()
            for m in range(groups):
                do(eng.match_replace(part(work, m), eight(val, m, 0), part(src, m), -3e38))
                do(eng.max_index(eight(ix, m, 0), eight(val, m, 0), part(src, m)))
            do.wait()
            for m in range(groups):
                do(eng.max(eight(val, m, 1), part(work, m)))
            do.wait()
            for m in range(groups):
                do(eng.max_index(eight(ix, m, 1), eight(val, m, 1), part(work, m)))

        def dve_keys(dve, blk):
            do = Counted(dve, S("tk"), TK * blk)
            if blk:
                do.wait(0)
            dve.wait_ge(S("sco_act"), 4 * (blk + 1))
            dve_sixteen(do, BLOCKS[blk], SCO, HOT, 16, PK, VAL, VIX.bitcast(U32))
            assert do.n == TK_KEYS

        def dve_candidates(dve, blk):
            n, do = BLOCKS[blk], Counted(dve, S("tk"), TK * blk + TK_KEYS)
            do.wait()
            r = slice(0, n)
            v = VAL[r, :].rearrange("p (h c k) -> p h c k", h=PH, c=2)
            do(dve.tensor_copy(VIF[r, :], VIX.bitcast(U32)[r, :]))
            do(dve.tensor_tensor(CAND[r, :].rearrange("p (h a b) -> p h a b", h=PH, a=16),
                                 v[:, :, 0].unsqueeze(3).to_broadcast([n, PH, 16, 16]),
                                 v[:, :, 1].unsqueeze(2).to_broadcast([n, PH, 16, 16]), ALU.add))
            do.wait()
            dve_sixteen(do, n, CAND, SCO, PH, 256, TOP, PIX.bitcast(U32))
            do.wait()
            t3 = TOP[r, :].rearrange("p (h k) -> p h k", h=PH)
            do(dve.tensor_tensor(WGT[blk][r, :].rearrange("p (h k) -> p h k", h=PH), t3,
                                 t3[:, :, 0:1].to_broadcast([n, PH, 16]), ALU.subtract))
            assert do.n + TK_KEYS == TK_CAND

        def dve_experts(dve, blk):
            n, do = BLOCKS[blk], Counted(dve, S("tk"), TK * blk + TK_CAND)
            do.wait()
            r = slice(0, n)
            vi = VIF[r, :].rearrange("p (h c k) -> p h c k", h=PH, c=2)
            do(dve.tensor_copy(PF[r, :], PIX.bitcast(U32)[r, :]))
            do.wait()
            do(dve.tensor_scalar(PA[r, :], PF[r, :], 1 / 16, -15 / 32, ALU.mult, ALU.add))
            do.wait()
            do(dve.tensor_scalar(PA[r, :], PA[r, :], MAGIC, None, ALU.add))
            do.wait()
            do(dve.tensor_scalar(PA[r, :], PA[r, :], MAGIC, None, ALU.subtract))
            do.wait()
            do(dve.scalar_tensor_tensor(out=PF[r, :], in0=PA[r, :], scalar=-16.0, in1=PF[r, :], op0=ALU.mult, op1=ALU.add))
            hot = HOT[r, :].rearrange("p (s k) -> p s k", k=16)
            hot4 = HOT[r, :].rearrange("p (h s k) -> p h s k", h=PH, k=16)
            for c, (pos, out) in enumerate(((PA, IA), (PF, IB))):
                do.wait()
                do(dve.tensor_tensor(hot, cc("iota")[r, :].unsqueeze(1).to_broadcast([n, SLOTS, 16]),
                                     pos[r, :].unsqueeze(2).to_broadcast([n, SLOTS, 16]), ALU.is_equal))
                do.wait()
                do(dve.tensor_tensor(hot4, hot4, vi[:, :, c].unsqueeze(2).to_broadcast([n, PH, 16, 16]), ALU.mult))
                do.wait()
                do(dve.tensor_reduce(out[r, :], hot, AXX, ALU.add))
            do.wait()
            do(dve.scalar_tensor_tensor(out=IA[r, :], in0=IA[r, :], scalar=float(PK), in1=IB[r, :], op0=ALU.mult, op1=ALU.add))
            if blk < 2:
                do.wait()
                do(dve.tensor_copy(EIX[blk], IA))
                assert do.n + TK_CAND == TK_IX
            w3 = WGT[blk][r, :].rearrange("p (h k) -> p h k", h=PH)
            dve.wait_ge(S("tk_exp"), blk + 1)
            do(dve.tensor_reduce(RED[r, 0:8], w3, AXX, ALU.add))
            do.wait()
            do(dve.reciprocal(RED[r, 8:16], RED[r, 0:8]))
            do.wait()
            do(dve.tensor_tensor(w3, w3, RED[r, 8:16].unsqueeze(2).to_broadcast([n, PH, 16]), ALU.mult))
            return do.n

        def pe_samples_expand(pe):
            pe.wait_ge(S("xn"), 6)
            for q in range(4):
                mm = pe.matmul(bank[4 + q][:, :], lhsT=cc("sel", rows=TS), rhs=XN[2][0:TS, q * 512:(q + 1) * 512],
                               start=True, stop=True)
            mm.then_inc(S("ex_pe"), 1)

        def act_samples_expand(act):
            act.wait_ge(S("ex_pe"), 1)
            for q in range(4):
                act.activation(XN[2][:, q * 512:(q + 1) * 512], bank[4 + q][:, :], ACT.Copy).then_inc(S("ex_act"), 1)

        def pe_samples_experts(pe):
            pe.wait_ge(S("ex_act"), 4)
            pe.wait_ge(S("tk"), 2 * TK + TK - 1)
            pe.matmul(bank[4][:, 0:P], lhsT=cc("sel", rows=TS), rhs=IA[0:TS, :], start=True, stop=True)
            pe.matmul(bank[5][:, 0:P], lhsT=cc("sel", rows=TS), rhs=WGT[2][0:TS, :], start=True, stop=True)\
                .then_inc(S("ex_pe"), 1)

        def dve_samples_experts(dve):
            do = Counted(dve, S("ex_dve"))
            dve.wait_ge(S("ex_pe"), 2)
            mask = cc("kmask").unsqueeze(1).to_broadcast([P, PH, 16])
            for n, out in enumerate((EXF, WS)):
                if n:
                    do.wait()
                do(dve.tensor_tensor(EXPW.rearrange("p (h k) -> p h k", h=PH),
                                     bank[4 + n][:, 0:P].rearrange("p (h k) -> p h k", h=PH), mask, ALU.mult))
                do.wait()
                do(dve.tensor_reduce(out, EXPW.rearrange("p (h k) -> p h k", h=PH), AXX, ALU.add))
            do(dve.tensor_scalar(EXF, EXF, MAGIC, None, ALU.add))
            do.wait()
            do(dve.tensor_scalar(EXF, EXF, MAGIC, None, ALU.subtract))
            do.wait()
            do(dve.tensor_copy(EXS, EXF))

        U_OF, V_OF = (0, 2 * SLOTS), (SLOTS, 3 * SLOTS)
        U_S, V_S = 4 * SLOTS, 4 * SLOTS + PH

        def pool_peer(pool):
            with pool.register("round") as rnd, pool.register("use") as use:
                pool.reg_mov(rnd, 3)
                pool.reg_mov(use, 1 + NSLOT)

                def gather(table, half, k):
                    pool.indirect_dma_start(SLOT[k], None, A[table], bass.IndirectOffsetOnAxis(IXS[half][:, k:k + 1], 0))\
                        .then_inc(S(f"slot{k}"), 16)

                def single(table, g, index):
                    half = g // NSLOT % 2
                    pool.tensor_copy(IXS[half], index).then_inc(S("ixs"), 1)
                    pool.wait_ge(S("ixs"), g // NSLOT + 1)
                    for k in range(NSLOT):
                        if g:
                            pool.wait_ge(S("peer_used"), g + k + 1 - NSLOT)
                        gather(table, half, k)

                def gathers(table, blk, i0=0):
                    with pool.Fori(i0, SLOTS // (2 * NSLOT)) as i:
                        for half in range(2):
                            pool.tensor_copy(IXS[half], EIX[blk][:, bass.ds(i * (2 * NSLOT) + half * NSLOT, NSLOT)])\
                                .then_inc(S("ixs"), 1)
                            pool.wait_ge(S("ixs"), rnd)
                            pool.reg_add(rnd, rnd, 1)
                            for k in range(NSLOT):
                                pool.wait_ge(S("peer_used"), use)
                                pool.reg_add(use, use, 1)
                                gather(table, half, k)

                pool.wait_ge(S("tk"), TK_IX)
                for half in range(2):
                    single("peer_u", half * NSLOT, EIX[0][:, half * NSLOT:(half + 1) * NSLOT])
                gathers("peer_u", 0, 1)
                gathers("peer_v", 0)
                pool.wait_ge(S("tk"), TK + TK_IX)
                gathers("peer_u", 1)
                gathers("peer_v", 1)
                pool.wait_ge(S("ex_dve"), 7)
                single("peer_u", U_S, EXS)
                single("peer_v", V_S, EXS)

        def dve_dots(dve, blk, quarter):
            with dve.Fori(quarter * SLOTS // 4 // NSLOT, (quarter + 1) * SLOTS // 4 // NSLOT) as i:
                for k in range(NSLOT):
                    dve.wait_ge(S(f"slot{k}"), i * 16 + 16 * (U_OF[blk] // NSLOT + 1))
                    dve.scalar_tensor_tensor(out=SLOT[k], in0=SLOT[k], scalar=1.0, in1=XN[blk], op0=ALU.mult, op1=ALU.mult,
                                             accum_out=ACTV[:, bass.ds(i * NSLOT + k, 1)]).then_inc(S("peer_used"), 1)

        def dve_sums(dve, blk, quarter):
            with dve.Fori(quarter * SLOTS // 4 // NSLOT, (quarter + 1) * SLOTS // 4 // NSLOT) as i:
                for k in range(NSLOT):
                    dve.wait_ge(S(f"slot{k}"), i * 16 + 16 * (V_OF[blk] // NSLOT + 1))
                    dve.wait_ge(S("peer_used"), i * NSLOT + (V_OF[blk] + k))
                    dve.scalar_tensor_tensor(out=HN[blk], in0=SLOT[k], scalar=WGT[blk][:, bass.ds(i * NSLOT + k, 1)],
                                             in1=HN[blk], op0=ALU.mult, op1=ALU.add).then_inc(S("peer_used"), 1)

        def dve_samples_dots(dve):
            for k in range(PH):
                dve.wait_ge(S(f"slot{k}"), 16 * (U_S // NSLOT + 1))
                dve.scalar_tensor_tensor(out=SLOT[k], in0=SLOT[k], scalar=1.0, in1=XN[2], op0=ALU.mult, op1=ALU.mult,
                                         accum_out=AS[:, k:k + 1]).then_inc(S("peer_used"), 1)

        def dve_samples_sums(dve):
            for k in range(PH):
                dve.wait_ge(S(f"slot{k}"), 16 * (V_S // NSLOT + 1))
                if k == 0:
                    dve.tensor_scalar(ACC_S, SLOT[k], WS[:, k:k + 1], None, ALU.mult).then_inc(S("peer_used"), 1)
                else:
                    dve.wait_ge(S("peer_used"), V_S + k)
                    dve.scalar_tensor_tensor(out=ACC_S, in0=SLOT[k], scalar=WS[:, k:k + 1], in1=ACC_S,
                                             op0=ALU.mult, op1=ALU.add).then_inc(S("peer_used"), 1)
            for q in range(4):
                dve.wait_ge(S("sum_pe"), q + 1)
                dve.tensor_tensor(HN[2][0:TS, q * 512:(q + 1) * 512], HN[2][0:TS, q * 512:(q + 1) * 512],
                                  bank[4 + q][0:TS, :], ALU.add).then_inc(S("sum_s"), 1)

        def pe_samples_sums(pe):
            pe.wait_ge(S("peer_used"), V_S + PH)
            for q in range(4):
                pe.matmul(bank[4 + q][0:TS, :], lhsT=cc("selT"), rhs=ACC_S[:, q * 512:(q + 1) * 512],
                          start=True, stop=True).then_inc(S("sum_pe"), 1)

        def act_gelu(act, blk):
            a, done = (AS, V_S) if blk == 2 else (ACTV, V_OF[blk])
            act.wait_ge(S("peer_used"), done)
            act.activation(a, a, ACT.Gelu_apprx_tanh).then_inc(S("gelu"), 1)

        def dve_gelu(dve, blk):
            w, a = (WS, AS) if blk == 2 else (WGT[blk], ACTV)
            dve.wait_ge(S("gelu"), blk + 1)
            dve.tensor_tensor(w, w, a, ALU.mult).then_inc(S("wgt"), 1)
            dve.wait_ge(S("wgt"), blk + 1)

        def act_final(act, blk):
            if blk < 2:
                act.wait_ge(S("peer_used"), V_OF[blk] + SLOTS)
            else:
                act.wait_ge(S("sum_s"), 4)
            if blk:
                act.wait_ge(S("f_rms"), 2 * blk)
            act_row_root(act, blk, HOT, "f_rms", 9)

        def dve_final(dve, blk):
            if blk == 0:
                dve.wait_ge(S("ld_last"), 16)
            dve_row_scale(dve, blk, HN[blk], "f_rms", "y", 9)

        def sp_peer(sp):
            sp.wait_ge(S("xn"), 6)
            sp.dma_start(GB, A["g_final"].partition_broadcast(P)).then_inc(S("ld_last"), 16)
            for blk in range(3):
                sp.wait_ge(S("y"), 2 * blk + 2)
                dst = A["y_p"][blk * P:(blk + 1) * P, :] if blk < 2 else A["y_s"]
                sp.dma_start(dst, HN[blk][0:BLOCKS[blk], :]).then_inc(S("y_stored"), 16)
            sp.wait_ge(S("y_stored"), 48)

        @block.sync
        def _(sp):
            sp_stream(sp)
            sp_peer(sp)

        @block.tensor
        def _(pe):
            pe_front(pe)
            pe_middle(pe)
            pe_keys(pe, 0)
            pe_keys(pe, 1)
            pe_samples_expand(pe)
            pe_keys(pe, 2)
            pe_samples_experts(pe)
            pe_samples_sums(pe)

        @block.scalar
        def _(act):
            act_front(act)
            act_middle(act)
            act_keys(act, 0)
            act_samples_expand(act)
            act_keys(act, 1)
            act_gelu(act, 0)
            act_keys(act, 2)
            act_final(act, 0)
            act_gelu(act, 1)
            act_final(act, 1)
            act_gelu(act, 2)
            act_final(act, 2)

        @block.vector
        def _(dve):
            dve_index(dve)
            dve_front(dve)
            dve_middle(dve)
            dve_keys(dve, 0)
            dve_candidates(dve, 0)
            dve_experts(dve, 0)
            dve_dots(dve, 0, 0)
            dve_keys(dve, 1)
            dve_dots(dve, 0, 1)
            dve_candidates(dve, 1)
            dve_dots(dve, 0, 2)
            dve_experts(dve, 1)
            dve_dots(dve, 0, 3)
            dve_gelu(dve, 0)
            dve_sums(dve, 0, 0)
            dve_keys(dve, 2)
            dve_sums(dve, 0, 1)
            dve_candidates(dve, 2)
            dve_sums(dve, 0, 2)
            dve_experts(dve, 2)
            dve_sums(dve, 0, 3)
            dve_dots(dve, 1, 0)
            dve_final(dve, 0)
            dve_dots(dve, 1, 1)
            dve_samples_experts(dve)
            dve_dots(dve, 1, 2)
            dve_dots(dve, 1, 3)
            dve_gelu(dve, 1)
            for quarter in range(4):
                dve_sums(dve, 1, quarter)
            dve_samples_dots(dve)
            dve_final(dve, 1)
            dve_gelu(dve, 2)
            dve_samples_sums(dve)
            dve_final(dve, 2)

        @block.gpsimd
        def _(pool):
            pool_front(pool)
            pool_middle(pool)
            pool_peer(pool)
            pool.wait_ge(S("stored"), 64)
            pool.wait_ge(S("z_stored"), 16)
            pool.wait_ge(S("m_stored"), 32)
            pool.wait_ge(S("new_stored"), 32)


def kernel(**inputs):
    import concourse.bacc as bacc
    from concourse.bass_utils import run_bass_kernel_spmd

    a = {k: np.asarray(v) for k, v in inputs.items()}

    def feature_tiles(x):
        return x.T.reshape(-1, P, x.shape[0]).transpose(1, 0, 2)

    def columns(v):
        return v.reshape(-1, P).T

    def weight(w):
        k, n = w.shape
        return w.reshape(k // P, P, n // P, P).transpose(2, 1, 0, 3).reshape(n // P, P, k)

    def pair_heads(w):
        return w.reshape(2, 2, GQ, HD, -1).transpose(0, 2, 1, 3, 4).reshape(HEADS * HD, -1)

    def states(v):
        return np.moveaxis(v.reshape(-1, ST, P), (2, 1, 0), (0, 1, 2))

    def groups(v):
        out = np.zeros((ST, 2, SN, 2, SG), np.float32)
        g = v.reshape(ST, 2, SN, SG)
        out[:, 0, :, 0], out[:, 1, :, 1] = g[:, 0], g[:, 1]
        return out.reshape(ST, P, 32).transpose(1, 0, 2).reshape(P, ST * 32)

    def pages(pool):
        return pool.reshape(20, P, 2, P).transpose(0, 3, 2, 1).reshape(2560, 256)

    tokens = np.concatenate([a["x_prompt"][0], a["x_sample"][:, 0]])
    w_in = a["w_in"][0]
    w_z = np.concatenate([pair_heads(w_in[:, :1024].T).T, w_in[:, 1024:2560], w_in[:, 2608:]], 1)
    w_out = np.concatenate([pair_heads(a["w_out"][0, :1024]), a["w_out"][0, 1024:]])
    log_dt = np.broadcast_to(a["log_dt"][0][:, None], (GROUPS, SN))
    w_cmp = np.stack([np.repeat(a[n][0], HD, 0).reshape(2, P, CMP) for n in ("w_cmp_k", "w_cmp_v")])
    given = {
        "consts": constants(),
        "gains": np.concatenate([columns(x) for x in (
            a["g_mix"][0], a["g_x"][0], a["g_mem"][0], a["g_ffn"][0],
            pair_heads(a["g_attn_out"][0][:, None])[:, 0], a["g_ssm_out"][0], a["d_skip"][0])], 1),
        "x_t": feature_tiles(tokens), "mem_t": feature_tiles(a["mem_prompt"][0]),
        "w_z": weight(w_z), "w_gate": w_in[:, 2560:2608].reshape(KT, P, 48).transpose(1, 0, 2).reshape(P, -1),
        "w_out": weight(w_out),
        **{n: weight(a[n][0]) for n in ("w_xk", "w_xv", "w_glu", "w_xq", "w_xo", "w_pq")},
        "s5_par": np.stack([states(x)[:, :, 0] for x in (a["lam_re"][0], a["lam_im"][0], log_dt)], 1),
        "s5_b": np.stack([groups(a[n][0]) for n in ("b_re", "b_im")], 1),
        "s5_c": np.stack([groups(a[n][0].transpose(0, 2, 1)) for n in ("c_re", "c_im")], 1),
        "s5_h0": np.stack([states(a[n][0]).reshape(P, -1) for n in ("state_s5_re", "state_s5_im")], 1),
        "w_cmp": w_cmp.transpose(2, 0, 1, 3), "page": a["page_table"].reshape(-1),
        "pool_kc": pages(a["cache_k_cmp"][0]), "pool_vc": pages(a["cache_v_cmp"][0]),
        "pool_ks": pages(a["cache_k_sel"][0]), "pool_vs": a["cache_v_sel"][0].reshape(2560, 256),
        "win_k": a["cache_k_win"][0].reshape(TS, 2, P, 2, P).transpose(0, 4, 1, 3, 2).reshape(TS, P, 512),
        "win_v": a["cache_v_win"][0].reshape(TS, 2, P, 256).transpose(0, 2, 1, 3).reshape(TS, P, 512),
        "mem_k": a["cache_mem_k"][0].reshape(TS, MEM, 2, 8, P).transpose(0, 2, 4, 3, 1).reshape(TS, 2, P, D),
        "mem_v": a["cache_mem_v"][0].reshape(TS, 2, P, D),
        "keys": np.stack([a["peer_k1"][0].T, a["peer_k2"][0].T], 1),
        "peer_u": a["peer_u"][0], "peer_v": a["peer_v"][0], "g_ffn": a["g_ffn"][0], "g_final": a["g_final"],
        "buf_k": a["cache_k_win"][0].reshape(TS, -1), "buf_v": a["cache_v_win"][0].reshape(TS, -1),
    }
    nc = bacc.Bacc("TRN2", target_bir_lowering=False, num_devices=1)
    arrays, args = {}, {}
    for name, shape in INS.items():
        x = np.ascontiguousarray(given[name])
        assert x.shape == shape, (name, x.shape, shape)
        arrays["in_" + name] = x
        args[name] = nc.dram_tensor("in_" + name, x.shape, mybir.dt.from_np(x.dtype), kind="ExternalInput").ap()
    for name, shape in OUTS.items():
        args[name] = nc.dram_tensor("out_" + name, shape, F32, kind="ExternalOutput").ap()
    build(nc, args)
    got = run_bass_kernel_spmd(nc, [arrays], core_ids=[0]).results[0]
    o = {name: np.asarray(got["out_" + name]) for name in OUTS}

    z = o["z_kv"].reshape(6, KV, HD, NT)
    kv_p = [z[i, :, :, :TP].transpose(2, 0, 1)[None, None] for i in range(6)]
    kv_s = [z[i, :, :, TP:].transpose(2, 0, 1)[None, :, None] for i in range(6)]

    def of_states(v, n):
        return [x.transpose(2, 1, 0).reshape((1, n, GROUPS, SN)) for x in v.reshape(P, 2, ST, n).swapaxes(0, 1)]

    return (o["y_p"][None], o["y_s"][:, None], *kv_p, *of_states(o["s5_p"], 1),
            o["m_k"].transpose(2, 0, 1).reshape(1, 1, MEM, XH, XD), o["m_v"].reshape(1, 1, MEM, XH, XD),
            *kv_s[:4], *(o[n].reshape(1, TS, 257, KV, HD) for n in ("new_k", "new_v")), *of_states(o["s5_s"], TS))
```

```python
from contextlib import ExitStack

import numpy as np
import concourse.bass as bass
from concourse import mybir

ALU = mybir.AluOpType
ACT = mybir.ActivationFunctionType
AXX = mybir.AxisListType.X
F32 = mybir.dt.float32
I32 = mybir.dt.int32
U32 = mybir.dt.uint32

P = 128
D = 2048
KT = D // P
TP, TS = 256, 8
NT = TP + TS
QB = TP // P
HEADS, KV, GQ, HD = 16, 4, 4, 64
CMP, STRIDE = 32, 16
NC = TP // STRIDE - 1
PAST = 256
SCALE = HD ** -0.5
NEG, TINY, EPS = -1e30, 1e-30, 1e-6
XH, XD, MEM = 4, 512, 256
XSCALE = XD ** -0.5
GROUPS, SG, SN = 64, 16, 64
ST = GROUPS * SN // P
PH, PK, TOPK = 8, 128, 16
SLOTS = PH * TOPK
SLOPE = [2.0 ** (-8.0 * (h + 1) / HEADS) for h in range(HEADS)]
MAGIC = 12582912.0
TWO_PI = 6.2831850

Q0, K_CMP, V_CMP, K_SEL, V_SEL, K_WIN, V_WIN, U0, NZ = 0, 8, 10, 12, 14, 16, 18, 20, 28

C = {}
for _name, _n in (("ident", P), ("ones", P), ("d0", P), ("d1", TP), ("cb", QB * TP), ("mc", QB * 16), ("ds", PAST + 1),
                  ("dcs", NC), ("t", TP), ("sel", P), ("selT", TS), ("kmask", 16), ("selk", P), ("kvm", KV), ("iota", 16), ("pidx", 1),
                  ("half_pi", 1), ("eps", 1)):
    C[_name] = (sum(n for _, n in C.values()), _n)
NCONST = sum(n for _, n in C.values())
G_MIX, G_X, G_MEM, G_FFN, G_ATT, G_SSM, D_SKIP, NGAIN = 0, 16, 32, 48, 64, 72, 80, 88


def constants():
    c = np.zeros((P, NCONST), np.float32)

    def put(name, value):
        a, n = C[name]
        c[: value.shape[0], a:a + n] = value

    p = np.arange(P)
    put("ident", np.eye(P))
    put("ones", np.ones((P, P)))
    for b, name in enumerate(("d0", "d1")):
        n = C[name][1]
        dist = (b * P + p)[:, None] - np.arange(n)[None]
        put(name, np.where(dist >= 0, -dist, NEG))
    n = np.arange(16)
    dist = np.stack([(b * P + p)[:, None] - (n * STRIDE + CMP - 1)[None] for b in range(QB)], 1)
    seen = (dist >= 0) & (n < NC)
    order = [4 * (2 * hp + hh) + g for hp in range(2) for g in range(GQ) for hh in range(2)]
    by_head = np.stack([np.where(seen, -dist * (SLOPE[h] / SCALE), NEG) for h in order], 2)
    put("cb", by_head.reshape(P, -1))
    put("mc", seen.reshape(P, -1))
    slope = np.array([SLOPE[i % HEADS] for i in range(P)])[:, None] / SCALE
    put("ds", -slope * (PAST - np.arange(PAST + 1))[None])
    put("dcs", -slope * (PAST - np.arange(NC) * STRIDE - CMP + 1)[None])
    put("t", np.tile(np.arange(TP), (P, 1)))
    put("sel", (p[None] // 16 == np.arange(TS)[:, None]))
    put("selT", (p[:, None] // 16 == np.arange(TS)[None]))
    put("kmask", (p[:, None] % 16 == np.arange(16)[None]))
    put("selk", (p[None] % 16 == n[:, None]))
    put("kvm", (p[:, None] % 16 // 4 == np.arange(KV)[None]))
    put("iota", np.tile(np.arange(16), (P, 1)))
    put("pidx", p[:, None])
    put("half_pi", np.full((P, 1), np.pi / 2))
    put("eps", np.full((P, 1), EPS))
    return c


INS = {
    "consts": (P, NCONST), "gains": (P, NGAIN), "x_t": (P, KT, NT), "mem_t": (P, KT, TP),
    "w_z": (NZ, P, KT * P), "w_gate": (P, KT * 48), "w_xk": (KT, P, D), "w_xv": (KT, P, D), "w_glu": (8, P, 8 * P),
    "w_out": (KT, P, D), "w_xq": (KT, P, D), "w_xo": (KT, P, D), "w_pq": (KT, P, D),
    "s5_par": (P, 3, ST), "s5_b": (P, 2, ST * 32), "s5_c": (P, 2, ST * 32), "s5_h0": (P, 2, ST * TS),
    "w_cmp": (P, 2, 2, CMP), "page": (16,),
    "pool_kc": (2560, 256), "pool_vc": (2560, 256), "pool_ks": (2560, 256), "pool_vs": (2560, 256),
    "win_k": (TS, P, 512), "win_v": (TS, P, 512), "mem_k": (TS, 2, P, D), "mem_v": (TS, 2, P, D),
    "keys": (P, 2, PK), "peer_u": (16384, D), "peer_v": (16384, D), "g_ffn": (D,), "g_final": (D,),
    "buf_k": (TS, 256 * 256), "buf_v": (TS, 256 * 256),
}
OUTS = {
    "y_p": (TP, D), "y_s": (TS, D), "z_kv": (12, P, NT), "s5_p": (P, 2 * ST), "s5_s": (P, 2 * ST * TS),
    "m_k": (KT, P, TP), "m_v": (QB, P, D), "new_k": (TS, 257 * 256), "new_v": (TS, 257 * 256),
}


class Counted:

    def __init__(self, eng, sem, loop=0):
        self.eng, self.sem, self.n, self.loop = eng, sem, 0, loop

    def __call__(self, ins):
        ins.then_inc(self.sem, 1)
        self.n += 1
        return self.n

    def wait(self, n=None):
        self.eng.wait_ge(self.sem, self.loop + (self.n if n is None else n))


def build(nc, A):
    with ExitStack() as ctx:
        def sb(name, n, dt=F32):
            return ctx.enter_context(nc.sbuf_tensor("sb_" + name, [P, n], dt))

        sems = {}

        def S(name):
            if name not in sems:
                sems[name] = ctx.enter_context(nc.semaphore("s_" + name))
            return sems[name]

        bank = [ctx.enter_context(nc.psum_tensor(f"bank{i}", [P, 512], F32)) for i in range(8)]

        con = sb("con", NCONST)
        gain = sb("gain", NGAIN)
        h_t = sb("h_t", KT * NT)
        x_t = sb("x_t", 19 * 256)
        m_t = sb("m_t", KT * TP)
        y_t = sb("y_t", KT * NT)
        z_t = sb("z_t", NZ * NT)
        gate = sb("gate", NT)
        ring = sb("ring", 4 * D)
        mk_t = sb("mk_t", KT * TP)
        mv_n = sb("mv_n", QB * D)
        b_st = sb("b_st", 2 * 8 * P)
        c_st = sb("c_st", 2 * ST * 32)
        par = sb("par", 3 * ST)
        prm = sb("prm", 26 * ST)
        s5s = sb("s5s", 8 * ST * TS)
        s5p = sb("s5p", 2 * ST)
        wcmp = sb("wcmp", 2 * 2 * CMP)
        rst = sb("rst", 2 * NT)
        gn = sb("gn", 208)
        small = sb("small", 160)
        idx_i = sb("idx_i", 16, I32)

        def cc(name, lo=0, n=None, rows=P):
            a, w = C[name]
            return con[0:rows, a + lo:a + lo + (w - lo if n is None else n)]

        ident = cc("ident")
        H = h_t[:, :].rearrange("p (t n) -> p t n", n=NT)
        X = x_t[:, 0:KT * NT].rearrange("p (t n) -> p t n", n=NT)
        M = m_t[:, :].rearrange("p (t n) -> p t n", n=TP)
        Y = y_t[:, :].rearrange("p (t n) -> p t n", n=NT)
        Z = z_t[:, :].rearrange("p (t n) -> p t n", n=NT)
        R = ring[:, :].rearrange("p (s t n) -> p s t n", s=4, n=P)
        MK = mk_t[:, :].rearrange("p (t n) -> p t n", n=TP)
        MV = mv_n[:, :].rearrange("p (b n) -> p b n", b=QB)

        segs = [("z", NZ), ("gate", 1), ("xk", 16), ("xv", 16), ("glu", 8), ("dk", 8), ("dv", 8), ("out", 16),
                ("xq", 16), ("mk", 16), ("mv", 16), ("xo", 16), ("pq", 16)]
        nd = {"dk": 7, "dv": 3}
        full, start, at, fill = {}, {}, 0, {}
        users = []
        tiles_before, tiles = {}, 0
        for seg, n in segs:
            start[seg] = at
            gemm = seg not in ("dk", "dv", "mk", "mv")
            tiles_before[seg] = tiles
            for j in range(n):
                s = at % 4
                by = ("cache" if seg in nd else "full") + str(s)
                fill[by] = fill.get(by, 0) + 16 * nd.get(seg, 1)
                full[seg, j] = (s, by, fill[by])
                last = j | 1 if seg == "xv" else j
                users.append(("tile", tiles + last + 1) if gemm else (seg + "_used", j + 1))
                at += 1
            tiles += n if gemm else 0
            if seg == "gate":
                at += 3
                users += [None] * 3

        def arrived(eng, seg, j):
            s, by, v = full[seg, j]
            eng.wait_ge(S(by), v)
            return s

        def free(eng, g):
            while g >= 4:
                g -= 4
                if users[g] is not None:
                    eng.wait_ge(S(users[g][0]), users[g][1])
                    return

        block = ctx.enter_context(nc.Block())

        def sp_stream(sp):
            sp.dma_start(h_t[:, :], A["x_t"].rearrange("p t n -> p (t n)")).then_inc(S("ld_x"), 16)
            sp.dma_start(con[:, :], A["consts"]).then_inc(S("ld_c"), 16)
            sp.dma_start(gain[:, :], A["gains"]).then_inc(S("ld_g"), 16)

            def stream(seg, src, cols=D):
                n = dict(segs)[seg]
                s0 = start[seg]

                def load(j, k):
                    sp.dma_start(ring[:, k * D:k * D + cols], src(j)).then_inc(S(f"full{k}"), 16)

                for j in range(min(4, n)):
                    free(sp, s0 + j)
                    load(j, (s0 + j) % 4)
                if n > 4:
                    with sp.Fori(1, n // 4) as i:
                        for k in range(4):
                            last = k | 1 if seg == "xv" else k
                            if seg in ("mk", "mv"):
                                sp.wait_ge(S(seg + "_used"), i * 4 + (k - 3))
                            else:
                                sp.wait_ge(S("tile"), i * 4 + (tiles_before[seg] + last - 3))
                            load(i * 4 + k, k)

            def tiles_of(w):
                return lambda j: w[bass.ds(j, 1)].rearrange("a p n -> (a p) n")

            stream("z", tiles_of(A["w_z"]))
            stream("gate", lambda j: A["w_gate"], KT * 48)
            stream("xk", tiles_of(A["w_xk"]))
            stream("xv", tiles_of(A["w_xv"]))
            stream("glu", tiles_of(A["w_glu"]), 8 * P)
            stream("out", tiles_of(A["w_out"]))
            stream("xq", tiles_of(A["w_xq"]))
            stream("mk", lambda j: A["mem_k"].rearrange("b c p n -> (b c) p n")[bass.ds(j, 1)].rearrange("a p n -> (a p) n"))
            stream("mv", lambda j: A["mem_v"].rearrange("b c p n -> (b c) p n")[bass.ds(j, 1)].rearrange("a p n -> (a p) n"))
            stream("xo", tiles_of(A["w_xo"]))
            stream("pq", tiles_of(A["w_pq"]))

        def act_norm(act, tag, src, sq, t, width, bk=7):
            for k in range(4):
                a, b = k * t // 4, (k + 1) * t // 4
                act.activation(sq[:, a:b, :], src[:, a:b, :], ACT.Square).then_inc(S(tag + "_sq"), 1)
            act.wait_ge(S(tag + "_sum"), 1)
            act.activation(rst[:, 0:src.shape[2]], bank[bk][:, 0:src.shape[2]], ACT.Sqrt, bias=cc("eps"),
                           scale=1.0 / width).then_inc(S(tag + "_rms"), 1)

        def pe_norm(pe, tag, sq, t, bk=7):
            n = sq.shape[2]
            for k in range(t):
                if k % (t // 4) == 0:
                    pe.wait_ge(S(tag + "_sq"), k // (t // 4) + 1)
                last = pe.matmul(bank[bk][:, 0:n], lhsT=cc("ones"), rhs=sq[:, k, :], start=(k == 0), stop=(k == t - 1))
            last.then_inc(S(tag + "_sum"), 1)

        def dve_norm(dve, tag, dst, src, t, g0):
            n = src.shape[2]
            dve.wait_ge(S(tag + "_rms"), 1)
            dve.reciprocal(rst[:, NT:NT + n], rst[:, 0:n]).then_inc(S(tag + "_x"), 1)
            dve.wait_ge(S(tag + "_x"), 1)
            for k in range(t):
                dve.scalar_tensor_tensor(out=dst[:, k, :], in0=src[:, k, :], scalar=gain[:, g0 + k:g0 + k + 1],
                                         in1=rst[:, NT:NT + n], op0=ALU.mult, op1=ALU.mult).then_inc(S(tag + "_x"), 1)

        SQ = Y
        SQM = y_t[:, 0:KT * TP].rearrange("p (t n) -> p t n", n=TP)

        def pe_gemm(pe, seg, src, kts, first=False):
            n, base = dict(segs)[seg], tiles_before[seg]

            def four(i, waits):
                for k in range(4):
                    s, by, v = full[seg, k]
                    pe.wait_ge(S(by), i * 16 + v)
                    if waits:
                        pe.wait_ge(S("evac"), i * 4 + (base + k - 3))
                    for t in range(kts):
                        mm = pe.matmul(bank[k][:, 0:src.shape[2]], lhsT=R[:, s, t, :], rhs=src[:, t, :],
                                       start=(t == 0), stop=(t == kts - 1))
                    mm.then_inc(S("tile"), 1)

            if first:
                four(0, False)
            else:
                pe.wait_ge(S("evac"), base)
            with pe.Fori(1 if first else 0, n // 4) as i:
                four(i, True)

        def copy_gemm(act, seg, dst, func=ACT.Copy):
            n, base = dict(segs)[seg], tiles_before[seg]
            with act.Fori(0, n // 4) as i:
                for k in range(4):
                    act.wait_ge(S("tile"), i * 4 + (base + k + 1))
                    act.activation(dst[:, bass.ds(i * 4 + k, 1), :].rearrange("p a n -> p (a n)"),
                                   bank[k][:, 0:dst.shape[2]], func).then_inc(S("evac"), 1)

        def add_gemm(dve, seg, dst):
            n, base = dict(segs)[seg], tiles_before[seg]
            with dve.Fori(0, n // 4) as i:
                for k in range(4):
                    at_ = dst[:, bass.ds(i * 4 + k, 1), :].rearrange("p a n -> p (a n)")
                    dve.wait_ge(S("tile"), i * 4 + (base + k + 1))
                    dve.tensor_tensor(at_, bank[k][:, 0:NT], at_, ALU.add).then_inc(S("evac"), 1)

        def W(i):
            return x_t[:, i * 256:(i + 1) * 256]

        COS, SIN = (W(0), W(1)), (W(2), W(3))
        ROUND, PROD, FRAC, ABS = W(4), W(5), W(6), W(7)
        M1, M2, M3, M4, GR, GI, N1 = (W(8 + i) for i in range(7))
        HR, HI = (W(15), W(16)), (W(17), W(18))

        def pr(i):
            return prm[:, i * ST:(i + 1) * ST]

        BRAW = mk_t[:, 0:D].rearrange("p (c j n) -> p c j n", c=2, n=32)
        BBAR = mk_t[:, D:2 * D].rearrange("p (c j n) -> p c j n", c=2, n=32)
        BT = b_st[:, :].rearrange("p (c t n) -> p c t n", c=2, n=P)
        CT = c_st[:, :].rearrange("p (c j n) -> p c j n", c=2, n=32)
        H0 = s5s[:, 0:2 * ST * TS].rearrange("p (c j b) -> p c j b", c=2, b=TS)
        BU = s5s[:, 2 * ST * TS:4 * ST * TS].rearrange("p (c j b) -> p c j b", c=2, b=TS)
        HS = s5s[:, 4 * ST * TS:6 * ST * TS].rearrange("p (c j b) -> p c j b", c=2, b=TS)
        TMP = s5s[:, 6 * ST * TS:8 * ST * TS].rearrange("p (c j b) -> p c j b", c=2, b=TS)

        def dve_s5_parameters(dve):
            lr, li = par[:, 0:ST], par[:, ST:2 * ST]
            do = Counted(dve, S("par_dve"))
            dve.wait_ge(S("ld_s5"), 16 * 4)
            dve.wait_ge(S("par_act"), 1)
            do(dve.tensor_tensor(pr(1), lr, pr(0), ALU.mult))
            do(dve.tensor_tensor(pr(2), li, pr(0), ALU.mult))
            do.wait()
            do(dve.tensor_scalar(pr(4), pr(2), 1 / (2 * np.pi), MAGIC, ALU.mult, ALU.add))
            do.wait()
            do(dve.tensor_scalar(pr(4), pr(4), MAGIC, None, ALU.subtract))
            do.wait()
            do(dve.scalar_tensor_tensor(out=pr(5), in0=pr(2), scalar=1 / (2 * np.pi), in1=pr(4),
                                        op0=ALU.mult, op1=ALU.subtract))
            dve.wait_ge(S("par_act"), 5)
            do(dve.tensor_tensor(pr(9), pr(3), pr(8), ALU.mult))
            do(dve.tensor_tensor(pr(10), pr(3), pr(7), ALU.mult))
            do(dve.tensor_tensor(pr(14), lr, lr, ALU.mult))
            do(dve.tensor_tensor(pr(15), li, li, ALU.mult))
            do.wait()
            do(dve.tensor_scalar(pr(11), pr(9), 1.0, None, ALU.subtract))
            do(dve.tensor_tensor(pr(14), pr(14), pr(15), ALU.add))
            do.wait()
            do(dve.reciprocal(pr(15), pr(14)))
            do(dve.tensor_tensor(pr(12), pr(11), lr, ALU.mult))
            do(dve.tensor_tensor(pr(13), pr(10), li, ALU.mult))
            do(dve.tensor_tensor(pr(18), pr(10), lr, ALU.mult))
            do(dve.tensor_tensor(pr(19), pr(11), li, ALU.mult))
            do.wait()
            do(dve.tensor_tensor(pr(12), pr(12), pr(13), ALU.add))
            do(dve.tensor_tensor(pr(18), pr(18), pr(19), ALU.subtract))
            do.wait()
            do(dve.tensor_tensor(pr(16), pr(12), pr(15), ALU.mult))
            do(dve.tensor_tensor(pr(17), pr(18), pr(15), ALU.mult))
            do(dve.tensor_scalar(c_st[:, 1024:2048], c_st[:, 1024:2048], -1.0, None, ALU.mult))
            do.wait()
            fr = pr(16).unsqueeze(2).to_broadcast([P, ST, 32])
            fi = pr(17).unsqueeze(2).to_broadcast([P, ST, 32])
            t1 = y_t[:, 0:1024].rearrange("p (j n) -> p j n", n=32)
            t2 = y_t[:, 1024:2048].rearrange("p (j n) -> p j n", n=32)
            for part, (f1, f2, op) in enumerate(((fr, fi, ALU.subtract), (fi, fr, ALU.add))):
                if part:
                    do.wait()
                do(dve.tensor_tensor(t1, BRAW[:, 0], f1, ALU.mult))
                do(dve.tensor_tensor(t2, BRAW[:, 1], f2, ALU.mult))
                do.wait()
                do(dve.tensor_tensor(BBAR[:, part], t1, t2, op))
            return do.n

        def act_s5_parameters(act):
            act.wait_ge(S("ld_s5"), 16 * 4)
            act.activation(pr(0), par[:, 2 * ST:3 * ST], ACT.Exp).then_inc(S("par_act"), 1)
            act.wait_ge(S("par_dve"), 1)
            act.activation(pr(3), pr(1), ACT.Exp).then_inc(S("par_act"), 1)
            act.wait_ge(S("par_dve"), 5)
            act.activation(pr(6), pr(5), ACT.Abs).then_inc(S("par_act"), 1)
            act.activation(pr(7), pr(5), ACT.Sin, scale=TWO_PI).then_inc(S("par_act"), 1)
            act.wait_ge(S("par_act"), 3)
            act.activation(pr(8), pr(6), ACT.Sin, scale=-TWO_PI, bias=cc("half_pi")).then_inc(S("par_act"), 1)

        PAR_DONE = 27

        def pe_b_transposes(pe):
            pe.wait_ge(S("par_dve"), PAR_DONE)
            for n in range(16):
                b = bank[4 + n // 4]
                tr = pe.transpose(b[:, (n % 4) * P:(n % 4 + 1) * P],
                                  mk_t[:, D + n * P:D + (n + 1) * P], ident)
                if n % 4 == 3:
                    tr.then_inc(S("b_turned"), 1)

        def act_b_transposes(act):
            for n in range(4):
                act.wait_ge(S("b_turned"), n + 1)
                act.activation(b_st[:, n * 512:(n + 1) * 512], bank[4 + n][:, :], ACT.Copy).then_inc(S("b_kept"), 1)

        DV, PO, AC = 13, 9, 3
        BANKS_READ, WR, GR_AT, ROT, HR_AT = 6, 8, 10, 12, 13

        def pool_s5_table(pool, j):
            f = pr(5)[:, j:j + 1]
            base = j * PO
            if j >= 1:
                pool.wait_ge(S("s5_act"), AC * j)
                pool.wait_ge(S("s5_tab"), 4 * j)
            pool.tensor_scalar(ROUND, cc("t"), f, MAGIC, ALU.mult, ALU.add).then_inc(S("s5_tab"), 1)
            pool.tensor_scalar(PROD, cc("t"), f, None, ALU.mult).then_inc(S("s5_tab"), 1)
            pool.wait_ge(S("s5_tab"), 4 * j + 2)
            pool.tensor_scalar(ROUND, ROUND, MAGIC, None, ALU.subtract).then_inc(S("s5_tab"), 1)
            pool.wait_ge(S("s5_tab"), 4 * j + 3)
            pool.tensor_tensor(FRAC, PROD, ROUND, ALU.subtract).then_inc(S("s5_tab"), 1)

        def act_s5_table(act, j):
            act.wait_ge(S("s5_tab"), 4 * j + 4)
            if j >= 2:
                act.wait_ge(S("s5_dve"), DV * (j - 2) + ROT)
                act.wait_ge(S("s5_im"), 5 * (j - 2) + 2)
            if j >= 1:
                act.wait_ge(S("s5_act"), AC * j)
            act.activation(ABS, FRAC, ACT.Abs).then_inc(S("s5_act"), 1)
            act.activation(SIN[j % 2], FRAC, ACT.Sin, scale=TWO_PI).then_inc(S("s5_act"), 1)
            act.wait_ge(S("s5_act"), AC * j + 1)
            act.activation(COS[j % 2], ABS, ACT.Sin, scale=-TWO_PI, bias=cc("half_pi")).then_inc(S("s5_act"), 1)

        def pe_s5_input(pe, j):
            jj, q = j % 4, j // 4
            if j >= 1:
                pe.wait_ge(S("s5_dve"), DV * (j - 1) + BANKS_READ)
            for part in range(2):
                mm = pe.matmul(bank[4 + part][:, 0:NT], lhsT=BT[32 * jj:32 * jj + 32, part, q, :],
                               rhs=Z[32 * jj:32 * jj + 32, U0 + q, :], start=True, stop=True, tile_position=(32 * jj, 0))
            mm.then_inc(S("s5_bu"), 1)

        def dve_s5(dve, j):
            do = Counted(dve, S("s5_dve"), DV * j)
            c, s = COS[j % 2], SIN[j % 2]
            br, bi = bank[4][:, 0:TP], bank[5][:, 0:TP]
            dve.wait_ge(S("s5_bu"), j + 1)
            dve.wait_ge(S("s5_act"), AC * (j + 1))
            if j >= 1:
                do.wait(0)
            do(dve.tensor_tensor(M1, c, br, ALU.mult))
            do(dve.tensor_tensor(M2, s, bi, ALU.mult))
            do(dve.tensor_tensor(M3, c, bi, ALU.mult))
            do(dve.tensor_tensor(M4, s, br, ALU.mult))
            do(dve.tensor_copy(BU[:, 0, j, :], bank[4][:, TP:NT]))
            do(dve.tensor_copy(BU[:, 1, j, :], bank[5][:, TP:NT]))
            do.wait(4)
            do(dve.tensor_tensor(M1, M1, M2, ALU.add))
            do(dve.tensor_tensor(M3, M3, M4, ALU.subtract))
            if j >= 1:
                dve.wait_ge(S("s5_im"), 5 * (j - 1) + 2)
            do.wait(7)
            r = pr(3)[:, j:j + 1].to_broadcast([P, TP])
            do(dve.tensor_tensor_scan(GR, r, M1, 0.0, ALU.mult, ALU.add))
            do.wait(8)
            do(dve.tensor_tensor_scan(GI, r, M3, 0.0, ALU.mult, ALU.add))
            do.wait(9)
            do(dve.tensor_tensor(M2, c, GR, ALU.mult))
            do.wait(10)
            do(dve.tensor_tensor(M4, s, GI, ALU.mult))
            if j >= 2:
                dve.wait_ge(S("s5_c"), j - 1)
                dve.wait_ge(S("s5_im"), 5 * (j - 2) + 5)
            do.wait(12)
            do(dve.tensor_tensor(HR[j % 2], M2, M4, ALU.subtract))

        def pool_s5(pool, j):
            do = Counted(pool, S("s5_im"), 5 * j)
            c, s = COS[j % 2], SIN[j % 2]
            pool.wait_ge(S("s5_dve"), DV * j + GR_AT)
            if j >= 1:
                do.wait(0)
            if j >= 2:
                pool.wait_ge(S("s5_c"), j - 1)
            do(pool.tensor_tensor(N1, s, GR, ALU.mult))
            do(pool.tensor_tensor(HI[j % 2], c, GI, ALU.mult))
            do.wait()
            do(pool.tensor_tensor(HI[j % 2], N1, HI[j % 2], ALU.add))
            do.wait()
            do(pool.tensor_copy(s5p[:, ST + j:ST + j + 1], HI[j % 2][:, TP - 1:TP]))
            pool.wait_ge(S("s5_dve"), DV * j + HR_AT)
            do(pool.tensor_copy(s5p[:, j:j + 1], HR[j % 2][:, TP - 1:TP]))

        def pe_s5_output(pe, j):
            jj, q = j % 4, j // 4
            pe.wait_ge(S("s5_dve"), DV * j + HR_AT)
            pe.wait_ge(S("s5_im"), 5 * j + 3)
            if jj == 0 and q >= 1:
                pe.wait_ge(S("s5_y"), q)
            for part, h in enumerate((HR, HI)):
                mm = pe.matmul(bank[6][32 * jj:32 * jj + 32, 0:TP], lhsT=CT[:, part, j, :], rhs=h[j % 2],
                               start=(part == 0), stop=(part == 1), tile_position=(0, 32 * jj))
            mm.then_inc(S("s5_c"), 1)

        def dve_s5_skip(dve, q):
            dve.wait_ge(S("s5_c"), 4 * q + 4)
            dve.scalar_tensor_tensor(out=Y[:, 8 + q, 0:TP], in0=Z[:, U0 + q, 0:TP],
                                     scalar=gain[:, D_SKIP + q:D_SKIP + q + 1], in1=bank[6][:, 0:TP],
                                     op0=ALU.mult, op1=ALU.add).then_inc(S("s5_y"), 1)

        def dve_s5_samples(dve):
            do = Counted(dve, S("s5_smp"))
            ar = pr(9).unsqueeze(2).to_broadcast([P, ST, TS])
            ai = pr(10).unsqueeze(2).to_broadcast([P, ST, TS])
            dve.wait_ge(S("s5_dve"), DV * ST)
            for part, (x, y, op) in enumerate(((ar, ai, ALU.subtract), (ai, ar, ALU.add))):
                if part:
                    do.wait()
                do(dve.tensor_tensor(TMP[:, 0], H0[:, 0], x, ALU.mult))
                do(dve.tensor_tensor(TMP[:, 1], H0[:, 1], y, ALU.mult))
                do.wait()
                do(dve.tensor_tensor(HS[:, part], TMP[:, 0], TMP[:, 1], op))
                do.wait()
                do(dve.tensor_tensor(HS[:, part], HS[:, part], BU[:, part], ALU.add))
            ds = gain[:, D_SKIP:D_SKIP + 8].unsqueeze(2).to_broadcast([P, 8, TS])
            do(dve.tensor_tensor(Y[:, 8:16, TP:NT], Z[:, U0:NZ, TP:NT], ds, ALU.mult))
            do.wait()
            dve.wait_ge(S("s5_cs"), 1)
            do(dve.tensor_tensor(Y[:, 8:16, TP:NT], Y[:, 8:16, TP:NT],
                                 bank[6][:, 0:8 * TS].rearrange("p (q b) -> p q b", b=TS), ALU.add))

        def pe_s5_samples(pe):
            pe.wait_ge(S("s5_y"), 8)
            pe.wait_ge(S("s5_smp"), 8)
            for j in range(ST):
                jj, q = j % 4, j // 4
                for part in range(2):
                    mm = pe.matmul(bank[6][32 * jj:32 * jj + 32, q * TS:(q + 1) * TS], lhsT=CT[:, part, j, :],
                                   rhs=HS[:, part, j, :], start=(part == 0), stop=(part == 1),
                                   tile_position=(0, 32 * jj))
            mm.then_inc(S("s5_cs"), 1)

        def pe_mem_tile(pe, n):
            base = tiles_before["xk"]
            pe.wait_ge(S("evac"), base + n - 3)
            if n < 16:
                s = arrived(pe, "xk", n)
                for t in range(KT):
                    mm = pe.matmul(bank[n % 4][:, 0:TP], lhsT=R[:, s, t, :], rhs=M[:, t, :],
                                   start=(t == 0), stop=(t == KT - 1))
            else:
                pair, b = (n - 16) // 2, n % 2
                s = arrived(pe, "xv", 2 * pair)
                arrived(pe, "xv", 2 * pair + 1)
                for t in range(KT):
                    mm = pe.matmul(bank[n % 4][:, 0:TP], lhsT=M[:, t, b * P:(b + 1) * P], rhs=R[:, s:s + 2, t, :],
                                   start=(t == 0), stop=(t == KT - 1))
            mm.then_inc(S("tile"), 1)

        def act_mem_tile(act, n):
            act.wait_ge(S("tile"), tiles_before["xk"] + n + 1)
            dst = MK[:, n, :] if n < 16 else MV[:, n % 2, (n - 16) // 2 * TP:((n - 16) // 2 + 1) * TP]
            act.activation(dst, bank[n % 4][:, 0:TP], ACT.Copy).then_inc(S("evac"), 1)

        def pe_front(pe):
            pe.wait_ge(S("ld_c"), 16)
            pe_norm(pe, "mix", SQ, KT)
            pe.wait_ge(S("mix_x"), KT + 1)
            pe_gemm(pe, "z", X, KT, first=True)
            pe.wait_ge(S("evac"), NZ - 3)
            s = arrived(pe, "gate", 0)
            for t in range(KT):
                mm = pe.matmul(bank[0][0:48, 0:NT], lhsT=ring[:, s * D + t * 48:s * D + (t + 1) * 48], rhs=X[:, t, :],
                               start=(t == 0), stop=(t == KT - 1))
            mm.then_inc(S("tile"), 1)
            pe_b_transposes(pe)
            pe.wait_ge(S("b_kept"), 4)
            pe_norm(pe, "mem", SQM, KT)
            pe.wait_ge(S("mem_x"), KT + 1)
            for j in range(ST):
                pe_s5_input(pe, j)
                pe_mem_tile(pe, j)
                if j >= 1:
                    pe_s5_output(pe, j - 1)
            pe_s5_output(pe, ST - 1)
            pe_s5_samples(pe)
            pe.wait_ge(S("y_gelu"), 1)
            pe_gemm(pe, "glu", Y[:, 8:16, :], 8)

        def act_front(act):
            act.wait_ge(S("ld_x"), 16)
            act.wait_ge(S("ld_c"), 16)
            act_norm(act, "mix", H, SQ, KT, D)
            act_s5_parameters(act)
            copy_gemm(act, "z", Z)
            act.wait_ge(S("tile"), NZ + 1)
            act.activation(gate[0:48, :], bank[0][0:48, 0:NT], ACT.Sigmoid).then_inc(S("evac"), 1)
            act_b_transposes(act)
            act.wait_ge(S("par_dve"), PAR_DONE)
            act.wait_ge(S("ld_m"), 16)
            act_norm(act, "mem", M, SQM, KT, D)
            for j in range(ST):
                act_s5_table(act, j)
                if j >= 1:
                    act_mem_tile(act, j - 1)
            act_mem_tile(act, ST - 1)
            act.wait_ge(S("s5_y"), 8)
            act.wait_ge(S("s5_smp"), 10)
            act.activation(Y[:, 8:16, :], Y[:, 8:16, :], ACT.Gelu_apprx_tanh).then_inc(S("y_gelu"), 1)
            copy_gemm(act, "glu", X, ACT.Sigmoid)

        def dve_front(dve):
            dve.wait_ge(S("ld_g"), 16)
            dve_norm(dve, "mix", X, H, KT, G_MIX)
            assert dve_s5_parameters(dve) == PAR_DONE
            dve_norm(dve, "mem", M, M, KT, G_MEM)
            dve.wait_ge(S("tile"), NZ + 1)
            for j in range(ST):
                dve_s5(dve, j)
                if j >= 5 and j % 4 == 1:
                    dve_s5_skip(dve, j // 4 - 1)
            dve_s5_skip(dve, 7)
            dve_s5_samples(dve)
            dve.wait_ge(S("evac"), tiles_before["glu"] + 8)
            dve.tensor_tensor(Y[:, 8:16, :], Y[:, 8:16, :], X[:, 0:8, :], ALU.mult).then_inc(S("o_ssm"), 1)

        def pool_front(pool):
            pool.dma_start(par[:, :], A["s5_par"].rearrange("p c j -> p (c j)")).then_inc(S("ld_s5"), 16)
            pool.dma_start(mk_t[:, 0:D], A["s5_b"].rearrange("p c n -> p (c n)")).then_inc(S("ld_s5"), 16)
            pool.dma_start(c_st[:, :], A["s5_c"].rearrange("p c n -> p (c n)")).then_inc(S("ld_s5"), 16)
            pool.dma_start(s5s[:, 0:2 * ST * TS], A["s5_h0"].rearrange("p c n -> p (c n)")).then_inc(S("ld_s5"), 16)
            pool.dma_start(m_t[:, :], A["mem_t"].rearrange("p t n -> p (t n)")).then_inc(S("ld_m"), 16)
            pool.dma_start(wcmp[:, :], A["w_cmp"].rearrange("p a b c -> p (a b c)")).then_inc(S("ld_w"), 16)
            pool.dma_start(idx_i[:, :], A["page"].partition_broadcast(P)).then_inc(S("ld_w"), 16)
            for name, src in (("new_k", "buf_k"), ("new_v", "buf_v")):
                pool.dma_start(A[name][:, 0:256 * 256], A[src]).then_inc(S("stored"), 16)
            pool.wait_ge(S("par_dve"), 5)
            pool.wait_ge(S("ld_c"), 16)
            pool.wait_ge(S("tile"), NZ + 1)
            for n in range(ST + 1):
                if n < ST:
                    pool_s5_table(pool, n)
                if n == 1:
                    pool.dma_start(A["z_kv"].rearrange("t p n -> p t n"), Z[:, K_CMP:U0, :]).then_inc(S("z_stored"), 16)
                if n >= 1:
                    pool_s5(pool, n - 1)
            pool.wait_ge(S("s5_im"), 5 * ST)
            pool.dma_start(A["s5_p"], s5p[:, :]).then_inc(S("stored"), 16)
            pool.wait_ge(S("s5_smp"), 8)
            pool.dma_start(A["s5_s"], s5s[:, 4 * ST * TS:6 * ST * TS]).then_inc(S("stored"), 16)
            pool.wait_ge(S("evac"), tiles_before["glu"])
            pool.dma_start(A["m_k"].rearrange("t p n -> p t n"), MK).then_inc(S("m_stored"), 16)
            pool.dma_start(A["m_v"].rearrange("b p n -> p b n"), MV).then_inc(S("m_stored"), 16)

        VN = c_st[:, 0:1024].rearrange("p (b n) -> p b n", b=QB)
        CVN = c_st[0:NC, 1024:1280]
        CK = c_st[:, 1280:1280 + 4 * NC].rearrange("p (t n) -> p t n", n=NC)
        HALVES = c_st[:, 1344:1472]
        CKZ = c_st[:, 1472:1536].rearrange("p (h e n) -> p h e n", h=2, e=2)
        CVZ = x_t[:, 0:1024].rearrange("p (h g e d) -> p h g e d", h=2, g=GQ, e=2)
        CW = [x_t[:, 1056 + b * 256:1312 + b * 256] for b in range(QB)]
        CPT = [x_t[:, 1568 + b * 256:1824 + b * 256] for b in range(QB)]
        WC = wcmp[:, :].rearrange("p (a b j) -> p a b j", a=2, b=2)

        def dve_compress(do, src, dst):
            prod = b_st[:, :].rearrange("p (t g c j) -> p t g c j", t=8, g=2, j=STRIDE)
            for t in range(4):
                for half in range(2):
                    w = WC[:, t // 2, t % 2, half * STRIDE:(half + 1) * STRIDE]
                    do(do.eng.tensor_tensor(prod[:, 2 * t + half], src(t // 2, t % 2),
                                            w.unsqueeze(1).unsqueeze(1).to_broadcast([P, 2, 8, STRIDE]), ALU.mult))
            do.wait()
            do(do.eng.tensor_reduce(HALVES, b_st[:, :].rearrange("p (n j) -> p n j", j=STRIDE), AXX, ALU.add))
            do.wait()
            hv = HALVES.rearrange("p (t h c) -> p t h c", t=4, h=2)
            return do(do.eng.tensor_tensor(dst, hv[:, :, 0, 0:NC], hv[:, :, 1, 1:NC + 1], ALU.add))

        COMPRESSED = 10

        NEW = x_t[0:TS, 2832:3600]
        GATE_S = gn[:, 192:195]

        def pe_by_token(pe):
            for b in range(QB):
                for n, t in enumerate((V_SEL, V_SEL + 1, V_WIN, V_WIN + 1)):
                    tr = pe.transpose(bank[4 + b][:, n * P:(n + 1) * P], Z[:, t, b * P:(b + 1) * P], ident)
                tr.then_inc(S("bt_pe"), 1)
            for b in range(QB):
                pe.transpose(bank[6][:, b * 48:(b + 1) * 48], gate[0:48, b * P:(b + 1) * P], ident[0:48, 0:48])
            pe.transpose(bank[6][0:TS, 96:144], gate[0:48, TP:NT], ident[0:48, 0:48]).then_inc(S("bt_pe"), 1)
            pe.wait_ge(S("evac"), tiles_before["out"])
            for n, t in enumerate((K_WIN, K_WIN + 1, V_SEL, V_SEL + 1, V_WIN, V_WIN + 1)):
                tr = pe.transpose(bank[n // 4][0:TS, n % 4 * P:(n % 4 + 1) * P], Z[:, t, TP:NT], ident)
            tr.then_inc(S("bt_pe"), 1)
            pe_norm(pe, "ssm", X[:, 0:8, :], 8, bk=3)
            pe.wait_ge(S("cmp_p"), COMPRESSED)
            for hp in range(2):
                tr = pe.transpose(bank[7][0:NC, hp * P:(hp + 1) * P], CK[:, 2 + hp, :], ident)
            tr.then_inc(S("bt_pe"), 1)
            pe.wait_ge(S("bt_act"), 4)
            pe.matmul(bank[6][:, 144:192], lhsT=cc("sel", rows=TS), rhs=gn[0:TS, 96:144], start=True, stop=True)\
                .then_inc(S("bt_pe"), 1)
            pe.wait_ge(S("bt_act"), 7)
            pe.wait_ge(S("gate_s"), 1)
            pe.matmul(bank[7][:, 0:256], lhsT=cc("selk", rows=NC), rhs=CVN, start=True, stop=True).then_inc(S("bt_pe"), 1)
            pe.wait_ge(S("ckz"), 5)
            for qb in range(QB):
                for t in range(8):
                    mm = pe.matmul(bank[5 + qb][:, t * 32:(t + 1) * 32], lhsT=Z[:, t, qb * P:(qb + 1) * P],
                                   rhs=CKZ[:, t // 4].rearrange("p e n -> p (e n)"), start=True, stop=True)
                mm.then_inc(S("c_s"), 1)

        def act_by_token(act):
            act.wait_ge(S("s5_cs"), 1)
            for b in range(QB):
                act.wait_ge(S("bt_pe"), b + 1)
                act.activation(VN[:, b, :], bank[4 + b][:, :], ACT.Copy).then_inc(S("bt_act"), 1)
            act.wait_ge(S("bt_pe"), 3)
            act.activation(gn[:, 0:96], bank[6][:, 0:96], ACT.Copy).then_inc(S("bt_act"), 1)
            act.activation(gn[0:TS, 96:144], bank[6][0:TS, 96:144], ACT.Copy).then_inc(S("bt_act"), 1)
            act.wait_ge(S("bt_pe"), 4)
            act.wait_ge(S("o_ssm"), 1)
            act.activation(NEW[:, 0:512], bank[0][0:TS, :], ACT.Copy).then_inc(S("bt_act"), 1)
            act.activation(NEW[:, 512:768], bank[1][0:TS, 0:256], ACT.Copy).then_inc(S("bt_act"), 1)
            act_norm(act, "ssm", Y[:, 8:16, :], X[:, 0:8, :], 8, 1024, bk=3)
            act.wait_ge(S("bt_pe"), 5)
            act.activation(CVN, bank[7][0:NC, 0:256], ACT.Copy).then_inc(S("bt_act"), 1)
            for qb in range(QB):
                act.wait_ge(S("c_d"), 9 * qb + 3)
                act.activation(CW[qb], CW[qb], ACT.Exp, scale=SCALE).then_inc(S("c_e"), 1)

        def dve_by_token(dve):
            dve.wait_ge(S("s5_cs"), 1)
            dve.wait_ge(S("ld_w"), 32)
            do = Counted(dve, S("cmp_p"))
            dve_compress(do, lambda kv, hp: Z[:, K_CMP + 2 * kv + hp, 0:TP].rearrange("p (g c j) -> p g c j", g=2, j=STRIDE), CK)
            dve.memset(c_st[:, 1472:1536], 0.0).then_inc(S("ckz"), 1)
            do.wait()
            dve.wait_ge(S("ckz"), 1)
            for hp in range(2):
                for hh in range(2):
                    r = slice(64 * hh, 64 * hh + 64)
                    dve.tensor_copy(CKZ[r, hp, hh, 0:NC], CK[r, hp, :]).then_inc(S("ckz"), 1)
            dve_sample_queries(dve)
            dve.wait_ge(S("bt_pe"), 6)
            gs = gn[:, 144:192].rearrange("p (r k) -> p r k", k=16)
            dve.tensor_tensor(gs, bank[6][:, 144:192].rearrange("p (r k) -> p r k", k=16),
                              cc("kmask").unsqueeze(1).to_broadcast([P, 3, 16]), ALU.mult).then_inc(S("gate_s"), 1)
            dve.wait_ge(S("gate_s"), 1)
            dve.tensor_reduce(GATE_S, gs, AXX, ALU.add).then_inc(S("gate_s"), 1)
            dve_norm(dve, "ssm", Y[:, 8:16, :], Y[:, 8:16, :], 8, G_SSM)

        def dve_compressed(dve):
            dve.wait_ge(S("ssm_sum"), 1)
            dve.wait_ge(S("bt_pe"), 7)
            for hp in range(2):
                dve.tensor_tensor(CVZ[:, hp],
                                  bank[7][:, hp * P:(hp + 1) * P].rearrange("p (e d) -> p e d", e=2).unsqueeze(1)
                                  .to_broadcast([P, GQ, 2, HD]),
                                  cc("selT").rearrange("p (g e) -> p g e", e=2).unsqueeze(3).to_broadcast([P, GQ, 2, HD]),
                                  ALU.mult).then_inc(S("cvz"), 1)
            do = Counted(dve, S("c_d"))
            for qb in range(QB):
                cm, cr = (small[:, 96 + 32 * qb + 16 * k:112 + 32 * qb + 16 * k] for k in range(2))
                w = CW[qb].rearrange("p (k n) -> p k n", n=16)
                dve.wait_ge(S("c_s"), qb + 1)
                do(dve.tensor_tensor(CW[qb], bank[5 + qb][:, 0:256], cc("cb", qb * TP, TP), ALU.add))
                do.wait()
                do(dve.tensor_reduce(cm, w, AXX, ALU.max))
                do.wait()
                do(dve.tensor_tensor(w, w, cm.unsqueeze(2).to_broadcast([P, HEADS, 16]), ALU.subtract))
                dve.wait_ge(S("c_e"), qb + 1)
                do(dve.tensor_tensor(w, w, cc("mc", qb * 16, 16).unsqueeze(1).to_broadcast([P, HEADS, 16]), ALU.mult))
                do.wait()
                do(dve.tensor_reduce(cr, w, AXX, ALU.add))
                do.wait()
                do(dve.tensor_scalar(cr, cr, TINY, None, ALU.max))
                do.wait()
                do(dve.reciprocal(cm, cr))
                do.wait()
                gate_c = gn[:, qb * 48:qb * 48 + 16].rearrange("p (h e g) -> p h g e", h=2, e=2)
                do(dve.tensor_tensor(cr.rearrange("p (h g e) -> p h g e", h=2, g=GQ),
                                     cm.rearrange("p (h g e) -> p h g e", h=2, g=GQ), gate_c, ALU.mult))
                do.wait()
                do(dve.tensor_tensor(w, w, cr.unsqueeze(2).to_broadcast([P, HEADS, 16]), ALU.mult))

        def pe_compressed(pe):
            for qb in range(QB):
                pe.wait_ge(S("c_d"), 9 * (qb + 1))
                for hp in range(2):
                    tr = pe.transpose(bank[3 + qb][:, hp * P:(hp + 1) * P], CW[qb][:, hp * P:(hp + 1) * P], ident)
                tr.then_inc(S("c_t"), 1)

        def act_compressed(act):
            for qb in range(QB):
                act.wait_ge(S("c_t"), qb + 1)
                act.activation(CPT[qb], bank[3 + qb][:, 0:256], ACT.Copy).then_inc(S("c_pt"), 1)

        UNITS = QB * HEADS
        SC = [m_t[:, b * 512:(b + 1) * 512] for b in range(3)]
        PT = [m_t[:, 1536 + b * 512:1536 + (b + 1) * 512] for b in range(3)]

        def st(b, k, n=3):
            return small[:, b * 15 + 3 * k:b * 15 + 3 * k + n]

        def unit(u):
            qb, hp, g, hh = u // 16, u // 8 % 2, u // 2 % 4, u % 2
            return qb, hp, g, hh, P * (qb + 1), 4 * (2 * hp + hh) + g

        def pe_scores(pe, u):
            qb, hp, g, hh, nk, _ = unit(u)
            r = slice(64 * hh, 64 * hh + 64)
            if u >= 2:
                pe.wait_ge(S("att_m"), 3 * (u - 2) + 1)
            q = Z[r, 4 * hp + g, qb * P:(qb + 1) * P]
            pe.matmul(bank[u % 2][:, 0:nk], lhsT=q, rhs=Z[r, K_SEL + hp, 0:nk], start=True, stop=True)
            pe.matmul(bank[u % 2][:, 256:256 + nk], lhsT=q, rhs=Z[r, K_WIN + hp, 0:nk], start=True, stop=True)\
                .then_inc(S("att_s"), 1)

        def dve_unit(dve, u):
            new, old = u < UNITS, u >= 1
            m, w = Counted(dve, S("att_m"), 3 * u), Counted(dve, S("att_w"), 4 * (u - 1))
            if new:
                qb, hp, g, hh, nk, head = unit(u)
                b, bk = u % 3, u % 2
                sc = SC[b][:, 0:2 * nk].rearrange("p (r n) -> p r n", r=2)
                dve.wait_ge(S("att_s"), u + 1)
                if u >= 3:
                    dve.wait_ge(S("att_t"), u - 2)
                m(dve.scalar_tensor_tensor(
                    out=sc, in0=cc(f"d{qb}").unsqueeze(1).to_broadcast([P, 2, nk]), scalar=SLOPE[head] / SCALE,
                    in1=bank[bk][:, :].rearrange("p (r n) -> p r n", r=2)[:, :, 0:nk], op0=ALU.mult, op1=ALU.add))
            if old:
                oqb, _, _, _, onk, ohead = unit(u - 1)
                ob = (u - 1) % 3
                dve.wait_ge(S("att_e"), 2 * u)
                w(dve.tensor_scalar(st(ob, 3, 2), st(ob, 2, 2), TINY, None, ALU.max))
            if new:
                m.wait()
                m(dve.tensor_reduce(st(b, 0, 2), sc, AXX, ALU.max))
            if old:
                w.wait()
                w(dve.reciprocal(st(ob, 4, 2), st(ob, 3, 2)))
            if new:
                m.wait()
                m(dve.tensor_scalar(st(b, 1, 2), st(b, 0, 2), -SCALE, None, ALU.mult))
            if old:
                w.wait()
                gv = gn[:, oqb * 48:(oqb + 1) * 48].rearrange("p (r k) -> p r k", k=16)
                for r in range(2):
                    where = SC[ob][:, r * onk:(r + 1) * onk]
                    w(dve.tensor_scalar(where, where, st(ob, 4, 2)[:, r:r + 1], gv[:, r + 1, ohead:ohead + 1],
                                        ALU.mult, ALU.mult))

        def act_exp(act, u):
            nk, b = unit(u)[4], u % 3
            act.wait_ge(S("att_m"), 3 * (u + 1))
            for r in range(2):
                act.activation(SC[b][:, r * nk:(r + 1) * nk], SC[b][:, r * nk:(r + 1) * nk], ACT.Exp, scale=SCALE,
                               bias=st(b, 1)[:, r:r + 1], accum_out=st(b, 2)[:, r:r + 1]).then_inc(S("att_e"), 1)

        def pe_turn(pe, u):
            nk, b = unit(u)[4], u % 3
            pe.wait_ge(S("att_w"), 4 * (u + 1))
            if u >= 2:
                pe.wait_ge(S("att_pt"), u - 1)
            else:
                pe.wait_ge(S("c_pt"), u + 1)
            for n in range(2 * nk // P):
                tr = pe.transpose(bank[3 + u % 2][:, n * P:(n + 1) * P], SC[b][:, n * P:(n + 1) * P], ident)
            tr.then_inc(S("att_t"), 1)

        def act_keep(act, u):
            nk, b = unit(u)[4], u % 3
            act.wait_ge(S("att_t"), u + 1)
            if u >= 3:
                act.wait_ge(S("att_pv"), u - 2)
            act.activation(PT[b][:, 0:2 * nk], bank[3 + u % 2][:, 0:2 * nk], ACT.Copy).then_inc(S("att_pt"), 1)

        def pe_values(pe, u):
            qb, hp, g, hh, nk, _ = unit(u)
            b, pair = u % 3, u // 2
            kv = (2 * hp + hh) * HD
            pe.wait_ge(S("att_pt"), u + 1)
            if u == 0:
                pe.wait_ge(S("cvz"), 2)
                pe.wait_ge(S("c_pt"), 2)
            if pair >= 2:
                pe.wait_ge(S("att_o"), pair - 1)
            out = bank[5 + pair % 2][64 * hh:64 * hh + 64, 0:P]
            n = nk // P
            pe.matmul(out, lhsT=CVZ[:, hp, g, hh, :], rhs=CPT[qb][:, hp * P:(hp + 1) * P], start=True, stop=False,
                      tile_position=(0, 64 * hh))
            for r in range(2):
                for k in range(n):
                    mm = pe.matmul(out, lhsT=VN[:, k, r * 256 + kv:r * 256 + kv + HD],
                                   rhs=PT[b][:, (r * n + k) * P:(r * n + k + 1) * P], start=False,
                                   stop=(r == 1 and k == n - 1), tile_position=(0, 64 * hh))
            mm.then_inc(S("att_pv"), 1)

        def act_attended(act, pair):
            qb, hp, g = unit(2 * pair)[:3]
            act.wait_ge(S("att_pv"), 2 * (pair + 1))
            act.activation(Y[:, 4 * hp + g, qb * P:(qb + 1) * P], bank[5 + pair % 2][:, 0:P], ACT.Copy)\
                .then_inc(S("att_o"), 1)

        SS = x_t[:, 0:2 * (PAST + 1) + 16]
        PZ = x_t[:, 544:1568].rearrange("p (m b n) -> p m b n", m=4, b=4)
        PZC = x_t[0:NC, 1568:1824].rearrange("p (b n) -> p b n", b=4)
        PTN = x_t[0:TS, 1824:2080]
        PN = x_t[:, 2080:2096]
        OX, OY = x_t[:, 2096:2096 + 256], x_t[:, 2352:2480]
        CKS = x_t[:, 2352:2832].rearrange("p (t b n) -> p t b n", t=4, b=TS)
        CVS = b_st[0:NC, :]
        NK = PAST + 1
        QZ = x_t[:, 3600:4112].rearrange("p (b n) -> p b n", n=P)

        def qs(hp, b):
            a = b % 2 * 64 + hp * 32
            return QZ[:, b // 2, a:a + 32]

        def dve_sample_queries(dve):
            dve.memset(x_t[:, 3600:4112], 0.0).then_inc(S("qz"), 1)
            dve.wait_ge(S("qz"), 1)
            for hh in range(2):
                r = slice(64 * hh, 64 * hh + 64)
                for c in range(2):
                    for hp in range(2):
                        a = c * 80 + hp * 40 + hh * 4
                        dve.tensor_copy(QZ[r, :, a:a + 4],
                                        Z[r, 4 * hp:4 * hp + 4, TP + c:NT:2].rearrange("p g b -> p b g")).then_inc(S("qz"), 1)

        def dve_index(dve):
            do = Counted(dve, S("idx"))
            dve.wait_ge(S("ld_w"), 32)
            dve.wait_ge(S("ld_c"), 16)
            do(dve.tensor_copy(small[:, 48:64], idx_i[:, :]))
            do.wait()
            do(dve.tensor_scalar(small[:, 64:80], small[:, 48:64], float(P), cc("pidx"), ALU.mult, ALU.add))
            do.wait()
            do(dve.tensor_copy(idx_i[:, :], small[:, 64:80]))

        def pool_caches(pool):
            pool.wait_ge(S("idx"), 3)
            for b in range(TS):
                free(pool, start["dk"] + b)
                s, by, _ = full["dk", b]
                at_ = lambda o, n=256: ring[:, s * D + o:s * D + o + n]
                for pg in range(2):
                    ix = bass.IndirectOffsetOnAxis(idx_i[:, 2 * b + pg:2 * b + pg + 1], 0)
                    for name, o in (("pool_ks", 0), ("pool_kc", 1024), ("pool_vc", 1536)):
                        pool.indirect_dma_start(at_(o + 256 * pg), None, A[name], ix).then_inc(S(by), 16)
                pool.dma_start(at_(512, 512), A["win_k"][b]).then_inc(S(by), 16)
            for b in range(TS):
                free(pool, start["dv"] + b)
                s, by, _ = full["dv", b]
                at_ = lambda o, n=256: ring[:, s * D + o:s * D + o + n]
                for pg in range(2):
                    ix = bass.IndirectOffsetOnAxis(idx_i[:, 2 * b + pg:2 * b + pg + 1], 0)
                    pool.indirect_dma_start(at_(256 * pg), None, A["pool_vs"], ix).then_inc(S(by), 16)
                pool.dma_start(at_(512, 512), A["win_v"][b]).then_inc(S(by), 16)

        def pool_new_rows(pool):
            pool.wait_ge(S("bt_act"), 6)
            for name, a in (("new_k", 0), ("new_v", 512)):
                pool.dma_start(A[name][:, 256 * 256:257 * 256], NEW[:, a:a + 256]).then_inc(S("new_stored"), 16)

        def dve_sample_compress(dve, b):
            if b == 0:
                dve.wait_ge(S("o_ssm"), 1)
                dve.wait_ge(S("cmp_p"), COMPRESSED)
            do = Counted(dve, S("cmp_s"), COMPRESSED * b)
            s = arrived(dve, "dk", b)
            if b:
                do.wait(0)
            dve_compress(do, lambda kv, hp: ring[:, s * D + 1024 + 512 * kv:s * D + 1536 + 512 * kv].rearrange(
                "p (g h c j) -> p g h c j", g=2, h=2, j=STRIDE)[:, :, hp], CKS[:, :, b, :])

        def pe_sample_scores(pe, b):
            if b == 0:
                pe.wait_ge(S("qz"), 9)
                pe.wait_ge(S("evac"), tiles_before["out"])
                pe.wait_ge(S("cvz"), 2)
            s = arrived(pe, "dk", b)
            rows = slice(32 * (b // 2), 32 * (b // 2) + 32)
            pages = ring[:, s * D:s * D + 1024].rearrange("p (m h n) -> p m h n", m=4, h=2)
            pe.wait_ge(S("cmp_s"), COMPRESSED * (b + 1))
            for hp in range(2):
                first, last = (b % 2 == 0 and hp == 0), (b % 2 == 1 and hp == 1)
                at_ = dict(tile_position=(0, rows.start), skip_group_check=True)
                pe.matmul(bank[2][rows, :], lhsT=qs(hp, b), rhs=pages[:, :, hp, :], start=first, stop=last, **at_)
                pe.matmul(bank[7][rows, 0:NC], lhsT=qs(hp, b), rhs=CKS[:, hp, b, :], start=first, stop=last, **at_)
                mm = pe.matmul(bank[7][rows, 16:18], lhsT=qs(hp, b), rhs=Z[:, K_SEL + hp:K_WIN + hp + 1:4, TP + b],
                               start=False, stop=last, **at_)
            mm.then_inc(S("dk_used"), 1)

        def pe_sample_turn(pe):
            pe.wait_ge(S("att_o"), UNITS // 2)
            for n in range(4):
                for k in range(4):
                    b, hp = (4 * n + k) // 2, k % 2
                    tr = pe.transpose(bank[(0, 1, 5, 6)[n]][0:NC, k * P:(k + 1) * P], CKS[:, 2 + hp, b, :], ident)
            tr.then_inc(S("dec_pe"), 1)
            pe.wait_ge(S("dec_dve"), 15)
            for n in range(4):
                r, k = n // 2, n % 2
                pe.transpose(bank[3][:, n * P:(n + 1) * P], SS[:, r * NK + k * P:r * NK + (k + 1) * P], ident)
            pe.transpose(bank[4][0:NC, 0:P], SS[:, 2 * NK:2 * NK + NC], ident)
            for r in range(2):
                tr = pe.transpose(bank[4][0:TS, P * (r + 1):P * (r + 2)], PN[:, r * TS:(r + 1) * TS], ident)
            tr.then_inc(S("dec_pe"), 1)

        def act_sample_scores(act):
            act.wait_ge(S("dec_pe"), 1)
            act.wait_ge(S("cmp_s"), COMPRESSED * TS)
            for n in range(4):
                act.activation(CVS[:, n * 512:(n + 1) * 512], bank[(0, 1, 5, 6)[n]][0:NC, :], ACT.Copy).then_inc(S("dec_act"), 1)
            act.wait_ge(S("dec_dve"), 6)
            for r, (a, n) in enumerate(((0, NK), (NK, NK), (2 * NK, NC))):
                act.activation(SS[:, a:a + n], SS[:, a:a + n], ACT.Exp, scale=SCALE, bias=st(0, 1)[:, r:r + 1],
                               accum_out=st(0, 2)[:, r:r + 1]).then_inc(S("dec_act"), 1)
            act.wait_ge(S("dec_pe"), 2)
            act.wait_ge(S("dec_dve"), 8)
            for c in range(2):
                w = slice(48 * c, 48 * c + 16)
                act.activation(PZ[:, :, :, w], bank[3][:, :].rearrange("p (m b c n) -> p m b c n", m=4, b=4, c=2)[:, :, :, c],
                               ACT.Copy).then_inc(S("dec_act"), 1)
                act.activation(PZC[:, :, w], bank[4][0:NC, 0:P].rearrange("p (b c n) -> p b c n", b=4, c=2)[:, :, c],
                               ACT.Copy).then_inc(S("dec_act"), 1)
            act.activation(PTN, bank[4][0:TS, P:3 * P], ACT.Copy).then_inc(S("dec_act"), 1)
            act.wait_ge(S("dec_pe"), 3)
            o = bank[6][:, 0:P].rearrange("p (b h e) -> p h e b", h=2, b=TS)
            for hh in range(2):
                r = slice(64 * hh, 64 * hh + 64)
                act.activation(Y[r, 0:8, TP:NT].rearrange("p (h g) b -> p h g b", h=2), o[r, :, 4 * hh:4 * hh + 4, :],
                               ACT.Copy).then_inc(S("dec_out"), 1)

        def dve_sample_weights(dve):
            do = Counted(dve, S("dec_dve"))
            dve.wait_ge(S("dk_used"), TS)
            dve.wait_ge(S("att_pv"), UNITS)
            sel_win = SS[:, 0:2 * NK].rearrange("p (r n) -> p r n", r=2)
            do(dve.tensor_tensor(sel_win[:, :, 0:PAST], bank[2][:, :].rearrange("p (r n) -> p r n", r=2),
                                 cc("ds", 0, PAST).unsqueeze(1).to_broadcast([P, 2, PAST]), ALU.add))
            do(dve.tensor_tensor(sel_win[:, :, PAST], bank[7][:, 16:18], cc("ds", PAST, 1).to_broadcast([P, 2]), ALU.add))
            do(dve.tensor_tensor(SS[:, 2 * NK:2 * NK + NC], bank[7][:, 0:NC], cc("dcs"), ALU.add))
            do.wait()
            do(dve.tensor_reduce(st(0, 0, 2), sel_win, AXX, ALU.max))
            do(dve.tensor_reduce(st(0, 0)[:, 2:3], SS[:, 2 * NK:2 * NK + NC], AXX, ALU.max))
            do.wait()
            do(dve.tensor_scalar(st(0, 1), st(0, 0), -SCALE, None, ALU.mult))
            do(dve.memset(x_t[:, 544:1568], 0.0))
            do(dve.memset(x_t[0:NC, 1568:1824], 0.0))
            dve.wait_ge(S("dec_act"), 7)
            do(dve.tensor_scalar(st(0, 3), st(0, 2), TINY, None, ALU.max))
            do.wait()
            do(dve.reciprocal(st(0, 4), st(0, 3)))
            do.wait()
            rc = st(0, 4)
            for k, (r, a, n) in enumerate(((1, 0, NK), (2, NK, NK), (0, 2 * NK, NC))):
                do(dve.tensor_scalar(SS[:, a:a + n], SS[:, a:a + n], rc[:, k:k + 1], GATE_S[:, r:r + 1], ALU.mult, ALU.mult))
            do.wait()
            for r in range(2):
                a = r * NK + PAST
                do(dve.tensor_scalar(PN[:, r * TS:(r + 1) * TS], cc("selT"), SS[:, a:a + 1], None, ALU.mult))
            assert do.n == 15
            do2 = Counted(dve, S("dec_own"))
            dve.wait_ge(S("dv_used"), TS)
            do2(dve.tensor_tensor(OX.rearrange("p (k d) -> p k d", k=KV), bank[5][:, 0:256].rearrange("p (k d) -> p k d", k=KV),
                                  cc("kvm").unsqueeze(2).to_broadcast([P, KV, HD]), ALU.mult))
            do2.wait()
            for n in range(2):
                do2(dve.tensor_reduce(OY[:, n * HD:(n + 1) * HD], OX.rearrange("p (k d) -> p d k", k=KV), AXX, ALU.add))

        def pe_sample_values(pe):
            pe.wait_ge(S("dec_act"), 12)
            for r in range(2):
                pe.matmul(bank[5][:, 0:256], lhsT=PTN[:, r * P:(r + 1) * P], rhs=NEW[:, 256 * (r + 1):256 * (r + 2)],
                          start=(r == 0), stop=False, skip_group_check=True)
            for b in range(TS):
                s = arrived(pe, "dv", b)
                rows, c = slice(32 * (b // 2), 32 * (b // 2) + 32), b % 2 * 32
                at_ = dict(start=False, tile_position=(0, rows.start), skip_group_check=True)
                for m in range(4):
                    pe.matmul(bank[5][rows, 0:256], lhsT=PZ[:, m, b // 2, c:c + 32],
                              rhs=ring[:, s * D + m * 256:s * D + (m + 1) * 256], stop=False, **at_)
                pe.matmul(bank[5][rows, 0:256], lhsT=PZC[:, b // 2, c:c + 32], rhs=CVS[:, b * 256:(b + 1) * 256],
                          stop=True, **at_).then_inc(S("dv_used"), 1)
            pe.wait_ge(S("dec_own"), 3)
            pe.transpose(bank[6][:, 0:P], OY, ident).then_inc(S("dec_pe"), 1)

        XQ = z_t[:, 0:KT * NT].rearrange("p (t n) -> p t n", n=NT)
        XP = [m_t[:, b * 256:(b + 1) * 256] for b in range(2)]
        XT = [m_t[:, 512 + b * 512:512 + (b + 1) * 512].rearrange("p (m n) -> p m n", m=2) for b in range(2)]
        XSP, XSO2 = m_t[0:32, 1536:1792], (m_t[0:32, 3840:4096], mk_t[0:32, 0:256])
        QX = x_t[:, 0:16 * 256].rearrange("p (t n) -> p t n", n=256)
        PX = m_t[:, 1792:3840].rearrange("p (m n) -> p m n", m=2)

        def pe_cross(pe):
            pe.wait_ge(S("evac"), tiles_before["xo"])

            def scores(u):
                h, qb = u // 2, u % 2
                if u >= 2:
                    pe.wait_ge(S("x_e"), u - 1)
                for d in range(4):
                    mm = pe.matmul(bank[u % 2][:, 0:MEM], lhsT=XQ[:, 4 * h + d, qb * P:(qb + 1) * P],
                                   rhs=MK[:, 4 * h + d, :], start=(d == 0), stop=(d == 3))
                mm.then_inc(S("x_s"), 1)

            def values(h):
                pe.wait_ge(S("x_pt"), 2 * h + 2)
                if h:
                    pe.wait_ge(S("x_o"), 4 * h)
                for d in range(4):
                    for m in range(2):
                        mm = pe.matmul(bank[4 + d][:, 0:TP], lhsT=MV[:, m, h * XD + d * P:h * XD + (d + 1) * P],
                                       rhs=XT[h % 2][:, m, :], start=(m == 0), stop=(m == 1))
                mm.then_inc(S("x_pv"), 1)

            scores(0)
            for u in range(8):
                if u < 7:
                    scores(u + 1)
                if u >= 3 and u % 2:
                    values(u // 2 - 1)
                pe.wait_ge(S("x_d"), 4 * (u + 1))
                if u >= 2:
                    pe.wait_ge(S("x_pt"), u - 1)
                for m in range(2):
                    tr = pe.transpose(bank[2 + u % 2][:, m * P:(m + 1) * P], XP[u % 2][:, m * P:(m + 1) * P], ident)
                tr.then_inc(S("x_t"), 1)
            values(3)
            pe.wait_ge(S("qx"), 5)
            for j in range(16):
                b, half = j // 2, j % 2
                s = arrived(pe, "mk", j)
                for t in range(8):
                    mm = pe.matmul(bank[0][0:32, 0:MEM], lhsT=QX[:, 8 * half + t, 32 * b:32 * b + 32],
                                   rhs=ring[:, s * D + t * 256:s * D + (t + 1) * 256],
                                   start=(j == 0 and t == 0), stop=(j == 15 and t == 7))
                mm.then_inc(S("mk_used"), 1)
            pe.wait_ge(S("xs_dve"), 4)
            for m in range(2):
                tr = pe.transpose(bank[2][:, m * 32:(m + 1) * 32], XSP[:, m * P:(m + 1) * P], ident[0:32, 0:32])
            tr.then_inc(S("xs_pe"), 1)
            pe.wait_ge(S("xs_act"), 2)
            for j in range(16):
                b, m = j // 2, j % 2
                s = arrived(pe, "mv", j)
                for h in range(XH):
                    r = b * XH + h
                    mm = pe.matmul(bank[3][0:32, :], lhsT=PX[:, m, 32 * r:32 * r + 32],
                                   rhs=ring[:, s * D + h * XD:s * D + (h + 1) * XD],
                                   start=(j == 0 and h == 0), stop=(j == 15 and h == XH - 1))
                mm.then_inc(S("mv_used"), 1)
            for n in range(2):
                pe.wait_ge(S("xs_act"), 3 + n)
                for d in range(2):
                    tr = pe.transpose(bank[n][:, d * 32:(d + 1) * 32], XSO2[n][:, d * P:(d + 1) * P], ident[0:32, 0:32])
                tr.then_inc(S("xs_pe"), 1)

        def dve_sample_xq(dve):
            dve.wait_ge(S("tile"), tiles_before["xo"])
            dve.memset(x_t[:, 0:16 * 256], 0.0).then_inc(S("qx"), 1)
            dve.wait_ge(S("evac"), tiles_before["xo"])
            dve.wait_ge(S("qx"), 1)
            for h in range(XH):
                dve.tensor_copy(QX[:, 4 * h:4 * h + 4, h::36], XQ[:, 4 * h:4 * h + 4, TP:NT]).then_inc(S("qx"), 1)
            dve.memset(m_t[:, 1792:3840], 0.0).then_inc(S("px"), 1)

        def dve_cross(dve):
            do = Counted(dve, S("x_d"))

            def outputs(h):
                dve.wait_ge(S("x_pv"), h + 1)
                for d in range(4):
                    dve.tensor_copy(Y[:, 4 * h + d, 0:TP], bank[4 + d][:, 0:TP]).then_inc(S("x_o"), 1)

            for u in range(8):
                b = u % 2
                dve.wait_ge(S("x_s"), u + 1)
                do(dve.tensor_reduce(st(b, 0, 1), bank[b][:, 0:MEM], AXX, ALU.max))
                do.wait()
                do(dve.tensor_scalar(st(b, 1, 1), st(b, 0, 1), -XSCALE, None, ALU.mult))
                dve.wait_ge(S("x_e"), u + 1)
                do(dve.reciprocal(st(b, 3, 1), st(b, 2, 1)))
                do.wait()
                do(dve.tensor_scalar(XP[b], XP[b], st(b, 3, 1), None, ALU.mult))
                if u >= 4 and u % 2 == 0:
                    outputs(u // 2 - 2)
            outputs(2)
            outputs(3)
            do = Counted(dve, S("xs_dve"))
            dve.wait_ge(S("mk_used"), 16)
            do(dve.tensor_reduce(small[0:32, 0:1], bank[0][0:32, 0:MEM], AXX, ALU.max))
            do.wait()
            do(dve.tensor_scalar(small[0:32, 3:4], small[0:32, 0:1], -XSCALE, None, ALU.mult))
            dve.wait_ge(S("xs_act"), 1)
            do(dve.reciprocal(small[0:32, 9:10], small[0:32, 6:7]))
            do.wait()
            do(dve.tensor_scalar(XSP, XSP, small[0:32, 9:10], None, ALU.mult))

        def act_cross(act):
            def keep(u):
                h, qb = u // 2, u % 2
                act.wait_ge(S("x_t"), u + 1)
                if h >= 2:
                    act.wait_ge(S("x_pv"), h - 1)
                act.activation(XT[h % 2][:, :, qb * P:(qb + 1) * P],
                               bank[2 + u % 2][:, 0:256].rearrange("p (m n) -> p m n", m=2), ACT.Copy).then_inc(S("x_pt"), 1)

            for u in range(8):
                b = u % 2
                act.wait_ge(S("x_d"), 4 * u + 2)
                if u >= 2:
                    act.wait_ge(S("x_t"), u - 1)
                act.activation(XP[b], bank[b][:, 0:MEM], ACT.Exp, scale=XSCALE, bias=st(b, 1, 1),
                               accum_out=st(b, 2, 1)).then_inc(S("x_e"), 1)
                if u:
                    keep(u - 1)
            keep(7)
            act.wait_ge(S("xs_dve"), 2)
            act.activation(XSP, bank[0][0:32, 0:MEM], ACT.Exp, scale=XSCALE, bias=small[0:32, 3:4],
                           accum_out=small[0:32, 6:7]).then_inc(S("xs_act"), 1)
            act.wait_ge(S("xs_pe"), 1)
            act.wait_ge(S("px"), 1)
            act.activation(PX[:, :, 0::33], bank[2][:, 0:64].rearrange("p (m r) -> p m r", m=2), ACT.Copy)\
                .then_inc(S("xs_act"), 1)
            act.wait_ge(S("mv_used"), 16)
            for n in range(2):
                act.activation(XSO2[n], bank[3][0:32, n * 256:(n + 1) * 256], ACT.Copy).then_inc(S("xs_act"), 1)
            y = Y[:, :, TP:NT].rearrange("p (h d) b -> p d b h", h=XH)
            for n in range(2):
                act.wait_ge(S("xs_pe"), 2 + n)
                act.activation(y[:, 2 * n:2 * n + 2], bank[n][:, 0:64].rearrange("p (d b h) -> p d b h", d=2, h=XH), ACT.Copy)\
                    .then_inc(S("xs_out"), 1)

        def pe_middle(pe):
            pe_by_token(pe)
            pe_scores(pe, 0)
            pe_scores(pe, 1)
            pe_compressed(pe)
            for u in range(UNITS + 2):
                if u + 2 < UNITS:
                    pe_scores(pe, u + 2)
                if u >= 2:
                    pe_values(pe, u - 2)
                if u < UNITS:
                    pe_turn(pe, u)
                if u % 4 == 3 and u < UNITS:
                    pe_sample_scores(pe, u // 4)
            pe_sample_turn(pe)
            pe_sample_values(pe)
            pe_norm(pe, "att", X[:, 0:8, :], 8)
            pe.wait_ge(S("att_x"), 9)
            pe.wait_ge(S("ssm_x"), 9)
            pe_gemm(pe, "out", Y, KT)
            pe_norm(pe, "x", SQ, KT)
            pe.wait_ge(S("x_x"), KT + 1)
            pe_gemm(pe, "xq", X, KT)
            pe_cross(pe)
            pe.wait_ge(S("x_o"), 16)
            pe.wait_ge(S("xs_out"), 2)
            pe_gemm(pe, "xo", Y, KT)
            pe_norm(pe, "ffn", SQ, KT)
            pe_by_rows(pe)
            pe.wait_ge(S("ffn_x"), KT + 1)
            pe_gemm(pe, "pq", X, KT)

        def act_middle(act):
            act_by_token(act)
            for u in range(UNITS):
                act_exp(act, u)
                if u == 0:
                    act_compressed(act)
                if u >= 1:
                    act_keep(act, u - 1)
                if u >= 4 and u % 2 == 0:
                    act_attended(act, (u - 4) // 2)
            act_keep(act, UNITS - 1)
            act_attended(act, UNITS // 2 - 2)
            act_attended(act, UNITS // 2 - 1)
            act_sample_scores(act)
            act.wait_ge(S("dec_out"), 2)
            act_norm(act, "att", Y[:, 0:8, :], X[:, 0:8, :], 8, 1024)
            act.wait_ge(S("evac"), tiles_before["xq"])
            act_norm(act, "x", H, SQ, KT, D)
            act.wait_ge(S("z_stored"), 16)
            copy_gemm(act, "xq", XQ)
            act_cross(act)
            act.wait_ge(S("evac"), tiles_before["pq"])
            act_norm(act, "ffn", H, SQ, KT, D)
            act_by_rows(act)
            copy_gemm(act, "pq", XQ)

        def dve_middle(dve):
            dve_by_token(dve)
            dve_compressed(dve)
            for u in range(UNITS + 1):
                dve_unit(dve, u)
                if u % 4 == 2:
                    dve_sample_compress(dve, u // 4)
            dve_sample_weights(dve)
            dve_norm(dve, "att", Y[:, 0:8, :], Y[:, 0:8, :], 8, G_ATT)
            add_gemm(dve, "out", H)
            dve.wait_ge(S("new_stored"), 32)
            dve_norm(dve, "x", X, H, KT, G_X)
            dve_sample_xq(dve)
            dve_cross(dve)
            add_gemm(dve, "xo", H)
            dve_norm(dve, "ffn", X, H, KT, G_FFN)
            dve_by_rows(dve)

        def pool_middle(pool):
            pool_new_rows(pool)
            pool_caches(pool)
            pool.wait_ge(S("evac"), tiles_before["xq"])
            pool.wait_ge(S("z_stored"), 16)
            pool.dma_start(KEYS, A["keys"]).then_inc(S("ld_keys"), 16)
            pool.dma_start(GB, A["g_ffn"].partition_broadcast(P)).then_inc(S("ld_gf"), 16)

        BLOCKS = (P, P, TS)
        HN = [mv_n[:, 0:D], mv_n[:, D:2 * D], b_st[:, :]]
        XN = [y_t[:, 0:D], y_t[:, D:2 * D], c_st[:, :]]
        ACC_S = y_t[:, 0:D]
        GB = z_t[:, KT * NT:KT * NT + D]
        SLOT = [ring[:, i * D:(i + 1) * D] for i in range(4)] + [m_t[:, 0:D], m_t[:, D:2 * D], mk_t[:, 0:D], mk_t[:, D:2 * D]]
        NSLOT = len(SLOT)
        SCO, CAND = x_t[:, 0:D], x_t[:, D:2 * D]
        HOT = h_t[:, 0:D]

        def hw(a, n=SLOTS):
            return h_t[:, D + a:D + a + n]

        VAL, VIX, VIF = hw(0, 256), hw(256, 256), hw(512, 256)
        TOP, PIX, PF, PA, IA, IB = (hw(768 + 128 * i) for i in range(6))
        WGT = [hw(1536 + 128 * i) for i in range(3)]
        ACTV = hw(1920)
        EIX = [z_t[:, 6272 + 128 * i:6272 + 128 * (i + 1)].bitcast(I32) for i in range(2)]
        EXF, EXS = z_t[:, 6528:6536], z_t[:, 6864:6872].bitcast(I32)
        WS, AS, RED, STAT = z_t[:, 6536:6544], z_t[:, 6544:6552], z_t[:, 6552:6568], z_t[:, 6568:6592]
        KEYS = z_t[:, 6592:6848].rearrange("p (c n) -> p c n", c=2)
        IXS = [z_t[:, 6848 + 8 * i:6856 + 8 * i].bitcast(I32) for i in range(2)]
        EXPW = z_t[:, 6880:7008]

        def pe_by_rows(pe):
            pe.wait_ge(S("ffn_rms"), 1)
            for blk, n in enumerate(BLOCKS):
                lo = blk * P
                for q in range(4):
                    k = 4 * blk + q
                    if k >= 4:
                        pe.wait_ge(S("hn_act"), k - 3)
                    for d in range(4):
                        tr = pe.transpose(bank[4 + q][0:n, d * P:(d + 1) * P], H[:, 4 * q + d, lo:lo + n], ident)
                    tr.then_inc(S("hn_pe"), 1)

        def act_row_root(act, blk, junk, tag, base):
            n, c = BLOCKS[blk], STAT[:, base + 3 * blk:base + 3 * blk + 3]
            act.activation(junk[0:n, :], HN[blk][0:n, :], ACT.Square, accum_out=c[0:n, 0:1]).then_inc(S(tag), 1)
            act.wait_ge(S(tag), 2 * blk + 1)
            act.activation(c[0:n, 1:2], c[0:n, 0:1], ACT.Sqrt, bias=cc("eps", rows=n), scale=1.0 / D).then_inc(S(tag), 1)

        def dve_row_scale(dve, blk, dst, tag, done, base):
            n, c = BLOCKS[blk], STAT[:, base + 3 * blk:base + 3 * blk + 3]
            dve.wait_ge(S(tag), 2 * blk + 2)
            dve.reciprocal(c[0:n, 2:3], c[0:n, 1:2]).then_inc(S(done), 1)
            dve.wait_ge(S(done), 2 * blk + 1)
            dve.scalar_tensor_tensor(out=dst[0:n, :], in0=HN[blk][0:n, :], scalar=c[0:n, 2:3], in1=GB[0:n, :],
                                     op0=ALU.mult, op1=ALU.mult).then_inc(S(done), 1)

        def act_by_rows(act):
            act.wait_ge(S("m_stored"), 32)
            for blk, n in enumerate(BLOCKS):
                for q in range(4):
                    act.wait_ge(S("hn_pe"), 4 * blk + q + 1)
                    act.activation(HN[blk][0:n, q * 512:(q + 1) * 512], bank[4 + q][0:n, :], ACT.Copy).then_inc(S("hn_act"), 1)
            act.wait_ge(S("hn_act"), 12)
            for blk in range(3):
                if blk:
                    act.wait_ge(S("row_rms"), 2 * blk)
                act_row_root(act, blk, m_t[:, 0:D], "row_rms", 0)

        def dve_by_rows(dve):
            dve.wait_ge(S("ld_gf"), 16)
            for blk in range(3):
                dve_row_scale(dve, blk, XN[blk], "row_rms", "xn", 0)

        def pe_keys(pe, blk):
            n, lo = BLOCKS[blk], blk * P
            pe.wait_ge(S("evac"), tiles_before["pq"] + 16)
            pe.wait_ge(S("ld_keys"), 16)
            if blk:
                pe.wait_ge(S("sco_act"), 4 * blk)
            for q in range(4):
                for k in range(4):
                    t = 4 * q + k
                    mm = pe.matmul(bank[q][0:n, k * PK:(k + 1) * PK], lhsT=XQ[:, t, lo:lo + n], rhs=KEYS[:, t % 2, :],
                                   start=True, stop=True)
                mm.then_inc(S("sco_pe"), 1)

        TK_KEYS, TK_CAND, TK_IX, TK = 80, 123, 136, 139

        def act_keys(act, blk):
            n = BLOCKS[blk]
            if blk:
                act.wait_ge(S("tk"), TK * (blk - 1) + TK_CAND)
            for q in range(4):
                act.wait_ge(S("sco_pe"), 4 * blk + q + 1)
                act.activation(SCO[0:n, q * 512:(q + 1) * 512], bank[q][0:n, :], ACT.Copy).then_inc(S("sco_act"), 1)
            act.wait_ge(S("tk"), TK * blk + TK_CAND)
            act.activation(WGT[blk][0:n, :], WGT[blk][0:n, :], ACT.Exp).then_inc(S("tk_exp"), 1)

        def dve_sixteen(do, n, src, work, groups, width, val, ix):
            r, eng = slice(0, n), do.eng

            def part(t, m, w=width):
                return t[r, m * w:(m + 1) * w]

            def eight(t, m, k):
                return t[r, m * 16 + 8 * k:m * 16 + 8 * k + 8]

            for m in range(groups):
                do(eng.max(eight(val, m, 0), part(src, m)))
            do.wait()
            for m in range(groups):
                do(eng.match_replace(part(work, m), eight(val, m, 0), part(src, m), -3e38))
                do(eng.max_index(eight(ix, m, 0), eight(val, m, 0), part(src, m)))
            do.wait()
            for m in range(groups):
                do(eng.max(eight(val, m, 1), part(work, m)))
            do.wait()
            for m in range(groups):
                do(eng.max_index(eight(ix, m, 1), eight(val, m, 1), part(work, m)))

        def dve_keys(dve, blk):
            do = Counted(dve, S("tk"), TK * blk)
            if blk:
                do.wait(0)
            dve.wait_ge(S("sco_act"), 4 * (blk + 1))
            dve_sixteen(do, BLOCKS[blk], SCO, HOT, 16, PK, VAL, VIX.bitcast(U32))
            assert do.n == TK_KEYS

        def dve_candidates(dve, blk):
            n, do = BLOCKS[blk], Counted(dve, S("tk"), TK * blk + TK_KEYS)
            do.wait()
            r = slice(0, n)
            v = VAL[r, :].rearrange("p (h c k) -> p h c k", h=PH, c=2)
            do(dve.tensor_copy(VIF[r, :], VIX.bitcast(U32)[r, :]))
            do(dve.tensor_tensor(CAND[r, :].rearrange("p (h a b) -> p h a b", h=PH, a=16),
                                 v[:, :, 0].unsqueeze(3).to_broadcast([n, PH, 16, 16]),
                                 v[:, :, 1].unsqueeze(2).to_broadcast([n, PH, 16, 16]), ALU.add))
            do.wait()
            dve_sixteen(do, n, CAND, SCO, PH, 256, TOP, PIX.bitcast(U32))
            do.wait()
            t3 = TOP[r, :].rearrange("p (h k) -> p h k", h=PH)
            do(dve.tensor_tensor(WGT[blk][r, :].rearrange("p (h k) -> p h k", h=PH), t3,
                                 t3[:, :, 0:1].to_broadcast([n, PH, 16]), ALU.subtract))
            assert do.n + TK_KEYS == TK_CAND

        def dve_experts(dve, blk):
            n, do = BLOCKS[blk], Counted(dve, S("tk"), TK * blk + TK_CAND)
            do.wait()
            r = slice(0, n)
            vi = VIF[r, :].rearrange("p (h c k) -> p h c k", h=PH, c=2)
            do(dve.tensor_copy(PF[r, :], PIX.bitcast(U32)[r, :]))
            do.wait()
            do(dve.tensor_scalar(PA[r, :], PF[r, :], 1 / 16, -15 / 32, ALU.mult, ALU.add))
            do.wait()
            do(dve.tensor_scalar(PA[r, :], PA[r, :], MAGIC, None, ALU.add))
            do.wait()
            do(dve.tensor_scalar(PA[r, :], PA[r, :], MAGIC, None, ALU.subtract))
            do.wait()
            do(dve.scalar_tensor_tensor(out=PF[r, :], in0=PA[r, :], scalar=-16.0, in1=PF[r, :], op0=ALU.mult, op1=ALU.add))
            hot = HOT[r, :].rearrange("p (s k) -> p s k", k=16)
            hot4 = HOT[r, :].rearrange("p (h s k) -> p h s k", h=PH, k=16)
            for c, (pos, out) in enumerate(((PA, IA), (PF, IB))):
                do.wait()
                do(dve.tensor_tensor(hot, cc("iota")[r, :].unsqueeze(1).to_broadcast([n, SLOTS, 16]),
                                     pos[r, :].unsqueeze(2).to_broadcast([n, SLOTS, 16]), ALU.is_equal))
                do.wait()
                do(dve.tensor_tensor(hot4, hot4, vi[:, :, c].unsqueeze(2).to_broadcast([n, PH, 16, 16]), ALU.mult))
                do.wait()
                do(dve.tensor_reduce(out[r, :], hot, AXX, ALU.add))
            do.wait()
            do(dve.scalar_tensor_tensor(out=IA[r, :], in0=IA[r, :], scalar=float(PK), in1=IB[r, :], op0=ALU.mult, op1=ALU.add))
            if blk < 2:
                do.wait()
                do(dve.tensor_copy(EIX[blk], IA))
                assert do.n + TK_CAND == TK_IX
            w3 = WGT[blk][r, :].rearrange("p (h k) -> p h k", h=PH)
            dve.wait_ge(S("tk_exp"), blk + 1)
            do(dve.tensor_reduce(RED[r, 0:8], w3, AXX, ALU.add))
            do.wait()
            do(dve.reciprocal(RED[r, 8:16], RED[r, 0:8]))
            do.wait()
            do(dve.tensor_tensor(w3, w3, RED[r, 8:16].unsqueeze(2).to_broadcast([n, PH, 16]), ALU.mult))
            return do.n

        def pe_samples_expand(pe):
            pe.wait_ge(S("xn"), 6)
            for q in range(4):
                mm = pe.matmul(bank[4 + q][:, :], lhsT=cc("sel", rows=TS), rhs=XN[2][0:TS, q * 512:(q + 1) * 512],
                               start=True, stop=True)
            mm.then_inc(S("ex_pe"), 1)

        def act_samples_expand(act):
            act.wait_ge(S("ex_pe"), 1)
            for q in range(4):
                act.activation(XN[2][:, q * 512:(q + 1) * 512], bank[4 + q][:, :], ACT.Copy).then_inc(S("ex_act"), 1)

        def pe_samples_experts(pe):
            pe.wait_ge(S("ex_act"), 4)
            pe.wait_ge(S("tk"), 2 * TK + TK - 1)
            pe.matmul(bank[4][:, 0:P], lhsT=cc("sel", rows=TS), rhs=IA[0:TS, :], start=True, stop=True)
            pe.matmul(bank[5][:, 0:P], lhsT=cc("sel", rows=TS), rhs=WGT[2][0:TS, :], start=True, stop=True)\
                .then_inc(S("ex_pe"), 1)

        def dve_samples_experts(dve):
            do = Counted(dve, S("ex_dve"))
            dve.wait_ge(S("ex_pe"), 2)
            mask = cc("kmask").unsqueeze(1).to_broadcast([P, PH, 16])
            for n, out in enumerate((EXF, WS)):
                if n:
                    do.wait()
                do(dve.tensor_tensor(EXPW.rearrange("p (h k) -> p h k", h=PH),
                                     bank[4 + n][:, 0:P].rearrange("p (h k) -> p h k", h=PH), mask, ALU.mult))
                do.wait()
                do(dve.tensor_reduce(out, EXPW.rearrange("p (h k) -> p h k", h=PH), AXX, ALU.add))
            do(dve.tensor_scalar(EXF, EXF, MAGIC, None, ALU.add))
            do.wait()
            do(dve.tensor_scalar(EXF, EXF, MAGIC, None, ALU.subtract))
            do.wait()
            do(dve.tensor_copy(EXS, EXF))

        U_OF, V_OF = (0, 2 * SLOTS), (SLOTS, 3 * SLOTS)
        U_S, V_S = 4 * SLOTS, 4 * SLOTS + PH

        def pool_peer(pool):
            with pool.register("round") as rnd, pool.register("use") as use:
                pool.reg_mov(rnd, 3)
                pool.reg_mov(use, 1 + NSLOT)

                def gather(table, half, k):
                    pool.indirect_dma_start(SLOT[k], None, A[table], bass.IndirectOffsetOnAxis(IXS[half][:, k:k + 1], 0))\
                        .then_inc(S(f"slot{k}"), 16)

                def single(table, g, index):
                    half = g // NSLOT % 2
                    pool.tensor_copy(IXS[half], index).then_inc(S("ixs"), 1)
                    pool.wait_ge(S("ixs"), g // NSLOT + 1)
                    for k in range(NSLOT):
                        if g:
                            pool.wait_ge(S("peer_used"), g + k + 1 - NSLOT)
                        gather(table, half, k)

                def gathers(table, blk, i0=0):
                    with pool.Fori(i0, SLOTS // (2 * NSLOT)) as i:
                        for half in range(2):
                            pool.tensor_copy(IXS[half], EIX[blk][:, bass.ds(i * (2 * NSLOT) + half * NSLOT, NSLOT)])\
                                .then_inc(S("ixs"), 1)
                            pool.wait_ge(S("ixs"), rnd)
                            pool.reg_add(rnd, rnd, 1)
                            for k in range(NSLOT):
                                pool.wait_ge(S("peer_used"), use)
                                pool.reg_add(use, use, 1)
                                gather(table, half, k)

                pool.wait_ge(S("tk"), TK_IX)
                for half in range(2):
                    single("peer_u", half * NSLOT, EIX[0][:, half * NSLOT:(half + 1) * NSLOT])
                gathers("peer_u", 0, 1)
                gathers("peer_v", 0)
                pool.wait_ge(S("tk"), TK + TK_IX)
                gathers("peer_u", 1)
                gathers("peer_v", 1)
                pool.wait_ge(S("ex_dve"), 7)
                single("peer_u", U_S, EXS)
                single("peer_v", V_S, EXS)

        def dve_dots(dve, blk, quarter):
            with dve.Fori(quarter * SLOTS // 4 // NSLOT, (quarter + 1) * SLOTS // 4 // NSLOT) as i:
                for k in range(NSLOT):
                    dve.wait_ge(S(f"slot{k}"), i * 16 + 16 * (U_OF[blk] // NSLOT + 1))
                    dve.scalar_tensor_tensor(out=SLOT[k], in0=SLOT[k], scalar=1.0, in1=XN[blk], op0=ALU.mult, op1=ALU.mult,
                                             accum_out=ACTV[:, bass.ds(i * NSLOT + k, 1)]).then_inc(S("peer_used"), 1)

        def dve_sums(dve, blk, quarter):
            with dve.Fori(quarter * SLOTS // 4 // NSLOT, (quarter + 1) * SLOTS // 4 // NSLOT) as i:
                for k in range(NSLOT):
                    dve.wait_ge(S(f"slot{k}"), i * 16 + 16 * (V_OF[blk] // NSLOT + 1))
                    dve.wait_ge(S("peer_used"), i * NSLOT + (V_OF[blk] + k))
                    dve.scalar_tensor_tensor(out=HN[blk], in0=SLOT[k], scalar=WGT[blk][:, bass.ds(i * NSLOT + k, 1)],
                                             in1=HN[blk], op0=ALU.mult, op1=ALU.add).then_inc(S("peer_used"), 1)

        def dve_samples_dots(dve):
            for k in range(PH):
                dve.wait_ge(S(f"slot{k}"), 16 * (U_S // NSLOT + 1))
                dve.scalar_tensor_tensor(out=SLOT[k], in0=SLOT[k], scalar=1.0, in1=XN[2], op0=ALU.mult, op1=ALU.mult,
                                         accum_out=AS[:, k:k + 1]).then_inc(S("peer_used"), 1)

        def dve_samples_sums(dve):
            for k in range(PH):
                dve.wait_ge(S(f"slot{k}"), 16 * (V_S // NSLOT + 1))
                if k == 0:
                    dve.tensor_scalar(ACC_S, SLOT[k], WS[:, k:k + 1], None, ALU.mult).then_inc(S("peer_used"), 1)
                else:
                    dve.wait_ge(S("peer_used"), V_S + k)
                    dve.scalar_tensor_tensor(out=ACC_S, in0=SLOT[k], scalar=WS[:, k:k + 1], in1=ACC_S,
                                             op0=ALU.mult, op1=ALU.add).then_inc(S("peer_used"), 1)
            for q in range(4):
                dve.wait_ge(S("sum_pe"), q + 1)
                dve.tensor_tensor(HN[2][0:TS, q * 512:(q + 1) * 512], HN[2][0:TS, q * 512:(q + 1) * 512],
                                  bank[4 + q][0:TS, :], ALU.add).then_inc(S("sum_s"), 1)

        def pe_samples_sums(pe):
            pe.wait_ge(S("peer_used"), V_S + PH)
            for q in range(4):
                pe.matmul(bank[4 + q][0:TS, :], lhsT=cc("selT"), rhs=ACC_S[:, q * 512:(q + 1) * 512],
                          start=True, stop=True).then_inc(S("sum_pe"), 1)

        def act_gelu(act, blk):
            a, done = (AS, V_S) if blk == 2 else (ACTV, V_OF[blk])
            act.wait_ge(S("peer_used"), done)
            act.activation(a, a, ACT.Gelu_apprx_tanh).then_inc(S("gelu"), 1)

        def dve_gelu(dve, blk):
            w, a = (WS, AS) if blk == 2 else (WGT[blk], ACTV)
            dve.wait_ge(S("gelu"), blk + 1)
            dve.tensor_tensor(w, w, a, ALU.mult).then_inc(S("wgt"), 1)
            dve.wait_ge(S("wgt"), blk + 1)

        def act_final(act, blk):
            if blk < 2:
                act.wait_ge(S("peer_used"), V_OF[blk] + SLOTS)
            else:
                act.wait_ge(S("sum_s"), 4)
            if blk:
                act.wait_ge(S("f_rms"), 2 * blk)
            act_row_root(act, blk, HOT, "f_rms", 9)

        def dve_final(dve, blk):
            if blk == 0:
                dve.wait_ge(S("ld_last"), 16)
            dve_row_scale(dve, blk, HN[blk], "f_rms", "y", 9)

        def sp_peer(sp):
            sp.wait_ge(S("xn"), 6)
            sp.dma_start(GB, A["g_final"].partition_broadcast(P)).then_inc(S("ld_last"), 16)
            for blk in range(3):
                sp.wait_ge(S("y"), 2 * blk + 2)
                dst = A["y_p"][blk * P:(blk + 1) * P, :] if blk < 2 else A["y_s"]
                sp.dma_start(dst, HN[blk][0:BLOCKS[blk], :]).then_inc(S("y_stored"), 16)
            sp.wait_ge(S("y_stored"), 48)

        @block.sync
        def _(sp):
            sp_stream(sp)
            sp_peer(sp)

        @block.tensor
        def _(pe):
            pe_front(pe)
            pe_middle(pe)
            pe_keys(pe, 0)
            pe_keys(pe, 1)
            pe_samples_expand(pe)
            pe_keys(pe, 2)
            pe_samples_experts(pe)
            pe_samples_sums(pe)

        @block.scalar
        def _(act):
            act_front(act)
            act_middle(act)
            act_keys(act, 0)
            act_samples_expand(act)
            act_keys(act, 1)
            act_gelu(act, 0)
            act_keys(act, 2)
            act_final(act, 0)
            act_gelu(act, 1)
            act_final(act, 1)
            act_gelu(act, 2)
            act_final(act, 2)

        @block.vector
        def _(dve):
            dve_index(dve)
            dve_front(dve)
            dve_middle(dve)
            dve_keys(dve, 0)
            dve_candidates(dve, 0)
            dve_experts(dve, 0)
            dve_dots(dve, 0, 0)
            dve_keys(dve, 1)
            dve_dots(dve, 0, 1)
            dve_candidates(dve, 1)
            dve_dots(dve, 0, 2)
            dve_experts(dve, 1)
            dve_dots(dve, 0, 3)
            dve_gelu(dve, 0)
            dve_sums(dve, 0, 0)
            dve_keys(dve, 2)
            dve_sums(dve, 0, 1)
            dve_candidates(dve, 2)
            dve_sums(dve, 0, 2)
            dve_experts(dve, 2)
            dve_sums(dve, 0, 3)
            dve_dots(dve, 1, 0)
            dve_final(dve, 0)
            dve_dots(dve, 1, 1)
            dve_samples_experts(dve)
            dve_dots(dve, 1, 2)
            dve_dots(dve, 1, 3)
            dve_gelu(dve, 1)
            for quarter in range(4):
                dve_sums(dve, 1, quarter)
            dve_samples_dots(dve)
            dve_final(dve, 1)
            dve_gelu(dve, 2)
            dve_samples_sums(dve)
            dve_final(dve, 2)

        @block.gpsimd
        def _(pool):
            pool_front(pool)
            pool_middle(pool)
            pool_peer(pool)
            pool.wait_ge(S("stored"), 64)
            pool.wait_ge(S("z_stored"), 16)
            pool.wait_ge(S("m_stored"), 32)
            pool.wait_ge(S("new_stored"), 32)


def kernel(**inputs):
    import concourse.bacc as bacc
    from concourse.bass_utils import run_bass_kernel_spmd

    a = {k: np.asarray(v) for k, v in inputs.items()}

    def feature_tiles(x):
        return x.T.reshape(-1, P, x.shape[0]).transpose(1, 0, 2)

    def columns(v):
        return v.reshape(-1, P).T

    def weight(w):
        k, n = w.shape
        return w.reshape(k // P, P, n // P, P).transpose(2, 1, 0, 3).reshape(n // P, P, k)

    def pair_heads(w):
        return w.reshape(2, 2, GQ, HD, -1).transpose(0, 2, 1, 3, 4).reshape(HEADS * HD, -1)

    def states(v):
        return np.moveaxis(v.reshape(-1, ST, P), (2, 1, 0), (0, 1, 2))

    def groups(v):
        out = np.zeros((ST, 2, SN, 2, SG), np.float32)
        g = v.reshape(ST, 2, SN, SG)
        out[:, 0, :, 0], out[:, 1, :, 1] = g[:, 0], g[:, 1]
        return out.reshape(ST, P, 32).transpose(1, 0, 2).reshape(P, ST * 32)

    def pages(pool):
        return pool.reshape(20, P, 2, P).transpose(0, 3, 2, 1).reshape(2560, 256)

    tokens = np.concatenate([a["x_prompt"][0], a["x_sample"][:, 0]])
    w_in = a["w_in"][0]
    w_z = np.concatenate([pair_heads(w_in[:, :1024].T).T, w_in[:, 1024:2560], w_in[:, 2608:]], 1)
    w_out = np.concatenate([pair_heads(a["w_out"][0, :1024]), a["w_out"][0, 1024:]])
    log_dt = np.broadcast_to(a["log_dt"][0][:, None], (GROUPS, SN))
    w_cmp = np.stack([np.repeat(a[n][0], HD, 0).reshape(2, P, CMP) for n in ("w_cmp_k", "w_cmp_v")])
    given = {
        "consts": constants(),
        "gains": np.concatenate([columns(x) for x in (
            a["g_mix"][0], a["g_x"][0], a["g_mem"][0], a["g_ffn"][0],
            pair_heads(a["g_attn_out"][0][:, None])[:, 0], a["g_ssm_out"][0], a["d_skip"][0])], 1),
        "x_t": feature_tiles(tokens), "mem_t": feature_tiles(a["mem_prompt"][0]),
        "w_z": weight(w_z), "w_gate": w_in[:, 2560:2608].reshape(KT, P, 48).transpose(1, 0, 2).reshape(P, -1),
        "w_out": weight(w_out),
        **{n: weight(a[n][0]) for n in ("w_xk", "w_xv", "w_glu", "w_xq", "w_xo", "w_pq")},
        "s5_par": np.stack([states(x)[:, :, 0] for x in (a["lam_re"][0], a["lam_im"][0], log_dt)], 1),
        "s5_b": np.stack([groups(a[n][0]) for n in ("b_re", "b_im")], 1),
        "s5_c": np.stack([groups(a[n][0].transpose(0, 2, 1)) for n in ("c_re", "c_im")], 1),
        "s5_h0": np.stack([states(a[n][0]).reshape(P, -1) for n in ("state_s5_re", "state_s5_im")], 1),
        "w_cmp": w_cmp.transpose(2, 0, 1, 3), "page": a["page_table"].reshape(-1),
        "pool_kc": pages(a["cache_k_cmp"][0]), "pool_vc": pages(a["cache_v_cmp"][0]),
        "pool_ks": pages(a["cache_k_sel"][0]), "pool_vs": a["cache_v_sel"][0].reshape(2560, 256),
        "win_k": a["cache_k_win"][0].reshape(TS, 2, P, 2, P).transpose(0, 4, 1, 3, 2).reshape(TS, P, 512),
        "win_v": a["cache_v_win"][0].reshape(TS, 2, P, 256).transpose(0, 2, 1, 3).reshape(TS, P, 512),
        "mem_k": a["cache_mem_k"][0].reshape(TS, MEM, 2, 8, P).transpose(0, 2, 4, 3, 1).reshape(TS, 2, P, D),
        "mem_v": a["cache_mem_v"][0].reshape(TS, 2, P, D),
        "keys": np.stack([a["peer_k1"][0].T, a["peer_k2"][0].T], 1),
        "peer_u": a["peer_u"][0], "peer_v": a["peer_v"][0], "g_ffn": a["g_ffn"][0], "g_final": a["g_final"],
        "buf_k": a["cache_k_win"][0].reshape(TS, -1), "buf_v": a["cache_v_win"][0].reshape(TS, -1),
    }
    nc = bacc.Bacc("TRN2", target_bir_lowering=False, num_devices=1)
    arrays, args = {}, {}
    for name, shape in INS.items():
        x = np.ascontiguousarray(given[name])
        assert x.shape == shape, (name, x.shape, shape)
        arrays["in_" + name] = x
        args[name] = nc.dram_tensor("in_" + name, x.shape, mybir.dt.from_np(x.dtype), kind="ExternalInput").ap()
    for name, shape in OUTS.items():
        args[name] = nc.dram_tensor("out_" + name, shape, F32, kind="ExternalOutput").ap()
    build(nc, args)
    got = run_bass_kernel_spmd(nc, [arrays], core_ids=[0]).results[0]
    o = {name: np.asarray(got["out_" + name]) for name in OUTS}

    z = o["z_kv"].reshape(6, KV, HD, NT)
    kv_p = [z[i, :, :, :TP].transpose(2, 0, 1)[None, None] for i in range(6)]
    kv_s = [z[i, :, :, TP:].transpose(2, 0, 1)[None, :, None] for i in range(6)]

    def of_states(v, n):
        return [x.transpose(2, 1, 0).reshape((1, n, GROUPS, SN)) for x in v.reshape(P, 2, ST, n).swapaxes(0, 1)]

    return (o["y_p"][None], o["y_s"][:, None], *kv_p, *of_states(o["s5_p"], 1),
            o["m_k"].transpose(2, 0, 1).reshape(1, 1, MEM, XH, XD), o["m_v"].reshape(1, 1, MEM, XH, XD),
            *kv_s[:4], *(o[n].reshape(1, TS, 257, KV, HD) for n in ("new_k", "new_v")), *of_states(o["s5_s"], TS))
```

```python
from contextlib import ExitStack

import numpy as np
import concourse.bass as bass
from concourse import mybir

ALU = mybir.AluOpType
ACT = mybir.ActivationFunctionType
AXX = mybir.AxisListType.X
F32 = mybir.dt.float32
I32 = mybir.dt.int32
U32 = mybir.dt.uint32

P = 128
D = 2048
KT = D // P
TP, TS = 256, 8
NT = TP + TS
QB = TP // P
HEADS, KV, GQ, HD = 16, 4, 4, 64
CMP, STRIDE = 32, 16
NC = TP // STRIDE - 1
PAST = 256
SCALE = HD ** -0.5
NEG, TINY, EPS = -1e30, 1e-30, 1e-6
XH, XD, MEM = 4, 512, 256
XSCALE = XD ** -0.5
GROUPS, SG, SN = 64, 16, 64
ST = GROUPS * SN // P
PH, PK, TOPK = 8, 128, 16
SLOTS = PH * TOPK
SLOPE = [2.0 ** (-8.0 * (h + 1) / HEADS) for h in range(HEADS)]
MAGIC = 12582912.0
TWO_PI = 6.2831850

Q0, K_CMP, V_CMP, K_SEL, V_SEL, K_WIN, V_WIN, U0, NZ = 0, 8, 10, 12, 14, 16, 18, 20, 28

C = {}
for _name, _n in (("ident", P), ("ones", P), ("d0", P), ("d1", TP), ("cb", QB * TP), ("mc", QB * 16), ("ds", PAST + 1),
                  ("dcs", NC), ("t", TP), ("sel", P), ("selT", TS), ("kmask", 16), ("selk", P), ("kvm", KV), ("iota", 16), ("pidx", 1),
                  ("half_pi", 1), ("eps", 1)):
    C[_name] = (sum(n for _, n in C.values()), _n)
NCONST = sum(n for _, n in C.values())
G_MIX, G_X, G_MEM, G_FFN, G_ATT, G_SSM, D_SKIP, NGAIN = 0, 16, 32, 48, 64, 72, 80, 88


def constants():
    c = np.zeros((P, NCONST), np.float32)

    def put(name, value):
        a, n = C[name]
        c[: value.shape[0], a:a + n] = value

    p = np.arange(P)
    put("ident", np.eye(P))
    put("ones", np.ones((P, P)))
    for b, name in enumerate(("d0", "d1")):
        n = C[name][1]
        dist = (b * P + p)[:, None] - np.arange(n)[None]
        put(name, np.where(dist >= 0, -dist, NEG))
    n = np.arange(16)
    dist = np.stack([(b * P + p)[:, None] - (n * STRIDE + CMP - 1)[None] for b in range(QB)], 1)
    seen = (dist >= 0) & (n < NC)
    order = [4 * (2 * hp + hh) + g for hp in range(2) for g in range(GQ) for hh in range(2)]
    by_head = np.stack([np.where(seen, -dist * (SLOPE[h] / SCALE), NEG) for h in order], 2)
    put("cb", by_head.reshape(P, -1))
    put("mc", seen.reshape(P, -1))
    slope = np.array([SLOPE[i % HEADS] for i in range(P)])[:, None] / SCALE
    put("ds", -slope * (PAST - np.arange(PAST + 1))[None])
    put("dcs", -slope * (PAST - np.arange(NC) * STRIDE - CMP + 1)[None])
    put("t", np.tile(np.arange(TP), (P, 1)))
    put("sel", (p[None] // 16 == np.arange(TS)[:, None]))
    put("selT", (p[:, None] // 16 == np.arange(TS)[None]))
    put("kmask", (p[:, None] % 16 == np.arange(16)[None]))
    put("selk", (p[None] % 16 == n[:, None]))
    put("kvm", (p[:, None] % 16 // 4 == np.arange(KV)[None]))
    put("iota", np.tile(np.arange(16), (P, 1)))
    put("pidx", p[:, None])
    put("half_pi", np.full((P, 1), np.pi / 2))
    put("eps", np.full((P, 1), EPS))
    return c


INS = {
    "consts": (P, NCONST), "gains": (P, NGAIN), "x_t": (P, KT, NT), "mem_t": (P, KT, TP),
    "w_z": (NZ, P, KT * P), "w_gate": (P, KT * 48), "w_xk": (KT, P, D), "w_xv": (KT, P, D), "w_glu": (8, P, 8 * P),
    "w_out": (KT, P, D), "w_xq": (KT, P, D), "w_xo": (KT, P, D), "w_pq": (KT, P, D),
    "s5_par": (P, 3, ST), "s5_b": (P, 2, ST * 32), "s5_c": (P, 2, ST * 32), "s5_h0": (P, 2, ST * TS),
    "w_cmp": (P, 2, 2, CMP), "page": (16,),
    "pool_kc": (2560, 256), "pool_vc": (2560, 256), "pool_ks": (2560, 256), "pool_vs": (2560, 256),
    "win_k": (TS, P, 512), "win_v": (TS, P, 512), "mem_k": (TS, 2, P, D), "mem_v": (TS, 2, P, D),
    "keys": (P, 2, PK), "peer_u": (16384, D), "peer_v": (16384, D), "g_ffn": (D,), "g_final": (D,),
    "buf_k": (TS, 256 * 256), "buf_v": (TS, 256 * 256),
}
OUTS = {
    "y_p": (TP, D), "y_s": (TS, D), "z_kv": (12, P, NT), "s5_p": (P, 2 * ST), "s5_s": (P, 2 * ST * TS),
    "m_k": (KT, P, TP), "m_v": (QB, P, D), "new_k": (TS, 257 * 256), "new_v": (TS, 257 * 256),
}


class Counted:

    def __init__(self, eng, sem, loop=0):
        self.eng, self.sem, self.n, self.loop = eng, sem, 0, loop

    def __call__(self, ins):
        ins.then_inc(self.sem, 1)
        self.n += 1
        return self.n

    def wait(self, n=None):
        self.eng.wait_ge(self.sem, self.loop + (self.n if n is None else n))


def build(nc, A):
    with ExitStack() as ctx:
        def sb(name, n, dt=F32):
            return ctx.enter_context(nc.sbuf_tensor("sb_" + name, [P, n], dt))

        sems = {}

        def S(name):
            if name not in sems:
                sems[name] = ctx.enter_context(nc.semaphore("s_" + name))
            return sems[name]

        bank = [ctx.enter_context(nc.psum_tensor(f"bank{i}", [P, 512], F32)) for i in range(8)]

        con = sb("con", NCONST)
        gain = sb("gain", NGAIN)
        h_t = sb("h_t", KT * NT)
        x_t = sb("x_t", 19 * 256)
        m_t = sb("m_t", KT * TP)
        y_t = sb("y_t", KT * NT)
        z_t = sb("z_t", NZ * NT)
        gate = sb("gate", NT)
        ring = sb("ring", 4 * D)
        mk_t = sb("mk_t", KT * TP)
        mv_n = sb("mv_n", QB * D)
        b_st = sb("b_st", 2 * 8 * P)
        c_st = sb("c_st", 2 * ST * 32)
        par = sb("par", 3 * ST)
        prm = sb("prm", 26 * ST)
        s5s = sb("s5s", 8 * ST * TS)
        s5p = sb("s5p", 2 * ST)
        wcmp = sb("wcmp", 2 * 2 * CMP)
        rst = sb("rst", 2 * NT)
        gn = sb("gn", 208)
        small = sb("small", 160)
        idx_i = sb("idx_i", 16, I32)

        def cc(name, lo=0, n=None, rows=P):
            a, w = C[name]
            return con[0:rows, a + lo:a + lo + (w - lo if n is None else n)]

        ident = cc("ident")
        H = h_t[:, :].rearrange("p (t n) -> p t n", n=NT)
        X = x_t[:, 0:KT * NT].rearrange("p (t n) -> p t n", n=NT)
        M = m_t[:, :].rearrange("p (t n) -> p t n", n=TP)
        Y = y_t[:, :].rearrange("p (t n) -> p t n", n=NT)
        Z = z_t[:, :].rearrange("p (t n) -> p t n", n=NT)
        R = ring[:, :].rearrange("p (s t n) -> p s t n", s=4, n=P)
        MK = mk_t[:, :].rearrange("p (t n) -> p t n", n=TP)
        MV = mv_n[:, :].rearrange("p (b n) -> p b n", b=QB)

        segs = [("z", NZ), ("gate", 1), ("xk", 16), ("xv", 16), ("glu", 8), ("dk", 8), ("dv", 8), ("out", 16),
                ("xq", 16), ("mk", 16), ("mv", 16), ("xo", 16), ("pq", 16)]
        nd = {"dk": 7, "dv": 3}
        full, start, at, fill = {}, {}, 0, {}
        users = []
        tiles_before, tiles = {}, 0
        for seg, n in segs:
            start[seg] = at
            gemm = seg not in ("dk", "dv", "mk", "mv")
            tiles_before[seg] = tiles
            for j in range(n):
                s = at % 4
                by = ("cache" if seg in nd else "full") + str(s)
                fill[by] = fill.get(by, 0) + 16 * nd.get(seg, 1)
                full[seg, j] = (s, by, fill[by])
                last = j | 1 if seg == "xv" else j
                users.append(("tile", tiles + last + 1) if gemm else (seg + "_used", j + 1))
                at += 1
            tiles += n if gemm else 0
            if seg == "gate":
                at += 3
                users += [None] * 3

        def arrived(eng, seg, j):
            s, by, v = full[seg, j]
            eng.wait_ge(S(by), v)
            return s

        def free(eng, g):
            while g >= 4:
                g -= 4
                if users[g] is not None:
                    eng.wait_ge(S(users[g][0]), users[g][1])
                    return

        block = ctx.enter_context(nc.Block())

        def sp_stream(sp):
            sp.dma_start(h_t[:, :], A["x_t"].rearrange("p t n -> p (t n)")).then_inc(S("ld_x"), 16)
            sp.dma_start(con[:, :], A["consts"]).then_inc(S("ld_c"), 16)
            sp.dma_start(gain[:, :], A["gains"]).then_inc(S("ld_g"), 16)

            def stream(seg, src, cols=D):
                n = dict(segs)[seg]
                s0 = start[seg]

                def load(j, k):
                    sp.dma_start(ring[:, k * D:k * D + cols], src(j)).then_inc(S(f"full{k}"), 16)

                for j in range(min(4, n)):
                    free(sp, s0 + j)
                    load(j, (s0 + j) % 4)
                if n > 4:
                    with sp.Fori(1, n // 4) as i:
                        for k in range(4):
                            last = k | 1 if seg == "xv" else k
                            if seg in ("mk", "mv"):
                                sp.wait_ge(S(seg + "_used"), i * 4 + (k - 3))
                            else:
                                sp.wait_ge(S("tile"), i * 4 + (tiles_before[seg] + last - 3))
                            load(i * 4 + k, k)

            def tiles_of(w):
                return lambda j: w[bass.ds(j, 1)].rearrange("a p n -> (a p) n")

            stream("z", tiles_of(A["w_z"]))
            stream("gate", lambda j: A["w_gate"], KT * 48)
            stream("xk", tiles_of(A["w_xk"]))
            stream("xv", tiles_of(A["w_xv"]))
            stream("glu", tiles_of(A["w_glu"]), 8 * P)
            stream("out", tiles_of(A["w_out"]))
            stream("xq", tiles_of(A["w_xq"]))
            stream("mk", lambda j: A["mem_k"].rearrange("b c p n -> (b c) p n")[bass.ds(j, 1)].rearrange("a p n -> (a p) n"))
            stream("mv", lambda j: A["mem_v"].rearrange("b c p n -> (b c) p n")[bass.ds(j, 1)].rearrange("a p n -> (a p) n"))
            stream("xo", tiles_of(A["w_xo"]))
            stream("pq", tiles_of(A["w_pq"]))

        def act_norm(act, tag, src, sq, t, width, bk=7):
            for k in range(4):
                a, b = k * t // 4, (k + 1) * t // 4
                act.activation(sq[:, a:b, :], src[:, a:b, :], ACT.Square).then_inc(S(tag + "_sq"), 1)
            act.wait_ge(S(tag + "_sum"), 1)
            act.activation(rst[:, 0:src.shape[2]], bank[bk][:, 0:src.shape[2]], ACT.Sqrt, bias=cc("eps"),
                           scale=1.0 / width).then_inc(S(tag + "_rms"), 1)

        def pe_norm(pe, tag, sq, t, bk=7):
            n = sq.shape[2]
            for k in range(t):
                if k % (t // 4) == 0:
                    pe.wait_ge(S(tag + "_sq"), k // (t // 4) + 1)
                last = pe.matmul(bank[bk][:, 0:n], lhsT=cc("ones"), rhs=sq[:, k, :], start=(k == 0), stop=(k == t - 1))
            last.then_inc(S(tag + "_sum"), 1)

        def dve_norm(dve, tag, dst, src, t, g0):
            n = src.shape[2]
            dve.wait_ge(S(tag + "_rms"), 1)
            dve.reciprocal(rst[:, NT:NT + n], rst[:, 0:n]).then_inc(S(tag + "_x"), 1)
            dve.wait_ge(S(tag + "_x"), 1)
            for k in range(t):
                dve.scalar_tensor_tensor(out=dst[:, k, :], in0=src[:, k, :], scalar=gain[:, g0 + k:g0 + k + 1],
                                         in1=rst[:, NT:NT + n], op0=ALU.mult, op1=ALU.mult).then_inc(S(tag + "_x"), 1)

        SQ = Y
        MSQ, MSUM = y_t[:, 2048:2048 + TP], y_t[:, 2304:2304 + TP]

        def dve_mem_squares(dve):
            do = Counted(dve, S("mem_acc"))
            dve.wait_ge(S("ld_m"), 16)
            do(dve.tensor_tensor(MSUM, M[:, 0, :], M[:, 0, :], ALU.mult))
            for t in range(1, KT):
                if t > 1:
                    do.wait()
                do(dve.tensor_tensor(MSQ, M[:, t, :], M[:, t, :], ALU.mult))
                do.wait()
                do(dve.tensor_tensor(MSUM, MSUM, MSQ, ALU.add))
            assert do.n == 2 * KT - 1

        def pe_gemm(pe, seg, src, kts, first=False, ready=None, between=None):
            n, base = dict(segs)[seg], tiles_before[seg]

            def four(i, waits, ready=None):
                for k in range(4):
                    s, by, v = full[seg, k]
                    pe.wait_ge(S(by), i * 16 + v)
                    if waits:
                        pe.wait_ge(S("evac"), i * 4 + (base + k - 3))
                    for t in range(kts):
                        if ready and k == 0:
                            pe.wait_ge(S(ready + "_x"), t + 2)
                        mm = pe.matmul(bank[k][:, 0:src.shape[2]], lhsT=R[:, s, t, :], rhs=src[:, t, :],
                                       start=(t == 0), stop=(t == kts - 1))
                    mm.then_inc(S("tile"), 1)

            if not first:
                pe.wait_ge(S("evac"), base)
            four(0, False, ready)
            if between:
                between()
            with pe.Fori(1, n // 4) as i:
                four(i, True)

        def copy_gemm(act, seg, dst, func=ACT.Copy, between=None):
            n, base = dict(segs)[seg], tiles_before[seg]
            if between:
                for k in range(4):
                    act.wait_ge(S("tile"), base + k + 1)
                    act.activation(dst[:, k, :], bank[k][:, 0:dst.shape[2]], func).then_inc(S("evac"), 1)
                between()
            with act.Fori(1 if between else 0, n // 4) as i:
                for k in range(4):
                    act.wait_ge(S("tile"), i * 4 + (base + k + 1))
                    act.activation(dst[:, bass.ds(i * 4 + k, 1), :].rearrange("p a n -> p (a n)"),
                                   bank[k][:, 0:dst.shape[2]], func).then_inc(S("evac"), 1)

        SQT = [x_t[:, k * NT:(k + 1) * NT] for k in range(2)]
        SUM = x_t[:, 2 * NT:3 * NT]

        def add_gemm(dve, seg, tag):
            n, base = dict(segs)[seg], tiles_before[seg]
            dve.memset(SUM, 0.0).then_inc(S(tag + "_acc"), 1)
            with dve.Fori(0, n // 4) as i:
                for k in range(4):
                    at_ = H[:, bass.ds(i * 4 + k, 1), :].rearrange("p a n -> p (a n)")
                    dve.wait_ge(S("tile"), i * 4 + (base + k + 1))
                    dve.tensor_tensor(at_, at_, bank[k][:, 0:NT], ALU.add).then_inc(S("evac"), 1)
                    dve.wait_ge(S(tag + "_sq"), i * 4 + (k + 1))
                    dve.wait_ge(S(tag + "_acc"), i * 4 + (k + 1))
                    dve.tensor_tensor(SUM, SUM, SQT[k % 2], ALU.add).then_inc(S(tag + "_acc"), 1)

        def act_squares(act, seg, tag):
            n, base = dict(segs)[seg], tiles_before[seg]
            with act.Fori(0, n // 4) as i:
                for k in range(4):
                    act.wait_ge(S("evac"), i * 4 + (base + k + 1))
                    act.activation(SQT[k % 2], H[:, bass.ds(i * 4 + k, 1), :].rearrange("p a n -> p (a n)"), ACT.Square)\
                        .then_inc(S(tag + "_sq"), 1)
            act_root(act, tag, NT, D)

        def act_root(act, tag, n, width):
            act.wait_ge(S(tag + "_sum"), 1)
            act.activation(rst[:, 0:n], bank[7][:, 0:n], ACT.Sqrt, bias=cc("eps"), scale=1.0 / width)\
                .then_inc(S(tag + "_rms"), 1)

        def pe_sum(pe, tag, squares, count):
            pe.wait_ge(S(tag + "_acc"), count)
            pe.matmul(bank[7][:, 0:squares.shape[1]], lhsT=cc("ones"), rhs=squares, start=True, stop=True)\
                .then_inc(S(tag + "_sum"), 1)

        def W(i):
            return x_t[:, i * 256:(i + 1) * 256]

        COS, SIN = (W(0), W(1)), (W(2), W(3))
        ROUND, PROD, FRAC, ABS = W(4), W(5), W(6), W(7)
        M1, M2, M3, M4, GR, GI, N1 = (W(8 + i) for i in range(7))
        HR, HI = (W(15), W(16)), (W(17), W(18))

        def pr(i):
            return prm[:, i * ST:(i + 1) * ST]

        BRAW = mk_t[:, 0:D].rearrange("p (c j n) -> p c j n", c=2, n=32)
        BBAR = mk_t[:, D:2 * D].rearrange("p (c j n) -> p c j n", c=2, n=32)
        BT = b_st[:, :].rearrange("p (c t n) -> p c t n", c=2, n=P)
        CT = c_st[:, :].rearrange("p (c j n) -> p c j n", c=2, n=32)
        H0 = s5s[:, 0:2 * ST * TS].rearrange("p (c j b) -> p c j b", c=2, b=TS)
        BU = s5s[:, 2 * ST * TS:4 * ST * TS].rearrange("p (c j b) -> p c j b", c=2, b=TS)
        HS = s5s[:, 4 * ST * TS:6 * ST * TS].rearrange("p (c j b) -> p c j b", c=2, b=TS)
        TMP = s5s[:, 6 * ST * TS:8 * ST * TS].rearrange("p (c j b) -> p c j b", c=2, b=TS)

        def dve_s5_parameters(dve):
            lr, li = par[:, 0:ST], par[:, ST:2 * ST]
            do = Counted(dve, S("par_dve"))
            dve.wait_ge(S("ld_s5"), 16 * 4)
            dve.wait_ge(S("par_act"), 1)
            do(dve.tensor_tensor(pr(1), lr, pr(0), ALU.mult))
            do(dve.tensor_tensor(pr(2), li, pr(0), ALU.mult))
            do.wait()
            do(dve.tensor_scalar(pr(4), pr(2), 1 / (2 * np.pi), MAGIC, ALU.mult, ALU.add))
            do.wait()
            do(dve.tensor_scalar(pr(4), pr(4), MAGIC, None, ALU.subtract))
            do.wait()
            do(dve.scalar_tensor_tensor(out=pr(5), in0=pr(2), scalar=1 / (2 * np.pi), in1=pr(4),
                                        op0=ALU.mult, op1=ALU.subtract))
            dve.wait_ge(S("par_act"), 5)
            do(dve.tensor_tensor(pr(9), pr(3), pr(8), ALU.mult))
            do(dve.tensor_tensor(pr(10), pr(3), pr(7), ALU.mult))
            do(dve.tensor_tensor(pr(14), lr, lr, ALU.mult))
            do(dve.tensor_tensor(pr(15), li, li, ALU.mult))
            do.wait()
            do(dve.tensor_scalar(pr(11), pr(9), 1.0, None, ALU.subtract))
            do(dve.tensor_tensor(pr(14), pr(14), pr(15), ALU.add))
            do.wait()
            do(dve.reciprocal(pr(15), pr(14)))
            do(dve.tensor_tensor(pr(12), pr(11), lr, ALU.mult))
            do(dve.tensor_tensor(pr(13), pr(10), li, ALU.mult))
            do(dve.tensor_tensor(pr(18), pr(10), lr, ALU.mult))
            do(dve.tensor_tensor(pr(19), pr(11), li, ALU.mult))
            do.wait()
            do(dve.tensor_tensor(pr(12), pr(12), pr(13), ALU.add))
            do(dve.tensor_tensor(pr(18), pr(18), pr(19), ALU.subtract))
            do.wait()
            do(dve.tensor_tensor(pr(16), pr(12), pr(15), ALU.mult))
            do(dve.tensor_tensor(pr(17), pr(18), pr(15), ALU.mult))
            do(dve.tensor_scalar(c_st[:, 1024:2048], c_st[:, 1024:2048], -1.0, None, ALU.mult))
            do.wait()
            fr = pr(16).unsqueeze(2).to_broadcast([P, ST, 32])
            fi = pr(17).unsqueeze(2).to_broadcast([P, ST, 32])
            t1 = y_t[:, 0:1024].rearrange("p (j n) -> p j n", n=32)
            t2 = y_t[:, 1024:2048].rearrange("p (j n) -> p j n", n=32)
            for part, (f1, f2, op) in enumerate(((fr, fi, ALU.subtract), (fi, fr, ALU.add))):
                if part:
                    do.wait()
                do(dve.tensor_tensor(t1, BRAW[:, 0], f1, ALU.mult))
                do(dve.tensor_tensor(t2, BRAW[:, 1], f2, ALU.mult))
                do.wait()
                do(dve.tensor_tensor(BBAR[:, part], t1, t2, op))
            return do.n

        def act_s5_parameters(act):
            act.wait_ge(S("ld_s5"), 16 * 4)
            act.activation(pr(0), par[:, 2 * ST:3 * ST], ACT.Exp).then_inc(S("par_act"), 1)
            act.wait_ge(S("par_dve"), 1)
            act.activation(pr(3), pr(1), ACT.Exp).then_inc(S("par_act"), 1)
            act.wait_ge(S("par_dve"), 5)
            act.activation(pr(6), pr(5), ACT.Abs).then_inc(S("par_act"), 1)
            act.activation(pr(7), pr(5), ACT.Sin, scale=TWO_PI).then_inc(S("par_act"), 1)
            act.wait_ge(S("par_act"), 3)
            act.activation(pr(8), pr(6), ACT.Sin, scale=-TWO_PI, bias=cc("half_pi")).then_inc(S("par_act"), 1)

        PAR_DONE = 27

        def pe_b_transposes(pe):
            pe.wait_ge(S("par_dve"), PAR_DONE)
            for n in range(16):
                b = bank[4 + n // 4]
                tr = pe.transpose(b[:, (n % 4) * P:(n % 4 + 1) * P],
                                  mk_t[:, D + n * P:D + (n + 1) * P], ident)
                if n % 4 == 3:
                    tr.then_inc(S("b_turned"), 1)

        def act_b_transposes(act):
            for n in range(4):
                act.wait_ge(S("b_turned"), n + 1)
                act.activation(b_st[:, n * 512:(n + 1) * 512], bank[4 + n][:, :], ACT.Copy).then_inc(S("b_kept"), 1)

        DV, PO, AC = 13, 9, 3
        BANKS_READ, WR, GR_AT, ROT, HR_AT = 6, 8, 10, 12, 13

        def pool_s5_table(pool, j):
            f = pr(5)[:, j:j + 1]
            base = j * PO
            if j >= 1:
                pool.wait_ge(S("s5_act"), AC * j)
                pool.wait_ge(S("s5_tab"), 4 * j)
            pool.tensor_scalar(ROUND, cc("t"), f, MAGIC, ALU.mult, ALU.add).then_inc(S("s5_tab"), 1)
            pool.tensor_scalar(PROD, cc("t"), f, None, ALU.mult).then_inc(S("s5_tab"), 1)
            pool.wait_ge(S("s5_tab"), 4 * j + 2)
            pool.tensor_scalar(ROUND, ROUND, MAGIC, None, ALU.subtract).then_inc(S("s5_tab"), 1)
            pool.wait_ge(S("s5_tab"), 4 * j + 3)
            pool.tensor_tensor(FRAC, PROD, ROUND, ALU.subtract).then_inc(S("s5_tab"), 1)

        def act_s5_table(act, j):
            act.wait_ge(S("s5_tab"), 4 * j + 4)
            if j >= 2:
                act.wait_ge(S("s5_dve"), DV * (j - 2) + ROT)
                act.wait_ge(S("s5_im"), 5 * (j - 2) + 2)
            if j >= 1:
                act.wait_ge(S("s5_act"), AC * j)
            act.activation(ABS, FRAC, ACT.Abs).then_inc(S("s5_act"), 1)
            act.activation(SIN[j % 2], FRAC, ACT.Sin, scale=TWO_PI).then_inc(S("s5_act"), 1)
            act.wait_ge(S("s5_act"), AC * j + 1)
            act.activation(COS[j % 2], ABS, ACT.Sin, scale=-TWO_PI, bias=cc("half_pi")).then_inc(S("s5_act"), 1)

        def pe_s5_input(pe, j):
            jj, q = j % 4, j // 4
            if j >= 1:
                pe.wait_ge(S("s5_dve"), DV * (j - 1) + BANKS_READ)
            for part in range(2):
                mm = pe.matmul(bank[4 + part][:, 0:NT], lhsT=BT[32 * jj:32 * jj + 32, part, q, :],
                               rhs=Z[32 * jj:32 * jj + 32, U0 + q, :], start=True, stop=True, tile_position=(32 * jj, 0))
            mm.then_inc(S("s5_bu"), 1)

        def dve_s5(dve, j):
            do = Counted(dve, S("s5_dve"), DV * j)
            c, s = COS[j % 2], SIN[j % 2]
            br, bi = bank[4][:, 0:TP], bank[5][:, 0:TP]
            dve.wait_ge(S("s5_bu"), j + 1)
            dve.wait_ge(S("s5_act"), AC * (j + 1))
            if j >= 1:
                do.wait(0)
            do(dve.tensor_tensor(M1, c, br, ALU.mult))
            do(dve.tensor_tensor(M2, s, bi, ALU.mult))
            do(dve.tensor_tensor(M3, c, bi, ALU.mult))
            do(dve.tensor_tensor(M4, s, br, ALU.mult))
            do(dve.tensor_copy(BU[:, 0, j, :], bank[4][:, TP:NT]))
            do(dve.tensor_copy(BU[:, 1, j, :], bank[5][:, TP:NT]))
            do.wait(4)
            do(dve.tensor_tensor(M1, M1, M2, ALU.add))
            do(dve.tensor_tensor(M3, M3, M4, ALU.subtract))
            if j >= 1:
                dve.wait_ge(S("s5_im"), 5 * (j - 1) + 2)
            do.wait(7)
            r = pr(3)[:, j:j + 1].to_broadcast([P, TP])
            do(dve.tensor_tensor_scan(GR, r, M1, 0.0, ALU.mult, ALU.add))
            do.wait(8)
            do(dve.tensor_tensor_scan(GI, r, M3, 0.0, ALU.mult, ALU.add))
            do.wait(9)
            do(dve.tensor_tensor(M2, c, GR, ALU.mult))
            do.wait(10)
            do(dve.tensor_tensor(M4, s, GI, ALU.mult))
            if j >= 2:
                dve.wait_ge(S("s5_c"), j - 1)
                dve.wait_ge(S("s5_im"), 5 * (j - 2) + 5)
            do.wait(12)
            do(dve.tensor_tensor(HR[j % 2], M2, M4, ALU.subtract))

        def pool_s5(pool, j):
            do = Counted(pool, S("s5_im"), 5 * j)
            c, s = COS[j % 2], SIN[j % 2]
            pool.wait_ge(S("s5_dve"), DV * j + GR_AT)
            if j >= 1:
                do.wait(0)
            if j >= 2:
                pool.wait_ge(S("s5_c"), j - 1)
            do(pool.tensor_tensor(N1, s, GR, ALU.mult))
            do(pool.tensor_tensor(HI[j % 2], c, GI, ALU.mult))
            do.wait()
            do(pool.tensor_tensor(HI[j % 2], N1, HI[j % 2], ALU.add))
            do.wait()
            do(pool.tensor_copy(s5p[:, ST + j:ST + j + 1], HI[j % 2][:, TP - 1:TP]))
            pool.wait_ge(S("s5_dve"), DV * j + HR_AT)
            do(pool.tensor_copy(s5p[:, j:j + 1], HR[j % 2][:, TP - 1:TP]))

        def pe_s5_output(pe, j):
            jj, q = j % 4, j // 4
            pe.wait_ge(S("s5_dve"), DV * j + HR_AT)
            pe.wait_ge(S("s5_im"), 5 * j + 3)
            if jj == 0 and q >= 1:
                pe.wait_ge(S("s5_y"), q)
            for part, h in enumerate((HR, HI)):
                mm = pe.matmul(bank[6][32 * jj:32 * jj + 32, 0:TP], lhsT=CT[:, part, j, :], rhs=h[j % 2],
                               start=(part == 0), stop=(part == 1), tile_position=(0, 32 * jj))
            mm.then_inc(S("s5_c"), 1)

        def dve_s5_skip(dve, q):
            dve.wait_ge(S("s5_c"), 4 * q + 4)
            dve.scalar_tensor_tensor(out=Y[:, 8 + q, 0:TP], in0=Z[:, U0 + q, 0:TP],
                                     scalar=gain[:, D_SKIP + q:D_SKIP + q + 1], in1=bank[6][:, 0:TP],
                                     op0=ALU.mult, op1=ALU.add).then_inc(S("s5_y"), 1)

        def dve_s5_samples(dve):
            do = Counted(dve, S("s5_smp"))
            ar = pr(9).unsqueeze(2).to_broadcast([P, ST, TS])
            ai = pr(10).unsqueeze(2).to_broadcast([P, ST, TS])
            dve.wait_ge(S("s5_dve"), DV * ST)
            for part, (x, y, op) in enumerate(((ar, ai, ALU.subtract), (ai, ar, ALU.add))):
                if part:
                    do.wait()
                do(dve.tensor_tensor(TMP[:, 0], H0[:, 0], x, ALU.mult))
                do(dve.tensor_tensor(TMP[:, 1], H0[:, 1], y, ALU.mult))
                do.wait()
                do(dve.tensor_tensor(HS[:, part], TMP[:, 0], TMP[:, 1], op))
                do.wait()
                do(dve.tensor_tensor(HS[:, part], HS[:, part], BU[:, part], ALU.add))
            ds = gain[:, D_SKIP:D_SKIP + 8].unsqueeze(2).to_broadcast([P, 8, TS])
            do(dve.tensor_tensor(Y[:, 8:16, TP:NT], Z[:, U0:NZ, TP:NT], ds, ALU.mult))
            do.wait()
            dve.wait_ge(S("s5_cs"), 1)
            do(dve.tensor_tensor(Y[:, 8:16, TP:NT], Y[:, 8:16, TP:NT],
                                 bank[6][:, 0:8 * TS].rearrange("p (q b) -> p q b", b=TS), ALU.add))

        def pe_s5_samples(pe):
            pe.wait_ge(S("s5_y"), 8)
            pe.wait_ge(S("s5_smp"), 8)
            for j in range(ST):
                jj, q = j % 4, j // 4
                for part in range(2):
                    mm = pe.matmul(bank[6][32 * jj:32 * jj + 32, q * TS:(q + 1) * TS], lhsT=CT[:, part, j, :],
                                   rhs=HS[:, part, j, :], start=(part == 0), stop=(part == 1),
                                   tile_position=(0, 32 * jj))
            mm.then_inc(S("s5_cs"), 1)

        def pe_mem_tile(pe, n):
            base = tiles_before["xk"]
            pe.wait_ge(S("evac"), base + n - 3)
            if n < 16:
                s = arrived(pe, "xk", n)
                for t in range(KT):
                    mm = pe.matmul(bank[n % 4][:, 0:TP], lhsT=R[:, s, t, :], rhs=M[:, t, :],
                                   start=(t == 0), stop=(t == KT - 1))
            else:
                pair, b = (n - 16) // 2, n % 2
                s = arrived(pe, "xv", 2 * pair)
                arrived(pe, "xv", 2 * pair + 1)
                for t in range(KT):
                    mm = pe.matmul(bank[n % 4][:, 0:TP], lhsT=M[:, t, b * P:(b + 1) * P], rhs=R[:, s:s + 2, t, :],
                                   start=(t == 0), stop=(t == KT - 1))
            mm.then_inc(S("tile"), 1)

        def act_mem_tile(act, n):
            act.wait_ge(S("tile"), tiles_before["xk"] + n + 1)
            dst = MK[:, n, :] if n < 16 else MV[:, n % 2, (n - 16) // 2 * TP:((n - 16) // 2 + 1) * TP]
            act.activation(dst, bank[n % 4][:, 0:TP], ACT.Copy).then_inc(S("evac"), 1)

        def pe_front(pe):
            pe.wait_ge(S("ld_c"), 16)
            pe_norm(pe, "mix", SQ, KT)

            def between():
                pe_b_transposes(pe)
                pe.wait_ge(S("b_kept"), 4)
                pe_sum(pe, "mem", MSUM, 2 * KT - 1)

            pe_gemm(pe, "z", X, KT, first=True, ready="mix", between=between)
            pe.wait_ge(S("evac"), NZ)
            s = arrived(pe, "gate", 0)
            for t in range(KT):
                mm = pe.matmul(bank[3][0:48, 0:NT], lhsT=ring[:, s * D + t * 48:s * D + (t + 1) * 48], rhs=X[:, t, :],
                               start=(t == 0), stop=(t == KT - 1))
            mm.then_inc(S("tile"), 1)
            pe.wait_ge(S("mem_x"), KT + 1)
            for j in range(ST):
                pe_s5_input(pe, j)
                pe_mem_tile(pe, j)
                if j >= 1:
                    pe_s5_output(pe, j - 1)
            pe_s5_output(pe, ST - 1)
            pe_s5_samples(pe)
            pe.wait_ge(S("y_gelu"), 1)
            pe_gemm(pe, "glu", Y[:, 8:16, :], 8)

        def act_front(act):
            act.wait_ge(S("ld_x"), 16)
            act.wait_ge(S("ld_c"), 16)
            act_norm(act, "mix", H, SQ, KT, D)
            act_s5_parameters(act)

            def between():
                act_b_transposes(act)
                act_root(act, "mem", TP, D)

            copy_gemm(act, "z", Z, between=between)
            act.wait_ge(S("tile"), NZ + 1)
            act.activation(gate[0:48, :], bank[3][0:48, 0:NT], ACT.Sigmoid).then_inc(S("evac"), 1)
            for j in range(ST):
                act_s5_table(act, j)
                if j >= 1:
                    act_mem_tile(act, j - 1)
            act_mem_tile(act, ST - 1)
            act.wait_ge(S("s5_y"), 8)
            act.wait_ge(S("s5_smp"), 10)
            act.activation(Y[:, 8:16, :], Y[:, 8:16, :], ACT.Gelu_apprx_tanh).then_inc(S("y_gelu"), 1)
            copy_gemm(act, "glu", X, ACT.Sigmoid)

        def dve_front(dve):
            dve.wait_ge(S("ld_g"), 16)
            dve_norm(dve, "mix", X, H, KT, G_MIX)
            assert dve_s5_parameters(dve) == PAR_DONE
            dve_mem_squares(dve)
            dve_norm(dve, "mem", M, M, KT, G_MEM)
            dve.wait_ge(S("tile"), NZ + 1)
            for j in range(ST):
                dve_s5(dve, j)
                if j >= 5 and j % 4 == 1:
                    dve_s5_skip(dve, j // 4 - 1)
            dve_s5_skip(dve, 7)
            dve_s5_samples(dve)
            dve.wait_ge(S("evac"), tiles_before["glu"] + 8)
            dve.tensor_tensor(Y[:, 8:16, :], Y[:, 8:16, :], X[:, 0:8, :], ALU.mult).then_inc(S("o_ssm"), 1)

        def pool_front(pool):
            pool.dma_start(par[:, :], A["s5_par"].rearrange("p c j -> p (c j)")).then_inc(S("ld_s5"), 16)
            pool.dma_start(mk_t[:, 0:D], A["s5_b"].rearrange("p c n -> p (c n)")).then_inc(S("ld_s5"), 16)
            pool.dma_start(c_st[:, :], A["s5_c"].rearrange("p c n -> p (c n)")).then_inc(S("ld_s5"), 16)
            pool.dma_start(s5s[:, 0:2 * ST * TS], A["s5_h0"].rearrange("p c n -> p (c n)")).then_inc(S("ld_s5"), 16)
            pool.dma_start(m_t[:, :], A["mem_t"].rearrange("p t n -> p (t n)")).then_inc(S("ld_m"), 16)
            pool.dma_start(wcmp[:, :], A["w_cmp"].rearrange("p a b c -> p (a b c)")).then_inc(S("ld_w"), 16)
            pool.dma_start(idx_i[:, :], A["page"].partition_broadcast(P)).then_inc(S("ld_w"), 16)
            for name, src in (("new_k", "buf_k"), ("new_v", "buf_v")):
                pool.dma_start(A[name][:, 0:256 * 256], A[src]).then_inc(S("stored"), 16)
            pool.wait_ge(S("par_dve"), 5)
            pool.wait_ge(S("ld_c"), 16)
            pool.wait_ge(S("tile"), NZ + 1)
            for n in range(ST + 1):
                if n < ST:
                    pool_s5_table(pool, n)
                if n == 1:
                    pool.dma_start(A["z_kv"].rearrange("t p n -> p t n"), Z[:, K_CMP:U0, :]).then_inc(S("z_stored"), 16)
                if n >= 1:
                    pool_s5(pool, n - 1)
            pool.wait_ge(S("s5_im"), 5 * ST)
            pool.dma_start(A["s5_p"], s5p[:, :]).then_inc(S("stored"), 16)
            pool.wait_ge(S("s5_smp"), 8)
            pool.dma_start(A["s5_s"], s5s[:, 4 * ST * TS:6 * ST * TS]).then_inc(S("stored"), 16)
            pool.wait_ge(S("evac"), tiles_before["glu"])
            pool.dma_start(A["m_k"].rearrange("t p n -> p t n"), MK).then_inc(S("m_stored"), 16)
            pool.dma_start(A["m_v"].rearrange("b p n -> p b n"), MV).then_inc(S("m_stored"), 16)

        VN = c_st[:, 0:1024].rearrange("p (b n) -> p b n", b=QB)
        CVN = c_st[0:NC, 1024:1280]
        CK = c_st[:, 1280:1280 + 4 * NC].rearrange("p (t n) -> p t n", n=NC)
        HALVES = c_st[:, 1344:1472]
        CKZ = c_st[:, 1472:1536].rearrange("p (h e n) -> p h e n", h=2, e=2)
        CVZ = x_t[:, 0:1024].rearrange("p (h g e d) -> p h g e d", h=2, g=GQ, e=2)
        CW = [x_t[:, 1056 + b * 256:1312 + b * 256] for b in range(QB)]
        CPT = [x_t[:, 1568 + b * 256:1824 + b * 256] for b in range(QB)]
        WC = wcmp[:, :].rearrange("p (a b j) -> p a b j", a=2, b=2)

        def dve_compress(do, src, dst):
            prod = b_st[:, :].rearrange("p (t g c j) -> p t g c j", t=8, g=2, j=STRIDE)
            for t in range(4):
                for half in range(2):
                    w = WC[:, t // 2, t % 2, half * STRIDE:(half + 1) * STRIDE]
                    do(do.eng.tensor_tensor(prod[:, 2 * t + half], src(t // 2, t % 2),
                                            w.unsqueeze(1).unsqueeze(1).to_broadcast([P, 2, 8, STRIDE]), ALU.mult))
            do.wait()
            do(do.eng.tensor_reduce(HALVES, b_st[:, :].rearrange("p (n j) -> p n j", j=STRIDE), AXX, ALU.add))
            do.wait()
            hv = HALVES.rearrange("p (t h c) -> p t h c", t=4, h=2)
            return do(do.eng.tensor_tensor(dst, hv[:, :, 0, 0:NC], hv[:, :, 1, 1:NC + 1], ALU.add))

        COMPRESSED = 10

        NEW = x_t[0:TS, 2832:3600]
        GATE_S = gn[:, 192:195]

        def pe_by_token(pe):
            for b in range(QB):
                for n, t in enumerate((V_SEL, V_SEL + 1, V_WIN, V_WIN + 1)):
                    tr = pe.transpose(bank[4 + b][:, n * P:(n + 1) * P], Z[:, t, b * P:(b + 1) * P], ident)
                tr.then_inc(S("bt_pe"), 1)
            for b in range(QB):
                pe.transpose(bank[6][:, b * 48:(b + 1) * 48], gate[0:48, b * P:(b + 1) * P], ident[0:48, 0:48])
            pe.transpose(bank[6][0:TS, 96:144], gate[0:48, TP:NT], ident[0:48, 0:48]).then_inc(S("bt_pe"), 1)
            pe.wait_ge(S("evac"), tiles_before["out"])
            for n, t in enumerate((K_WIN, K_WIN + 1, V_SEL, V_SEL + 1, V_WIN, V_WIN + 1)):
                tr = pe.transpose(bank[n // 4][0:TS, n % 4 * P:(n % 4 + 1) * P], Z[:, t, TP:NT], ident)
            tr.then_inc(S("bt_pe"), 1)
            pe_norm(pe, "ssm", X[:, 0:8, :], 8, bk=3)
            pe.wait_ge(S("cmp_p"), COMPRESSED)
            for hp in range(2):
                tr = pe.transpose(bank[7][0:NC, hp * P:(hp + 1) * P], CK[:, 2 + hp, :], ident)
            tr.then_inc(S("bt_pe"), 1)
            pe.wait_ge(S("bt_act"), 4)
            pe.matmul(bank[6][:, 144:192], lhsT=cc("sel", rows=TS), rhs=gn[0:TS, 96:144], start=True, stop=True)\
                .then_inc(S("bt_pe"), 1)
            pe.wait_ge(S("bt_act"), 7)
            pe.wait_ge(S("gate_s"), 1)
            pe.matmul(bank[7][:, 0:256], lhsT=cc("selk", rows=NC), rhs=CVN, start=True, stop=True).then_inc(S("bt_pe"), 1)
            pe.wait_ge(S("ckz"), 5)
            for qb in range(QB):
                for t in range(8):
                    mm = pe.matmul(bank[5 + qb][:, t * 32:(t + 1) * 32], lhsT=Z[:, t, qb * P:(qb + 1) * P],
                                   rhs=CKZ[:, t // 4].rearrange("p e n -> p (e n)"), start=True, stop=True)
                mm.then_inc(S("c_s"), 1)

        def act_by_token(act):
            act.wait_ge(S("s5_cs"), 1)
            for b in range(QB):
                act.wait_ge(S("bt_pe"), b + 1)
                act.activation(VN[:, b, :], bank[4 + b][:, :], ACT.Copy).then_inc(S("bt_act"), 1)
            act.wait_ge(S("bt_pe"), 3)
            act.activation(gn[:, 0:96], bank[6][:, 0:96], ACT.Copy).then_inc(S("bt_act"), 1)
            act.activation(gn[0:TS, 96:144], bank[6][0:TS, 96:144], ACT.Copy).then_inc(S("bt_act"), 1)
            act.wait_ge(S("bt_pe"), 4)
            act.wait_ge(S("o_ssm"), 1)
            act.activation(NEW[:, 0:512], bank[0][0:TS, :], ACT.Copy).then_inc(S("bt_act"), 1)
            act.activation(NEW[:, 512:768], bank[1][0:TS, 0:256], ACT.Copy).then_inc(S("bt_act"), 1)
            act_norm(act, "ssm", Y[:, 8:16, :], X[:, 0:8, :], 8, 1024, bk=3)
            act.wait_ge(S("bt_pe"), 5)
            act.activation(CVN, bank[7][0:NC, 0:256], ACT.Copy).then_inc(S("bt_act"), 1)
            for qb in range(QB):
                act.wait_ge(S("c_d"), 9 * qb + 3)
                act.activation(CW[qb], CW[qb], ACT.Exp, scale=SCALE).then_inc(S("c_e"), 1)

        def dve_by_token(dve):
            dve.wait_ge(S("s5_cs"), 1)
            dve.wait_ge(S("ld_w"), 32)
            do = Counted(dve, S("cmp_p"))
            dve_compress(do, lambda kv, hp: Z[:, K_CMP + 2 * kv + hp, 0:TP].rearrange("p (g c j) -> p g c j", g=2, j=STRIDE), CK)
            dve.memset(c_st[:, 1472:1536], 0.0).then_inc(S("ckz"), 1)
            do.wait()
            dve.wait_ge(S("ckz"), 1)
            for hp in range(2):
                for hh in range(2):
                    r = slice(64 * hh, 64 * hh + 64)
                    dve.tensor_copy(CKZ[r, hp, hh, 0:NC], CK[r, hp, :]).then_inc(S("ckz"), 1)
            dve_sample_queries(dve)
            dve.wait_ge(S("bt_pe"), 6)
            gs = gn[:, 144:192].rearrange("p (r k) -> p r k", k=16)
            dve.tensor_tensor(gs, bank[6][:, 144:192].rearrange("p (r k) -> p r k", k=16),
                              cc("kmask").unsqueeze(1).to_broadcast([P, 3, 16]), ALU.mult).then_inc(S("gate_s"), 1)
            dve.wait_ge(S("gate_s"), 1)
            dve.tensor_reduce(GATE_S, gs, AXX, ALU.add).then_inc(S("gate_s"), 1)
            dve_norm(dve, "ssm", Y[:, 8:16, :], Y[:, 8:16, :], 8, G_SSM)

        def dve_compressed(dve):
            dve.wait_ge(S("ssm_sum"), 1)
            dve.wait_ge(S("bt_pe"), 7)
            for hp in range(2):
                dve.tensor_tensor(CVZ[:, hp],
                                  bank[7][:, hp * P:(hp + 1) * P].rearrange("p (e d) -> p e d", e=2).unsqueeze(1)
                                  .to_broadcast([P, GQ, 2, HD]),
                                  cc("selT").rearrange("p (g e) -> p g e", e=2).unsqueeze(3).to_broadcast([P, GQ, 2, HD]),
                                  ALU.mult).then_inc(S("cvz"), 1)
            do = Counted(dve, S("c_d"))
            for qb in range(QB):
                cm, cr = (small[:, 96 + 32 * qb + 16 * k:112 + 32 * qb + 16 * k] for k in range(2))
                w = CW[qb].rearrange("p (k n) -> p k n", n=16)
                dve.wait_ge(S("c_s"), qb + 1)
                do(dve.tensor_tensor(CW[qb], bank[5 + qb][:, 0:256], cc("cb", qb * TP, TP), ALU.add))
                do.wait()
                do(dve.tensor_reduce(cm, w, AXX, ALU.max))
                do.wait()
                do(dve.tensor_tensor(w, w, cm.unsqueeze(2).to_broadcast([P, HEADS, 16]), ALU.subtract))
                dve.wait_ge(S("c_e"), qb + 1)
                do(dve.tensor_tensor(w, w, cc("mc", qb * 16, 16).unsqueeze(1).to_broadcast([P, HEADS, 16]), ALU.mult))
                do.wait()
                do(dve.tensor_reduce(cr, w, AXX, ALU.add))
                do.wait()
                do(dve.tensor_scalar(cr, cr, TINY, None, ALU.max))
                do.wait()
                do(dve.reciprocal(cm, cr))
                do.wait()
                gate_c = gn[:, qb * 48:qb * 48 + 16].rearrange("p (h e g) -> p h g e", h=2, e=2)
                do(dve.tensor_tensor(cr.rearrange("p (h g e) -> p h g e", h=2, g=GQ),
                                     cm.rearrange("p (h g e) -> p h g e", h=2, g=GQ), gate_c, ALU.mult))
                do.wait()
                do(dve.tensor_tensor(w, w, cr.unsqueeze(2).to_broadcast([P, HEADS, 16]), ALU.mult))

        def pe_compressed(pe):
            for qb in range(QB):
                pe.wait_ge(S("c_d"), 9 * (qb + 1))
                for hp in range(2):
                    tr = pe.transpose(bank[3 + qb][:, hp * P:(hp + 1) * P], CW[qb][:, hp * P:(hp + 1) * P], ident)
                tr.then_inc(S("c_t"), 1)

        def act_compressed(act):
            for qb in range(QB):
                act.wait_ge(S("c_t"), qb + 1)
                act.activation(CPT[qb], bank[3 + qb][:, 0:256], ACT.Copy).then_inc(S("c_pt"), 1)

        UNITS = QB * HEADS
        SC = [m_t[:, b * 512:(b + 1) * 512] for b in range(3)]
        PT = [m_t[:, 1536 + b * 512:1536 + (b + 1) * 512] for b in range(3)]

        def st(b, k, n=3):
            return small[:, b * 15 + 3 * k:b * 15 + 3 * k + n]

        def unit(u):
            qb, hp, g, hh = u // 16, u // 8 % 2, u // 2 % 4, u % 2
            return qb, hp, g, hh, P * (qb + 1), 4 * (2 * hp + hh) + g

        def pe_scores(pe, u):
            qb, hp, g, hh, nk, _ = unit(u)
            r = slice(64 * hh, 64 * hh + 64)
            if u >= 2:
                pe.wait_ge(S("att_m"), 3 * (u - 2) + 1)
            q = Z[r, 4 * hp + g, qb * P:(qb + 1) * P]
            pe.matmul(bank[u % 2][:, 0:nk], lhsT=q, rhs=Z[r, K_SEL + hp, 0:nk], start=True, stop=True)
            pe.matmul(bank[u % 2][:, 256:256 + nk], lhsT=q, rhs=Z[r, K_WIN + hp, 0:nk], start=True, stop=True)\
                .then_inc(S("att_s"), 1)

        def dve_unit(dve, u):
            new, old = u < UNITS, u >= 1
            m, w = Counted(dve, S("att_m"), 3 * u), Counted(dve, S("att_w"), 4 * (u - 1))
            if new:
                qb, hp, g, hh, nk, head = unit(u)
                b, bk = u % 3, u % 2
                sc = SC[b][:, 0:2 * nk].rearrange("p (r n) -> p r n", r=2)
                dve.wait_ge(S("att_s"), u + 1)
                if u >= 3:
                    dve.wait_ge(S("att_t"), u - 2)
                m(dve.scalar_tensor_tensor(
                    out=sc, in0=cc(f"d{qb}").unsqueeze(1).to_broadcast([P, 2, nk]), scalar=SLOPE[head] / SCALE,
                    in1=bank[bk][:, :].rearrange("p (r n) -> p r n", r=2)[:, :, 0:nk], op0=ALU.mult, op1=ALU.add))
            if old:
                oqb, _, _, _, onk, ohead = unit(u - 1)
                ob = (u - 1) % 3
                dve.wait_ge(S("att_e"), 2 * u)
                w(dve.tensor_scalar(st(ob, 3, 2), st(ob, 2, 2), TINY, None, ALU.max))
            if new:
                m.wait()
                m(dve.tensor_reduce(st(b, 0, 2), sc, AXX, ALU.max))
            if old:
                w.wait()
                w(dve.reciprocal(st(ob, 4, 2), st(ob, 3, 2)))
            if new:
                m.wait()
                m(dve.tensor_scalar(st(b, 1, 2), st(b, 0, 2), -SCALE, None, ALU.mult))
            if old:
                w.wait()
                gv = gn[:, oqb * 48:(oqb + 1) * 48].rearrange("p (r k) -> p r k", k=16)
                for r in range(2):
                    where = SC[ob][:, r * onk:(r + 1) * onk]
                    w(dve.tensor_scalar(where, where, st(ob, 4, 2)[:, r:r + 1], gv[:, r + 1, ohead:ohead + 1],
                                        ALU.mult, ALU.mult))

        def act_exp(act, u):
            nk, b = unit(u)[4], u % 3
            act.wait_ge(S("att_m"), 3 * (u + 1))
            for r in range(2):
                act.activation(SC[b][:, r * nk:(r + 1) * nk], SC[b][:, r * nk:(r + 1) * nk], ACT.Exp, scale=SCALE,
                               bias=st(b, 1)[:, r:r + 1], accum_out=st(b, 2)[:, r:r + 1]).then_inc(S("att_e"), 1)

        def pe_turn(pe, u):
            nk, b = unit(u)[4], u % 3
            pe.wait_ge(S("att_w"), 4 * (u + 1))
            if u >= 2:
                pe.wait_ge(S("att_pt"), u - 1)
            else:
                pe.wait_ge(S("c_pt"), u + 1)
            for n in range(2 * nk // P):
                tr = pe.transpose(bank[3 + u % 2][:, n * P:(n + 1) * P], SC[b][:, n * P:(n + 1) * P], ident)
            tr.then_inc(S("att_t"), 1)

        def act_keep(act, u):
            nk, b = unit(u)[4], u % 3
            act.wait_ge(S("att_t"), u + 1)
            if u >= 3:
                act.wait_ge(S("att_pv"), u - 2)
            act.activation(PT[b][:, 0:2 * nk], bank[3 + u % 2][:, 0:2 * nk], ACT.Copy).then_inc(S("att_pt"), 1)

        def pe_values(pe, u):
            qb, hp, g, hh, nk, _ = unit(u)
            b, pair = u % 3, u // 2
            kv = (2 * hp + hh) * HD
            pe.wait_ge(S("att_pt"), u + 1)
            if u == 0:
                pe.wait_ge(S("cvz"), 2)
                pe.wait_ge(S("c_pt"), 2)
            if pair >= 2:
                pe.wait_ge(S("att_o"), pair - 1)
            out = bank[5 + pair % 2][64 * hh:64 * hh + 64, 0:P]
            n = nk // P
            pe.matmul(out, lhsT=CVZ[:, hp, g, hh, :], rhs=CPT[qb][:, hp * P:(hp + 1) * P], start=True, stop=False,
                      tile_position=(0, 64 * hh))
            for r in range(2):
                for k in range(n):
                    mm = pe.matmul(out, lhsT=VN[:, k, r * 256 + kv:r * 256 + kv + HD],
                                   rhs=PT[b][:, (r * n + k) * P:(r * n + k + 1) * P], start=False,
                                   stop=(r == 1 and k == n - 1), tile_position=(0, 64 * hh))
            mm.then_inc(S("att_pv"), 1)

        def act_attended(act, pair):
            qb, hp, g = unit(2 * pair)[:3]
            act.wait_ge(S("att_pv"), 2 * (pair + 1))
            act.activation(Y[:, 4 * hp + g, qb * P:(qb + 1) * P], bank[5 + pair % 2][:, 0:P], ACT.Copy)\
                .then_inc(S("att_o"), 1)

        SS = x_t[:, 0:2 * (PAST + 1) + 16]
        PZ = x_t[:, 544:1568].rearrange("p (m b n) -> p m b n", m=4, b=4)
        PZC = x_t[0:NC, 1568:1824].rearrange("p (b n) -> p b n", b=4)
        PTN = x_t[0:TS, 1824:2080]
        PN = x_t[:, 2080:2096]
        OX, OY = x_t[:, 2096:2096 + 256], x_t[:, 2352:2480]
        CKS = x_t[:, 2352:2832].rearrange("p (t b n) -> p t b n", t=4, b=TS)
        CVS = b_st[0:NC, :]
        NK = PAST + 1
        QZ = x_t[:, 3600:4112].rearrange("p (b n) -> p b n", n=P)

        def qs(hp, b):
            a = b % 2 * 64 + hp * 32
            return QZ[:, b // 2, a:a + 32]

        def dve_sample_queries(dve):
            dve.memset(x_t[:, 3600:4112], 0.0).then_inc(S("qz"), 1)
            dve.wait_ge(S("qz"), 1)
            for hh in range(2):
                r = slice(64 * hh, 64 * hh + 64)
                for c in range(2):
                    for hp in range(2):
                        a = c * 80 + hp * 40 + hh * 4
                        dve.tensor_copy(QZ[r, :, a:a + 4],
                                        Z[r, 4 * hp:4 * hp + 4, TP + c:NT:2].rearrange("p g b -> p b g")).then_inc(S("qz"), 1)

        def dve_index(dve):
            do = Counted(dve, S("idx"))
            dve.wait_ge(S("ld_w"), 32)
            dve.wait_ge(S("ld_c"), 16)
            do(dve.tensor_copy(small[:, 48:64], idx_i[:, :]))
            do.wait()
            do(dve.tensor_scalar(small[:, 64:80], small[:, 48:64], float(P), cc("pidx"), ALU.mult, ALU.add))
            do.wait()
            do(dve.tensor_copy(idx_i[:, :], small[:, 64:80]))

        def pool_caches(pool):
            pool.wait_ge(S("idx"), 3)
            for b in range(TS):
                free(pool, start["dk"] + b)
                s, by, _ = full["dk", b]
                at_ = lambda o, n=256: ring[:, s * D + o:s * D + o + n]
                for pg in range(2):
                    ix = bass.IndirectOffsetOnAxis(idx_i[:, 2 * b + pg:2 * b + pg + 1], 0)
                    for name, o in (("pool_ks", 0), ("pool_kc", 1024), ("pool_vc", 1536)):
                        pool.indirect_dma_start(at_(o + 256 * pg), None, A[name], ix).then_inc(S(by), 16)
                pool.dma_start(at_(512, 512), A["win_k"][b]).then_inc(S(by), 16)
            for b in range(TS):
                free(pool, start["dv"] + b)
                s, by, _ = full["dv", b]
                at_ = lambda o, n=256: ring[:, s * D + o:s * D + o + n]
                for pg in range(2):
                    ix = bass.IndirectOffsetOnAxis(idx_i[:, 2 * b + pg:2 * b + pg + 1], 0)
                    pool.indirect_dma_start(at_(256 * pg), None, A["pool_vs"], ix).then_inc(S(by), 16)
                pool.dma_start(at_(512, 512), A["win_v"][b]).then_inc(S(by), 16)

        def pool_new_rows(pool):
            pool.wait_ge(S("bt_act"), 6)
            for name, a in (("new_k", 0), ("new_v", 512)):
                pool.dma_start(A[name][:, 256 * 256:257 * 256], NEW[:, a:a + 256]).then_inc(S("new_stored"), 16)

        def dve_sample_compress(dve, b):
            if b == 0:
                dve.wait_ge(S("o_ssm"), 1)
                dve.wait_ge(S("cmp_p"), COMPRESSED)
            do = Counted(dve, S("cmp_s"), COMPRESSED * b)
            s = arrived(dve, "dk", b)
            if b:
                do.wait(0)
            dve_compress(do, lambda kv, hp: ring[:, s * D + 1024 + 512 * kv:s * D + 1536 + 512 * kv].rearrange(
                "p (g h c j) -> p g h c j", g=2, h=2, j=STRIDE)[:, :, hp], CKS[:, :, b, :])

        def pe_sample_scores(pe, b):
            if b == 0:
                pe.wait_ge(S("qz"), 9)
                pe.wait_ge(S("evac"), tiles_before["out"])
                pe.wait_ge(S("cvz"), 2)
            s = arrived(pe, "dk", b)
            rows = slice(32 * (b // 2), 32 * (b // 2) + 32)
            pages = ring[:, s * D:s * D + 1024].rearrange("p (m h n) -> p m h n", m=4, h=2)
            pe.wait_ge(S("cmp_s"), COMPRESSED * (b + 1))
            for hp in range(2):
                first, last = (b % 2 == 0 and hp == 0), (b % 2 == 1 and hp == 1)
                at_ = dict(tile_position=(0, rows.start), skip_group_check=True)
                pe.matmul(bank[2][rows, :], lhsT=qs(hp, b), rhs=pages[:, :, hp, :], start=first, stop=last, **at_)
                pe.matmul(bank[7][rows, 0:NC], lhsT=qs(hp, b), rhs=CKS[:, hp, b, :], start=first, stop=last, **at_)
                mm = pe.matmul(bank[7][rows, 16:18], lhsT=qs(hp, b), rhs=Z[:, K_SEL + hp:K_WIN + hp + 1:4, TP + b],
                               start=False, stop=last, **at_)
            mm.then_inc(S("dk_used"), 1)

        def pe_sample_turn(pe):
            pe.wait_ge(S("att_o"), UNITS // 2)
            for n in range(4):
                for k in range(4):
                    b, hp = (4 * n + k) // 2, k % 2
                    tr = pe.transpose(bank[(0, 1, 5, 6)[n]][0:NC, k * P:(k + 1) * P], CKS[:, 2 + hp, b, :], ident)
            tr.then_inc(S("dec_pe"), 1)
            pe.wait_ge(S("dec_dve"), 15)
            for n in range(4):
                r, k = n // 2, n % 2
                pe.transpose(bank[3][:, n * P:(n + 1) * P], SS[:, r * NK + k * P:r * NK + (k + 1) * P], ident)
            pe.transpose(bank[4][0:NC, 0:P], SS[:, 2 * NK:2 * NK + NC], ident)
            for r in range(2):
                tr = pe.transpose(bank[4][0:TS, P * (r + 1):P * (r + 2)], PN[:, r * TS:(r + 1) * TS], ident)
            tr.then_inc(S("dec_pe"), 1)

        def act_sample_scores(act):
            act.wait_ge(S("dec_pe"), 1)
            act.wait_ge(S("cmp_s"), COMPRESSED * TS)
            for n in range(4):
                act.activation(CVS[:, n * 512:(n + 1) * 512], bank[(0, 1, 5, 6)[n]][0:NC, :], ACT.Copy).then_inc(S("dec_act"), 1)
            act.wait_ge(S("dec_dve"), 6)
            for r, (a, n) in enumerate(((0, NK), (NK, NK), (2 * NK, NC))):
                act.activation(SS[:, a:a + n], SS[:, a:a + n], ACT.Exp, scale=SCALE, bias=st(0, 1)[:, r:r + 1],
                               accum_out=st(0, 2)[:, r:r + 1]).then_inc(S("dec_act"), 1)
            act.wait_ge(S("dec_pe"), 2)
            act.wait_ge(S("dec_dve"), 8)
            for c in range(2):
                w = slice(48 * c, 48 * c + 16)
                act.activation(PZ[:, :, :, w], bank[3][:, :].rearrange("p (m b c n) -> p m b c n", m=4, b=4, c=2)[:, :, :, c],
                               ACT.Copy).then_inc(S("dec_act"), 1)
                act.activation(PZC[:, :, w], bank[4][0:NC, 0:P].rearrange("p (b c n) -> p b c n", b=4, c=2)[:, :, c],
                               ACT.Copy).then_inc(S("dec_act"), 1)
            act.activation(PTN, bank[4][0:TS, P:3 * P], ACT.Copy).then_inc(S("dec_act"), 1)
            act.wait_ge(S("dec_pe"), 3)
            o = bank[6][:, 0:P].rearrange("p (b h e) -> p h e b", h=2, b=TS)
            for hh in range(2):
                r = slice(64 * hh, 64 * hh + 64)
                act.activation(Y[r, 0:8, TP:NT].rearrange("p (h g) b -> p h g b", h=2), o[r, :, 4 * hh:4 * hh + 4, :],
                               ACT.Copy).then_inc(S("dec_out"), 1)

        def dve_sample_weights(dve):
            do = Counted(dve, S("dec_dve"))
            dve.wait_ge(S("dk_used"), TS)
            dve.wait_ge(S("att_pv"), UNITS)
            sel_win = SS[:, 0:2 * NK].rearrange("p (r n) -> p r n", r=2)
            do(dve.tensor_tensor(sel_win[:, :, 0:PAST], bank[2][:, :].rearrange("p (r n) -> p r n", r=2),
                                 cc("ds", 0, PAST).unsqueeze(1).to_broadcast([P, 2, PAST]), ALU.add))
            do(dve.tensor_tensor(sel_win[:, :, PAST], bank[7][:, 16:18], cc("ds", PAST, 1).to_broadcast([P, 2]), ALU.add))
            do(dve.tensor_tensor(SS[:, 2 * NK:2 * NK + NC], bank[7][:, 0:NC], cc("dcs"), ALU.add))
            do.wait()
            do(dve.tensor_reduce(st(0, 0, 2), sel_win, AXX, ALU.max))
            do(dve.tensor_reduce(st(0, 0)[:, 2:3], SS[:, 2 * NK:2 * NK + NC], AXX, ALU.max))
            do.wait()
            do(dve.tensor_scalar(st(0, 1), st(0, 0), -SCALE, None, ALU.mult))
            do(dve.memset(x_t[:, 544:1568], 0.0))
            do(dve.memset(x_t[0:NC, 1568:1824], 0.0))
            dve.wait_ge(S("dec_act"), 7)
            do(dve.tensor_scalar(st(0, 3), st(0, 2), TINY, None, ALU.max))
            do.wait()
            do(dve.reciprocal(st(0, 4), st(0, 3)))
            do.wait()
            rc = st(0, 4)
            for k, (r, a, n) in enumerate(((1, 0, NK), (2, NK, NK), (0, 2 * NK, NC))):
                do(dve.tensor_scalar(SS[:, a:a + n], SS[:, a:a + n], rc[:, k:k + 1], GATE_S[:, r:r + 1], ALU.mult, ALU.mult))
            do.wait()
            for r in range(2):
                a = r * NK + PAST
                do(dve.tensor_scalar(PN[:, r * TS:(r + 1) * TS], cc("selT"), SS[:, a:a + 1], None, ALU.mult))
            assert do.n == 15
            do2 = Counted(dve, S("dec_own"))
            dve.wait_ge(S("dv_used"), TS)
            do2(dve.tensor_tensor(OX.rearrange("p (k d) -> p k d", k=KV), bank[5][:, 0:256].rearrange("p (k d) -> p k d", k=KV),
                                  cc("kvm").unsqueeze(2).to_broadcast([P, KV, HD]), ALU.mult))
            do2.wait()
            for n in range(2):
                do2(dve.tensor_reduce(OY[:, n * HD:(n + 1) * HD], OX.rearrange("p (k d) -> p d k", k=KV), AXX, ALU.add))

        def pe_sample_values(pe):
            pe.wait_ge(S("dec_act"), 12)
            for r in range(2):
                pe.matmul(bank[5][:, 0:256], lhsT=PTN[:, r * P:(r + 1) * P], rhs=NEW[:, 256 * (r + 1):256 * (r + 2)],
                          start=(r == 0), stop=False, skip_group_check=True)
            for b in range(TS):
                s = arrived(pe, "dv", b)
                rows, c = slice(32 * (b // 2), 32 * (b // 2) + 32), b % 2 * 32
                at_ = dict(start=False, tile_position=(0, rows.start), skip_group_check=True)
                for m in range(4):
                    pe.matmul(bank[5][rows, 0:256], lhsT=PZ[:, m, b // 2, c:c + 32],
                              rhs=ring[:, s * D + m * 256:s * D + (m + 1) * 256], stop=False, **at_)
                pe.matmul(bank[5][rows, 0:256], lhsT=PZC[:, b // 2, c:c + 32], rhs=CVS[:, b * 256:(b + 1) * 256],
                          stop=True, **at_).then_inc(S("dv_used"), 1)
            pe.wait_ge(S("dec_own"), 3)
            pe.transpose(bank[6][:, 0:P], OY, ident).then_inc(S("dec_pe"), 1)

        XQ = z_t[:, 0:KT * NT].rearrange("p (t n) -> p t n", n=NT)
        XP = [m_t[:, b * 256:(b + 1) * 256] for b in range(2)]
        XT = [m_t[:, 512 + b * 512:512 + (b + 1) * 512].rearrange("p (m n) -> p m n", m=2) for b in range(2)]
        XSP, XSO2 = m_t[0:32, 1536:1792], (m_t[0:32, 3840:4096], mk_t[0:32, 0:256])
        QX = x_t[:, 0:16 * 256].rearrange("p (t n) -> p t n", n=256)
        PX = m_t[:, 1792:3840].rearrange("p (m n) -> p m n", m=2)

        def pe_cross(pe):
            pe.wait_ge(S("evac"), tiles_before["xo"])

            def scores(u):
                h, qb = u // 2, u % 2
                if u >= 2:
                    pe.wait_ge(S("x_e"), u - 1)
                for d in range(4):
                    mm = pe.matmul(bank[u % 2][:, 0:MEM], lhsT=XQ[:, 4 * h + d, qb * P:(qb + 1) * P],
                                   rhs=MK[:, 4 * h + d, :], start=(d == 0), stop=(d == 3))
                mm.then_inc(S("x_s"), 1)

            def values(h):
                pe.wait_ge(S("x_pt"), 2 * h + 2)
                if h:
                    pe.wait_ge(S("x_o"), 4 * h)
                for d in range(4):
                    for m in range(2):
                        mm = pe.matmul(bank[4 + d][:, 0:TP], lhsT=MV[:, m, h * XD + d * P:h * XD + (d + 1) * P],
                                       rhs=XT[h % 2][:, m, :], start=(m == 0), stop=(m == 1))
                mm.then_inc(S("x_pv"), 1)

            scores(0)
            for u in range(8):
                if u < 7:
                    scores(u + 1)
                if u >= 3 and u % 2:
                    values(u // 2 - 1)
                pe.wait_ge(S("x_d"), 4 * (u + 1))
                if u >= 2:
                    pe.wait_ge(S("x_pt"), u - 1)
                for m in range(2):
                    tr = pe.transpose(bank[2 + u % 2][:, m * P:(m + 1) * P], XP[u % 2][:, m * P:(m + 1) * P], ident)
                tr.then_inc(S("x_t"), 1)
            values(3)
            pe.wait_ge(S("qx"), 5)
            for j in range(16):
                b, half = j // 2, j % 2
                s = arrived(pe, "mk", j)
                for t in range(8):
                    mm = pe.matmul(bank[0][0:32, 0:MEM], lhsT=QX[:, 8 * half + t, 32 * b:32 * b + 32],
                                   rhs=ring[:, s * D + t * 256:s * D + (t + 1) * 256],
                                   start=(j == 0 and t == 0), stop=(j == 15 and t == 7))
                mm.then_inc(S("mk_used"), 1)
            pe.wait_ge(S("xs_dve"), 4)
            for m in range(2):
                tr = pe.transpose(bank[2][:, m * 32:(m + 1) * 32], XSP[:, m * P:(m + 1) * P], ident[0:32, 0:32])
            tr.then_inc(S("xs_pe"), 1)
            pe.wait_ge(S("xs_act"), 2)
            for j in range(16):
                b, m = j // 2, j % 2
                s = arrived(pe, "mv", j)
                for h in range(XH):
                    r = b * XH + h
                    mm = pe.matmul(bank[3][0:32, :], lhsT=PX[:, m, 32 * r:32 * r + 32],
                                   rhs=ring[:, s * D + h * XD:s * D + (h + 1) * XD],
                                   start=(j == 0 and h == 0), stop=(j == 15 and h == XH - 1))
                mm.then_inc(S("mv_used"), 1)
            for n in range(2):
                pe.wait_ge(S("xs_act"), 3 + n)
                for d in range(2):
                    tr = pe.transpose(bank[n][:, d * 32:(d + 1) * 32], XSO2[n][:, d * P:(d + 1) * P], ident[0:32, 0:32])
                tr.then_inc(S("xs_pe"), 1)

        def dve_sample_xq(dve):
            dve.wait_ge(S("tile"), tiles_before["xo"])
            dve.memset(x_t[:, 0:16 * 256], 0.0).then_inc(S("qx"), 1)
            dve.wait_ge(S("evac"), tiles_before["xo"])
            dve.wait_ge(S("qx"), 1)
            for h in range(XH):
                dve.tensor_copy(QX[:, 4 * h:4 * h + 4, h::36], XQ[:, 4 * h:4 * h + 4, TP:NT]).then_inc(S("qx"), 1)
            dve.memset(m_t[:, 1792:3840], 0.0).then_inc(S("px"), 1)

        def dve_cross(dve):
            do = Counted(dve, S("x_d"))

            def outputs(h):
                dve.wait_ge(S("x_pv"), h + 1)
                for d in range(4):
                    dve.tensor_copy(Y[:, 4 * h + d, 0:TP], bank[4 + d][:, 0:TP]).then_inc(S("x_o"), 1)

            for u in range(8):
                b = u % 2
                dve.wait_ge(S("x_s"), u + 1)
                do(dve.tensor_reduce(st(b, 0, 1), bank[b][:, 0:MEM], AXX, ALU.max))
                do.wait()
                do(dve.tensor_scalar(st(b, 1, 1), st(b, 0, 1), -XSCALE, None, ALU.mult))
                dve.wait_ge(S("x_e"), u + 1)
                do(dve.reciprocal(st(b, 3, 1), st(b, 2, 1)))
                do.wait()
                do(dve.tensor_scalar(XP[b], XP[b], st(b, 3, 1), None, ALU.mult))
                if u >= 4 and u % 2 == 0:
                    outputs(u // 2 - 2)
            outputs(2)
            outputs(3)
            do = Counted(dve, S("xs_dve"))
            dve.wait_ge(S("mk_used"), 16)
            do(dve.tensor_reduce(small[0:32, 0:1], bank[0][0:32, 0:MEM], AXX, ALU.max))
            do.wait()
            do(dve.tensor_scalar(small[0:32, 3:4], small[0:32, 0:1], -XSCALE, None, ALU.mult))
            dve.wait_ge(S("xs_act"), 1)
            do(dve.reciprocal(small[0:32, 9:10], small[0:32, 6:7]))
            do.wait()
            do(dve.tensor_scalar(XSP, XSP, small[0:32, 9:10], None, ALU.mult))

        def act_cross(act):
            def keep(u):
                h, qb = u // 2, u % 2
                act.wait_ge(S("x_t"), u + 1)
                if h >= 2:
                    act.wait_ge(S("x_pv"), h - 1)
                act.activation(XT[h % 2][:, :, qb * P:(qb + 1) * P],
                               bank[2 + u % 2][:, 0:256].rearrange("p (m n) -> p m n", m=2), ACT.Copy).then_inc(S("x_pt"), 1)

            for u in range(8):
                b = u % 2
                act.wait_ge(S("x_d"), 4 * u + 2)
                if u >= 2:
                    act.wait_ge(S("x_t"), u - 1)
                act.activation(XP[b], bank[b][:, 0:MEM], ACT.Exp, scale=XSCALE, bias=st(b, 1, 1),
                               accum_out=st(b, 2, 1)).then_inc(S("x_e"), 1)
                if u:
                    keep(u - 1)
            keep(7)
            act.wait_ge(S("xs_dve"), 2)
            act.activation(XSP, bank[0][0:32, 0:MEM], ACT.Exp, scale=XSCALE, bias=small[0:32, 3:4],
                           accum_out=small[0:32, 6:7]).then_inc(S("xs_act"), 1)
            act.wait_ge(S("xs_pe"), 1)
            act.wait_ge(S("px"), 1)
            act.activation(PX[:, :, 0::33], bank[2][:, 0:64].rearrange("p (m r) -> p m r", m=2), ACT.Copy)\
                .then_inc(S("xs_act"), 1)
            act.wait_ge(S("mv_used"), 16)
            for n in range(2):
                act.activation(XSO2[n], bank[3][0:32, n * 256:(n + 1) * 256], ACT.Copy).then_inc(S("xs_act"), 1)
            y = Y[:, :, TP:NT].rearrange("p (h d) b -> p d b h", h=XH)
            for n in range(2):
                act.wait_ge(S("xs_pe"), 2 + n)
                act.activation(y[:, 2 * n:2 * n + 2], bank[n][:, 0:64].rearrange("p (d b h) -> p d b h", d=2, h=XH), ACT.Copy)\
                    .then_inc(S("xs_out"), 1)

        def pe_middle(pe):
            pe_by_token(pe)
            pe_scores(pe, 0)
            pe_scores(pe, 1)
            pe_compressed(pe)
            for u in range(UNITS + 2):
                if u + 2 < UNITS:
                    pe_scores(pe, u + 2)
                if u >= 2:
                    pe_values(pe, u - 2)
                if u < UNITS:
                    pe_turn(pe, u)
                if u % 4 == 3 and u < UNITS:
                    pe_sample_scores(pe, u // 4)
            pe_sample_turn(pe)
            pe_sample_values(pe)
            pe_norm(pe, "att", X[:, 0:8, :], 8)
            pe.wait_ge(S("ssm_x"), 9)
            pe.wait_ge(S("att_x"), 9)
            pe_gemm(pe, "out", Y, KT)
            pe_sum(pe, "x", SUM, KT + 1)
            pe_gemm(pe, "xq", X, KT, ready="x")
            pe_cross(pe)
            pe.wait_ge(S("x_o"), 16)
            pe.wait_ge(S("xs_out"), 2)
            pe_gemm(pe, "xo", Y, KT)
            pe_sum(pe, "ffn", SUM, KT + 1)
            pe_by_rows(pe)

        def act_middle(act):
            act_by_token(act)
            for u in range(UNITS):
                act_exp(act, u)
                if u == 0:
                    act_compressed(act)
                if u >= 1:
                    act_keep(act, u - 1)
                if u >= 4 and u % 2 == 0:
                    act_attended(act, (u - 4) // 2)
            act_keep(act, UNITS - 1)
            act_attended(act, UNITS // 2 - 2)
            act_attended(act, UNITS // 2 - 1)
            act_sample_scores(act)
            act.wait_ge(S("dec_out"), 2)
            act_norm(act, "att", Y[:, 0:8, :], X[:, 0:8, :], 8, 1024)
            act_squares(act, "out", "x")
            act.wait_ge(S("z_stored"), 16)
            copy_gemm(act, "xq", XQ)
            act_cross(act)
            act_squares(act, "xo", "ffn")
            act_by_rows(act)

        def dve_middle(dve):
            dve_by_token(dve)
            dve_compressed(dve)
            for u in range(UNITS + 1):
                dve_unit(dve, u)
                if u % 4 == 2:
                    dve_sample_compress(dve, u // 4)
            dve_sample_weights(dve)
            dve_norm(dve, "att", Y[:, 0:8, :], Y[:, 0:8, :], 8, G_ATT)
            add_gemm(dve, "out", "x")
            dve.wait_ge(S("new_stored"), 32)
            dve_norm(dve, "x", X, H, KT, G_X)
            dve_sample_xq(dve)
            dve_cross(dve)
            add_gemm(dve, "xo", "ffn")
            dve_norm(dve, "ffn", X, H, KT, G_FFN)
            dve_by_rows(dve)

        def pool_middle(pool):
            pool_new_rows(pool)
            pool_caches(pool)
            pool.wait_ge(S("evac"), tiles_before["xq"])
            pool.wait_ge(S("z_stored"), 16)
            pool.dma_start(KEYS, A["keys"]).then_inc(S("ld_keys"), 16)
            pool.dma_start(GB, A["g_ffn"].partition_broadcast(P)).then_inc(S("ld_gf"), 16)

        BLOCKS = (P, P, TS)
        HN = [mv_n[:, 0:D], mv_n[:, D:2 * D], b_st[:, :]]
        XN = [y_t[:, 0:D], y_t[:, D:2 * D], c_st[:, :]]
        ACC_S = y_t[:, 0:D]
        GB = z_t[:, KT * NT:KT * NT + D]
        SLOT = [ring[:, i * D:(i + 1) * D] for i in range(4)] + [m_t[:, 0:D], m_t[:, D:2 * D], mk_t[:, 0:D], mk_t[:, D:2 * D]]
        NSLOT = len(SLOT)
        HOT = h_t[:, 0:D]
        PARTS = 4

        def marks(heads):
            return 10 * heads, 15 * heads + 3, 15 * heads + 16, 15 * heads + 19

        RETRIEVAL = [(0, 2 * q, 2 * q + 2, q * marks(2)[3], h_t[:, 512 + q % 2 * 512:1024 + q % 2 * 512], h_t[:, 1536:2048])
                     for q in range(PARTS)]
        for _blk in (1, 2):
            RETRIEVAL.append((_blk, 0, PH, PARTS * marks(2)[3] + (_blk - 1) * marks(PH)[3], x_t[:, 0:D], x_t[:, D:2 * D]))
        SECOND, THIRD = RETRIEVAL[PARTS][3], RETRIEVAL[PARTS + 1][3]

        def hw(a, n=SLOTS):
            return h_t[:, D + a:D + a + n]

        VAL, VIX, VIF = hw(0, 256), hw(256, 256), hw(512, 256)
        TOP, PIX, PF, PA, IA, IB = (hw(768 + 128 * i) for i in range(6))
        WGT = [hw(1536 + 128 * i) for i in range(3)]
        ACTV = hw(1920)
        EIX = [z_t[:, 6272 + 128 * i:6272 + 128 * (i + 1)].bitcast(I32) for i in range(2)]
        EXF, EXS = z_t[:, 6528:6536], z_t[:, 6864:6872].bitcast(I32)
        WS, AS, RED, STAT = z_t[:, 6536:6544], z_t[:, 6544:6552], z_t[:, 6552:6568], z_t[:, 6568:6592]
        KEYS = z_t[:, 6592:6848].rearrange("p (c n) -> p c n", c=2)
        IXS = [z_t[:, 6848 + 8 * i:6856 + 8 * i].bitcast(I32) for i in range(2)]
        EXPW = z_t[:, 6880:7008]

        def pe_by_rows(pe):
            pe.wait_ge(S("ffn_rms"), 1)
            for blk, n in enumerate(BLOCKS):
                lo = blk * P
                for q in range(4):
                    k = 4 * blk + q
                    if k >= 4:
                        pe.wait_ge(S("hn_act"), k - 3)
                    for d in range(4):
                        tr = pe.transpose(bank[4 + q][0:n, d * P:(d + 1) * P], H[:, 4 * q + d, lo:lo + n], ident)
                    tr.then_inc(S("hn_pe"), 1)

        def act_row_root(act, blk, junk, tag, base):
            n, c = BLOCKS[blk], STAT[:, base + 3 * blk:base + 3 * blk + 3]
            act.activation(junk[0:n, :], HN[blk][0:n, :], ACT.Square, accum_out=c[0:n, 0:1]).then_inc(S(tag), 1)
            act.wait_ge(S(tag), 2 * blk + 1)
            act.activation(c[0:n, 1:2], c[0:n, 0:1], ACT.Sqrt, bias=cc("eps", rows=n), scale=1.0 / D).then_inc(S(tag), 1)

        def dve_row_scale(dve, blk, dst, tag, done, base):
            n, c = BLOCKS[blk], STAT[:, base + 3 * blk:base + 3 * blk + 3]
            dve.wait_ge(S(tag), 2 * blk + 2)
            dve.reciprocal(c[0:n, 2:3], c[0:n, 1:2]).then_inc(S(done), 1)
            dve.wait_ge(S(done), 2 * blk + 1)
            dve.scalar_tensor_tensor(out=dst[0:n, :], in0=HN[blk][0:n, :], scalar=c[0:n, 2:3], in1=GB[0:n, :],
                                     op0=ALU.mult, op1=ALU.mult).then_inc(S(done), 1)

        def act_by_rows(act):
            act.wait_ge(S("m_stored"), 32)
            for blk, n in enumerate(BLOCKS):
                for q in range(4):
                    act.wait_ge(S("hn_pe"), 4 * blk + q + 1)
                    act.activation(HN[blk][0:n, q * 512:(q + 1) * 512], bank[4 + q][0:n, :], ACT.Copy).then_inc(S("hn_act"), 1)
            act.wait_ge(S("hn_act"), 12)
            for blk in range(3):
                if blk:
                    act.wait_ge(S("row_rms"), 2 * blk)
                act_row_root(act, blk, m_t[:, 0:D], "row_rms", 0)

        def dve_by_rows(dve):
            dve.wait_ge(S("ld_gf"), 16)
            for blk in range(3):
                dve_row_scale(dve, blk, XN[blk], "row_rms", "xn", 0)

        def pe_key_scores(pe, blk, q, b):
            n, lo = BLOCKS[blk], blk * P
            for k in range(4):
                t = 4 * q + k
                mm = pe.matmul(bank[b][0:n, k * PK:(k + 1) * PK], lhsT=XQ[:, t, lo:lo + n], rhs=KEYS[:, t % 2, :],
                               start=True, stop=True)
            mm.then_inc(S("sco_pe"), 1)

        def pe_queries(pe):
            base = tiles_before["pq"]
            for n in range(16):
                s = arrived(pe, "pq", n)
                pe.wait_ge(S("evac"), base + max(n - 3, 0))
                for t in range(KT):
                    if n == 0:
                        pe.wait_ge(S("ffn_x"), t + 2)
                    mm = pe.matmul(bank[n % 4][:, 0:NT], lhsT=R[:, s, t, :], rhs=X[:, t, :],
                                   start=(t == 0), stop=(t == KT - 1))
                mm.then_inc(S("tile"), 1)
                if n == 4:
                    pe.wait_ge(S("hn_act"), 12)
                    pe.wait_ge(S("ld_keys"), 16)
                if n >= 4 and n % 4 == 0:
                    pe.wait_ge(S("evac"), base + n)
                    pe_key_scores(pe, 0, n // 4 - 1, 3 + n // 4)
            pe.wait_ge(S("evac"), base + 16)
            pe_key_scores(pe, 0, 3, 7)

        def act_queries(act):
            base = tiles_before["pq"]
            for n in range(16):
                act.wait_ge(S("tile"), base + n + 1)
                act.activation(XQ[:, n, :], bank[n % 4][:, 0:NT], ACT.Copy).then_inc(S("evac"), 1)
                if n >= 4 and n % 4 == 0:
                    act_scores(act, n // 4 - 1)
                if n >= 4 and n % 4 == 2:
                    act_softmax(act, n // 4 - 1)
            act_scores(act, 3)
            act_softmax(act, 3)

        def act_scores(act, q):
            if q >= 2:
                act.wait_ge(S("tk"), RETRIEVAL[q - 2][3] + marks(2)[1])
            act.wait_ge(S("sco_pe"), q + 1)
            act.activation(RETRIEVAL[q][4], bank[4 + q][:, :], ACT.Copy).then_inc(S("sco_act"), 1)

        def act_softmax(act, r):
            blk, h0, h1, base = RETRIEVAL[r][:4]
            act.wait_ge(S("tk"), base + marks(h1 - h0)[1])
            w = WGT[blk][0:BLOCKS[blk], h0 * TOPK:h1 * TOPK]
            act.activation(w, w, ACT.Exp).then_inc(S("tk_exp"), 1)

        def pe_keys(pe, blk):
            if blk == 2:
                pe.wait_ge(S("sco_act"), PARTS + 4)
            for q in range(4):
                pe_key_scores(pe, blk, q, q)

        def act_keys(act, blk):
            n, sco = BLOCKS[blk], RETRIEVAL[PARTS + blk - 1][4]
            if blk == 2:
                act.wait_ge(S("tk"), SECOND + marks(PH)[1])
            for q in range(4):
                act.wait_ge(S("sco_pe"), 4 * blk + q + 1)
                act.activation(sco[0:n, q * 512:(q + 1) * 512], bank[q][0:n, :], ACT.Copy).then_inc(S("sco_act"), 1)
            act_softmax(act, PARTS + blk - 1)

        def dve_sixteen(do, n, src, work, groups, width, val, ix):
            r, eng = slice(0, n), do.eng

            def part(t, m, w=width):
                return t[r, m * w:(m + 1) * w]

            def eight(t, m, k):
                return t[r, m * 16 + 8 * k:m * 16 + 8 * k + 8]

            for m in range(groups):
                do(eng.max(eight(val, m, 0), part(src, m)))
            do.wait()
            for m in range(groups):
                do(eng.match_replace(part(work, m), eight(val, m, 0), part(src, m), -3e38))
                do(eng.max_index(eight(ix, m, 0), eight(val, m, 0), part(src, m)))
            do.wait()
            for m in range(groups):
                do(eng.max(eight(val, m, 1), part(work, m)))
            do.wait()
            for m in range(groups):
                do(eng.max_index(eight(ix, m, 1), eight(val, m, 1), part(work, m)))

        def dve_keys(dve, i):
            blk, h0, h1, base, sco, _ = RETRIEVAL[i]
            do = Counted(dve, S("tk"), base)
            if i:
                do.wait(0)
            dve.wait_ge(S("sco_act"), i + 1 if i < PARTS else 4 * (blk + 1))
            c = slice(h0 * 32, h1 * 32)
            dve_sixteen(do, BLOCKS[blk], sco, HOT, 2 * (h1 - h0), PK, VAL[:, c], VIX.bitcast(U32)[:, c])
            assert do.n == marks(h1 - h0)[0]

        def dve_candidates(dve, i):
            blk, h0, h1, base, sco, cand = RETRIEVAL[i]
            nh = h1 - h0
            n, do = BLOCKS[blk], Counted(dve, S("tk"), base + marks(nh)[0])
            do.wait()
            r, c, k = slice(0, n), slice(h0 * 32, h1 * 32), slice(h0 * TOPK, h1 * TOPK)
            v = VAL[r, c].rearrange("p (h c k) -> p h c k", h=nh, c=2)
            do(dve.tensor_copy(VIF[r, c], VIX.bitcast(U32)[r, c]))
            do(dve.tensor_tensor(cand[r, 0:nh * 256].rearrange("p (h a b) -> p h a b", h=nh, a=16),
                                 v[:, :, 0].unsqueeze(3).to_broadcast([n, nh, 16, 16]),
                                 v[:, :, 1].unsqueeze(2).to_broadcast([n, nh, 16, 16]), ALU.add))
            do.wait()
            dve_sixteen(do, n, cand, sco, nh, 256, TOP[:, k], PIX.bitcast(U32)[:, k])
            do.wait()
            t3 = TOP[r, k].rearrange("p (h k) -> p h k", h=nh)
            do(dve.tensor_tensor(WGT[blk][r, k].rearrange("p (h k) -> p h k", h=nh), t3,
                                 t3[:, :, 0:1].to_broadcast([n, nh, 16]), ALU.subtract))
            assert do.n + marks(nh)[0] == marks(nh)[1]

        def dve_experts(dve, i):
            blk, h0, h1, base = RETRIEVAL[i][:4]
            nh = h1 - h0
            n, do = BLOCKS[blk], Counted(dve, S("tk"), base + marks(nh)[1])
            do.wait()
            r, k = slice(0, n), slice(h0 * TOPK, h1 * TOPK)
            pf, pa, ia, ib = (x[r, k] for x in (PF, PA, IA, IB))
            vi = VIF[r, h0 * 32:h1 * 32].rearrange("p (h c k) -> p h c k", h=nh, c=2)
            do(dve.tensor_copy(pf, PIX.bitcast(U32)[r, k]))
            do.wait()
            do(dve.tensor_scalar(pa, pf, 1 / 16, -15 / 32, ALU.mult, ALU.add))
            do.wait()
            do(dve.tensor_scalar(pa, pa, MAGIC, None, ALU.add))
            do.wait()
            do(dve.tensor_scalar(pa, pa, MAGIC, None, ALU.subtract))
            do.wait()
            do(dve.scalar_tensor_tensor(out=pf, in0=pa, scalar=-16.0, in1=pf, op0=ALU.mult, op1=ALU.add))
            hot = HOT[r, 0:nh * 256].rearrange("p (s k) -> p s k", k=16)
            hot4 = HOT[r, 0:nh * 256].rearrange("p (h s k) -> p h s k", h=nh, k=16)
            for c, (pos, out) in enumerate(((pa, ia), (pf, ib))):
                do.wait()
                do(dve.tensor_tensor(hot, cc("iota")[r, :].unsqueeze(1).to_broadcast([n, nh * TOPK, 16]),
                                     pos.unsqueeze(2).to_broadcast([n, nh * TOPK, 16]), ALU.is_equal))
                do.wait()
                do(dve.tensor_tensor(hot4, hot4, vi[:, :, c].unsqueeze(2).to_broadcast([n, nh, 16, 16]), ALU.mult))
                do.wait()
                do(dve.tensor_reduce(out, hot, AXX, ALU.add))
            do.wait()
            do(dve.scalar_tensor_tensor(out=ia, in0=ia, scalar=float(PK), in1=ib, op0=ALU.mult, op1=ALU.add))
            if blk < 2:
                do.wait()
                do(dve.tensor_copy(EIX[blk][:, k], ia))
                assert do.n + marks(nh)[1] == marks(nh)[2]
            w3 = WGT[blk][r, k].rearrange("p (h k) -> p h k", h=nh)
            dve.wait_ge(S("tk_exp"), i + 1)
            do(dve.tensor_reduce(RED[r, 0:nh], w3, AXX, ALU.add))
            do.wait()
            do(dve.reciprocal(RED[r, 8:8 + nh], RED[r, 0:nh]))
            do.wait()
            do(dve.tensor_tensor(w3, w3, RED[r, 8:8 + nh].unsqueeze(2).to_broadcast([n, nh, 16]), ALU.mult))

        def dve_retrieve(dve, i):
            dve_keys(dve, i)
            dve_candidates(dve, i)
            dve_experts(dve, i)

        def pe_samples_expand(pe):
            pe.wait_ge(S("xn"), 6)
            pe.wait_ge(S("sco_act"), PARTS)
            for q in range(4):
                mm = pe.matmul(bank[4 + q][:, :], lhsT=cc("sel", rows=TS), rhs=XN[2][0:TS, q * 512:(q + 1) * 512],
                               start=True, stop=True)
            mm.then_inc(S("ex_pe"), 1)

        def act_samples_expand(act):
            act.wait_ge(S("ex_pe"), 1)
            for q in range(4):
                act.activation(XN[2][:, q * 512:(q + 1) * 512], bank[4 + q][:, :], ACT.Copy).then_inc(S("ex_act"), 1)

        def pe_samples_experts(pe):
            pe.wait_ge(S("ex_act"), 4)
            pe.wait_ge(S("tk"), THIRD + marks(PH)[3] - 1)
            pe.matmul(bank[4][:, 0:P], lhsT=cc("sel", rows=TS), rhs=IA[0:TS, :], start=True, stop=True)
            pe.matmul(bank[5][:, 0:P], lhsT=cc("sel", rows=TS), rhs=WGT[2][0:TS, :], start=True, stop=True)\
                .then_inc(S("ex_pe"), 1)

        def dve_samples_experts(dve):
            do = Counted(dve, S("ex_dve"))
            dve.wait_ge(S("ex_pe"), 2)
            mask = cc("kmask").unsqueeze(1).to_broadcast([P, PH, 16])
            for n, out in enumerate((EXF, WS)):
                if n:
                    do.wait()
                do(dve.tensor_tensor(EXPW.rearrange("p (h k) -> p h k", h=PH),
                                     bank[4 + n][:, 0:P].rearrange("p (h k) -> p h k", h=PH), mask, ALU.mult))
                do.wait()
                do(dve.tensor_reduce(out, EXPW.rearrange("p (h k) -> p h k", h=PH), AXX, ALU.add))
            do(dve.tensor_scalar(EXF, EXF, MAGIC, None, ALU.add))
            do.wait()
            do(dve.tensor_scalar(EXF, EXF, MAGIC, None, ALU.subtract))
            do.wait()
            do(dve.tensor_copy(EXS, EXF))

        U_OF, V_OF = (0, 2 * SLOTS), (SLOTS, 3 * SLOTS)
        U_S, V_S = 4 * SLOTS, 4 * SLOTS + PH
        EARLY = 2 * NSLOT

        def landed(g, k):
            return 16 * ((g - EARLY) // NSLOT + 1) + (16 * EARLY // 4 if k >= 4 else 0)

        def pool_peer(pool):
            with pool.register("round") as rnd, pool.register("use") as use:
                pool.reg_mov(rnd, 1 + 4)
                pool.reg_mov(use, 1 + 3 * NSLOT)

                def gather(table, half, k, slot):
                    pool.indirect_dma_start(SLOT[slot], None, A[table], bass.IndirectOffsetOnAxis(IXS[half][:, k:k + 1], 0))\
                        .then_inc(S(f"slot{slot}"), 16)

                def single(table, g, index, early=False):
                    half = g // NSLOT % 2
                    pool.tensor_copy(IXS[half], index).then_inc(S("ixs"), 1)
                    pool.wait_ge(S("ixs"), g // NSLOT + 1)
                    for k in range(NSLOT):
                        if early and g + k >= 4:
                            pool.wait_ge(S("peer_used"), g + k - 3)
                        elif not early and (g > EARLY or k >= 4):
                            pool.wait_ge(S("peer_used"), g + k + 1 - NSLOT)
                        gather(table, half, k, 4 + k % 4 if early else k)

                def gathers(table, blk, i0=0):
                    with pool.Fori(i0, SLOTS // (2 * NSLOT)) as i:
                        for half in range(2):
                            pool.tensor_copy(IXS[half], EIX[blk][:, bass.ds(i * (2 * NSLOT) + half * NSLOT, NSLOT)])\
                                .then_inc(S("ixs"), 1)
                            pool.wait_ge(S("ixs"), rnd)
                            pool.reg_add(rnd, rnd, 1)
                            for k in range(NSLOT):
                                pool.wait_ge(S("peer_used"), use)
                                pool.reg_add(use, use, 1)
                                gather(table, half, k, k)

                pool.wait_ge(S("tk"), marks(2)[2])
                pool.wait_ge(S("m_stored"), 32)
                for g in range(0, EARLY, NSLOT):
                    single("peer_u", g, EIX[0][:, g:g + NSLOT], early=True)
                pool.wait_ge(S("tile"), tiles_before["pq"] + 16)
                for g in range(EARLY, 2 * EARLY, NSLOT):
                    single("peer_u", g, EIX[0][:, g:g + NSLOT])
                pool.wait_ge(S("tk"), RETRIEVAL[3][3] + marks(2)[2])
                gathers("peer_u", 0, 2)
                gathers("peer_v", 0)
                pool.wait_ge(S("tk"), SECOND + marks(PH)[2])
                gathers("peer_u", 1)
                gathers("peer_v", 1)
                pool.wait_ge(S("ex_dve"), 7)
                single("peer_u", U_S, EXS)
                single("peer_v", V_S, EXS)

        def dve_early_dots(dve, lo, hi):
            for g in range(lo, hi):
                k = 4 + g % 4
                dve.wait_ge(S(f"slot{k}"), 16 * (g // 4 + 1))
                dve.scalar_tensor_tensor(out=SLOT[k], in0=SLOT[k], scalar=1.0, in1=XN[0], op0=ALU.mult, op1=ALU.mult,
                                         accum_out=ACTV[:, g:g + 1]).then_inc(S("peer_used"), 1)

        def dve_dots(dve, blk, lo, hi):
            with dve.Fori(lo, hi) as i:
                for k in range(NSLOT):
                    dve.wait_ge(S(f"slot{k}"), i * 16 + landed(U_OF[blk], k))
                    dve.scalar_tensor_tensor(out=SLOT[k], in0=SLOT[k], scalar=1.0, in1=XN[blk], op0=ALU.mult, op1=ALU.mult,
                                             accum_out=ACTV[:, bass.ds(i * NSLOT + k, 1)]).then_inc(S("peer_used"), 1)

        def dve_sums(dve, blk, lo, hi):
            with dve.Fori(lo, hi) as i:
                for k in range(NSLOT):
                    dve.wait_ge(S(f"slot{k}"), i * 16 + landed(V_OF[blk], k))
                    dve.wait_ge(S("peer_used"), i * NSLOT + (V_OF[blk] + k))
                    dve.scalar_tensor_tensor(out=HN[blk], in0=SLOT[k], scalar=WGT[blk][:, bass.ds(i * NSLOT + k, 1)],
                                             in1=HN[blk], op0=ALU.mult, op1=ALU.add).then_inc(S("peer_used"), 1)

        def dve_samples_dots(dve):
            for k in range(PH):
                dve.wait_ge(S(f"slot{k}"), landed(U_S, k))
                dve.scalar_tensor_tensor(out=SLOT[k], in0=SLOT[k], scalar=1.0, in1=XN[2], op0=ALU.mult, op1=ALU.mult,
                                         accum_out=AS[:, k:k + 1]).then_inc(S("peer_used"), 1)

        def dve_samples_sums(dve):
            for k in range(PH):
                dve.wait_ge(S(f"slot{k}"), landed(V_S, k))
                if k == 0:
                    dve.tensor_scalar(ACC_S, SLOT[k], WS[:, k:k + 1], None, ALU.mult).then_inc(S("peer_used"), 1)
                else:
                    dve.wait_ge(S("peer_used"), V_S + k)
                    dve.scalar_tensor_tensor(out=ACC_S, in0=SLOT[k], scalar=WS[:, k:k + 1], in1=ACC_S,
                                             op0=ALU.mult, op1=ALU.add).then_inc(S("peer_used"), 1)
            for q in range(4):
                dve.wait_ge(S("sum_pe"), q + 1)
                dve.tensor_tensor(HN[2][0:TS, q * 512:(q + 1) * 512], HN[2][0:TS, q * 512:(q + 1) * 512],
                                  bank[4 + q][0:TS, :], ALU.add).then_inc(S("sum_s"), 1)

        def pe_samples_sums(pe):
            pe.wait_ge(S("peer_used"), V_S + PH)
            for q in range(4):
                pe.matmul(bank[4 + q][0:TS, :], lhsT=cc("selT"), rhs=ACC_S[:, q * 512:(q + 1) * 512],
                          start=True, stop=True).then_inc(S("sum_pe"), 1)

        def act_gelu(act, blk):
            a, done = (AS, V_S) if blk == 2 else (ACTV, V_OF[blk])
            act.wait_ge(S("peer_used"), done)
            act.activation(a, a, ACT.Gelu_apprx_tanh).then_inc(S("gelu"), 1)

        def dve_gelu(dve, blk):
            w, a = (WS, AS) if blk == 2 else (WGT[blk], ACTV)
            dve.wait_ge(S("gelu"), blk + 1)
            dve.tensor_tensor(w, w, a, ALU.mult).then_inc(S("wgt"), 1)
            dve.wait_ge(S("wgt"), blk + 1)

        def act_final(act, blk):
            if blk < 2:
                act.wait_ge(S("peer_used"), V_OF[blk] + SLOTS)
            else:
                act.wait_ge(S("sum_s"), 4)
            if blk:
                act.wait_ge(S("f_rms"), 2 * blk)
            act_row_root(act, blk, HOT, "f_rms", 9)

        def dve_final(dve, blk):
            if blk == 0:
                dve.wait_ge(S("ld_last"), 16)
            dve_row_scale(dve, blk, HN[blk], "f_rms", "y", 9)

        def sp_peer(sp):
            sp.wait_ge(S("xn"), 6)
            sp.dma_start(GB, A["g_final"].partition_broadcast(P)).then_inc(S("ld_last"), 16)
            for blk in range(3):
                sp.wait_ge(S("y"), 2 * blk + 2)
                dst = A["y_p"][blk * P:(blk + 1) * P, :] if blk < 2 else A["y_s"]
                sp.dma_start(dst, HN[blk][0:BLOCKS[blk], :]).then_inc(S("y_stored"), 16)
            sp.wait_ge(S("y_stored"), 48)

        @block.sync
        def _(sp):
            sp_stream(sp)
            sp_peer(sp)

        @block.tensor
        def _(pe):
            pe_front(pe)
            pe_middle(pe)
            pe_queries(pe)
            pe_keys(pe, 1)
            pe_samples_expand(pe)
            pe_keys(pe, 2)
            pe_samples_experts(pe)
            pe_samples_sums(pe)

        @block.scalar
        def _(act):
            act_front(act)
            act_middle(act)
            act_queries(act)
            act_samples_expand(act)
            act_keys(act, 1)
            act_gelu(act, 0)
            act_keys(act, 2)
            act_final(act, 0)
            act_gelu(act, 1)
            act_final(act, 1)
            act_gelu(act, 2)
            act_final(act, 2)

        @block.vector
        def _(dve):
            dve_index(dve)
            dve_front(dve)
            dve_middle(dve)
            dve_retrieve(dve, 0)
            dve_early_dots(dve, 0, 4)
            dve_retrieve(dve, 1)
            dve_early_dots(dve, 4, 12)
            dve_retrieve(dve, 2)
            dve_early_dots(dve, 12, EARLY)
            dve_retrieve(dve, 3)
            dve_dots(dve, 0, 2, 6)
            dve_keys(dve, PARTS)
            dve_dots(dve, 0, 6, 10)
            dve_candidates(dve, PARTS)
            dve_dots(dve, 0, 10, 13)
            dve_experts(dve, PARTS)
            dve_dots(dve, 0, 13, 16)
            dve_gelu(dve, 0)
            dve_sums(dve, 0, 0, 4)
            dve_keys(dve, PARTS + 1)
            dve_sums(dve, 0, 4, 8)
            dve_candidates(dve, PARTS + 1)
            dve_sums(dve, 0, 8, 12)
            dve_experts(dve, PARTS + 1)
            dve_sums(dve, 0, 12, 16)
            dve_dots(dve, 1, 0, 4)
            dve_final(dve, 0)
            dve_dots(dve, 1, 4, 8)
            dve_samples_experts(dve)
            dve_dots(dve, 1, 8, 16)
            dve_gelu(dve, 1)
            dve_sums(dve, 1, 0, 16)
            dve_samples_dots(dve)
            dve_final(dve, 1)
            dve_gelu(dve, 2)
            dve_samples_sums(dve)
            dve_final(dve, 2)

        @block.gpsimd
        def _(pool):
            pool_front(pool)
            pool_middle(pool)
            pool_peer(pool)
            pool.wait_ge(S("stored"), 64)
            pool.wait_ge(S("z_stored"), 16)
            pool.wait_ge(S("m_stored"), 32)
            pool.wait_ge(S("new_stored"), 32)


def kernel(**inputs):
    import concourse.bacc as bacc
    from concourse.bass_utils import run_bass_kernel_spmd

    a = {k: np.asarray(v) for k, v in inputs.items()}

    def feature_tiles(x):
        return x.T.reshape(-1, P, x.shape[0]).transpose(1, 0, 2)

    def columns(v):
        return v.reshape(-1, P).T

    def weight(w):
        k, n = w.shape
        return w.reshape(k // P, P, n // P, P).transpose(2, 1, 0, 3).reshape(n // P, P, k)

    def pair_heads(w):
        return w.reshape(2, 2, GQ, HD, -1).transpose(0, 2, 1, 3, 4).reshape(HEADS * HD, -1)

    def states(v):
        return np.moveaxis(v.reshape(-1, ST, P), (2, 1, 0), (0, 1, 2))

    def groups(v):
        out = np.zeros((ST, 2, SN, 2, SG), np.float32)
        g = v.reshape(ST, 2, SN, SG)
        out[:, 0, :, 0], out[:, 1, :, 1] = g[:, 0], g[:, 1]
        return out.reshape(ST, P, 32).transpose(1, 0, 2).reshape(P, ST * 32)

    def pages(pool):
        return pool.reshape(20, P, 2, P).transpose(0, 3, 2, 1).reshape(2560, 256)

    tokens = np.concatenate([a["x_prompt"][0], a["x_sample"][:, 0]])
    w_in = a["w_in"][0]
    w_z = np.concatenate([pair_heads(w_in[:, :1024].T).T, w_in[:, 1024:2560], w_in[:, 2608:]], 1)
    w_out = np.concatenate([pair_heads(a["w_out"][0, :1024]), a["w_out"][0, 1024:]])
    log_dt = np.broadcast_to(a["log_dt"][0][:, None], (GROUPS, SN))
    w_cmp = np.stack([np.repeat(a[n][0], HD, 0).reshape(2, P, CMP) for n in ("w_cmp_k", "w_cmp_v")])
    given = {
        "consts": constants(),
        "gains": np.concatenate([columns(x) for x in (
            a["g_mix"][0], a["g_x"][0], a["g_mem"][0], a["g_ffn"][0],
            pair_heads(a["g_attn_out"][0][:, None])[:, 0], a["g_ssm_out"][0], a["d_skip"][0])], 1),
        "x_t": feature_tiles(tokens), "mem_t": feature_tiles(a["mem_prompt"][0]),
        "w_z": weight(w_z), "w_gate": w_in[:, 2560:2608].reshape(KT, P, 48).transpose(1, 0, 2).reshape(P, -1),
        "w_out": weight(w_out),
        **{n: weight(a[n][0]) for n in ("w_xk", "w_xv", "w_glu", "w_xq", "w_xo", "w_pq")},
        "s5_par": np.stack([states(x)[:, :, 0] for x in (a["lam_re"][0], a["lam_im"][0], log_dt)], 1),
        "s5_b": np.stack([groups(a[n][0]) for n in ("b_re", "b_im")], 1),
        "s5_c": np.stack([groups(a[n][0].transpose(0, 2, 1)) for n in ("c_re", "c_im")], 1),
        "s5_h0": np.stack([states(a[n][0]).reshape(P, -1) for n in ("state_s5_re", "state_s5_im")], 1),
        "w_cmp": w_cmp.transpose(2, 0, 1, 3), "page": a["page_table"].reshape(-1),
        "pool_kc": pages(a["cache_k_cmp"][0]), "pool_vc": pages(a["cache_v_cmp"][0]),
        "pool_ks": pages(a["cache_k_sel"][0]), "pool_vs": a["cache_v_sel"][0].reshape(2560, 256),
        "win_k": a["cache_k_win"][0].reshape(TS, 2, P, 2, P).transpose(0, 4, 1, 3, 2).reshape(TS, P, 512),
        "win_v": a["cache_v_win"][0].reshape(TS, 2, P, 256).transpose(0, 2, 1, 3).reshape(TS, P, 512),
        "mem_k": a["cache_mem_k"][0].reshape(TS, MEM, 2, 8, P).transpose(0, 2, 4, 3, 1).reshape(TS, 2, P, D),
        "mem_v": a["cache_mem_v"][0].reshape(TS, 2, P, D),
        "keys": np.stack([a["peer_k1"][0].T, a["peer_k2"][0].T], 1),
        "peer_u": a["peer_u"][0], "peer_v": a["peer_v"][0], "g_ffn": a["g_ffn"][0], "g_final": a["g_final"],
        "buf_k": a["cache_k_win"][0].reshape(TS, -1), "buf_v": a["cache_v_win"][0].reshape(TS, -1),
    }
    nc = bacc.Bacc("TRN2", target_bir_lowering=False, num_devices=1)
    arrays, args = {}, {}
    for name, shape in INS.items():
        x = np.ascontiguousarray(given[name])
        assert x.shape == shape, (name, x.shape, shape)
        arrays["in_" + name] = x
        args[name] = nc.dram_tensor("in_" + name, x.shape, mybir.dt.from_np(x.dtype), kind="ExternalInput").ap()
    for name, shape in OUTS.items():
        args[name] = nc.dram_tensor("out_" + name, shape, F32, kind="ExternalOutput").ap()
    build(nc, args)
    got = run_bass_kernel_spmd(nc, [arrays], core_ids=[0]).results[0]
    o = {name: np.asarray(got["out_" + name]) for name in OUTS}

    z = o["z_kv"].reshape(6, KV, HD, NT)
    kv_p = [z[i, :, :, :TP].transpose(2, 0, 1)[None, None] for i in range(6)]
    kv_s = [z[i, :, :, TP:].transpose(2, 0, 1)[None, :, None] for i in range(6)]

    def of_states(v, n):
        return [x.transpose(2, 1, 0).reshape((1, n, GROUPS, SN)) for x in v.reshape(P, 2, ST, n).swapaxes(0, 1)]

    return (o["y_p"][None], o["y_s"][:, None], *kv_p, *of_states(o["s5_p"], 1),
            o["m_k"].transpose(2, 0, 1).reshape(1, 1, MEM, XH, XD), o["m_v"].reshape(1, 1, MEM, XH, XD),
            *kv_s[:4], *(o[n].reshape(1, TS, 257, KV, HD) for n in ("new_k", "new_v")), *of_states(o["s5_s"], TS))
```
